# Optimizing a Trainium2 kernel written in Bass

```python
import math
import jax, jax.numpy as jnp
from jax import lax
import numpy as np
import jax
import jax.numpy as jnp

D_MODEL = 1024
BATCH = 1
SEQ = 512
DEPTH = 2

N_BRANCHES = 4
BRANCH_WIDTH = 256
HEAD_DIM = 64
N_HEADS = BRANCH_WIDTH // HEAD_DIM
N_IDX_HEADS = 4
IDX_DIM = 32
TOPK_MAX = 256
CONV_WIDTH = 3
CHUNK = 128
N_GROUPS = 4
GROUP_DIM = BRANCH_WIDTH // N_GROUPS
Q_BLOCK = 128
PLE_DIM = 256
ROPE_THETA = 10000.0
EPS = 1e-6
IDX_W_SCALE = (N_IDX_HEADS * IDX_DIM) ** -0.5

IN_SPLITS = (
    BRANCH_WIDTH, BRANCH_WIDTH, BRANCH_WIDTH,
    N_IDX_HEADS * IDX_DIM, IDX_DIM, N_IDX_HEADS,
    BRANCH_WIDTH, BRANCH_WIDTH, BRANCH_WIDTH,
    BRANCH_WIDTH, BRANCH_WIDTH, BRANCH_WIDTH,
    BRANCH_WIDTH, BRANCH_WIDTH,
    N_BRANCHES * BRANCH_WIDTH,
    N_BRANCHES * D_MODEL,
)
IN_COLS = sum(IN_SPLITS)


def _split_cols(h, sizes):
    out, off = [], 0
    for n in sizes:
        out.append(h[..., off:off + n])
        off += n
    return out

def rmsnorm(x, g):
    xf = x.astype(jnp.float32)
    y = xf * lax.rsqrt(jnp.mean(xf * xf, axis=-1, keepdims=True) + EPS)
    return (y * g.astype(jnp.float32)).astype(x.dtype)

def layernorm(x, g, b):
    xf = x.astype(jnp.float32)
    mu = jnp.mean(xf, axis=-1, keepdims=True)
    var = jnp.mean(jnp.square(xf - mu), axis=-1, keepdims=True)
    y = (xf - mu) * lax.rsqrt(var + EPS)
    return (y * g.astype(jnp.float32) + b.astype(jnp.float32)).astype(x.dtype)

def rope(x, pos):
    d = x.shape[-1]
    inv_freq = ROPE_THETA ** (-jnp.arange(0, d, 2, dtype=jnp.float32) / d)
    ang = pos.astype(jnp.float32)[..., None] * inv_freq
    cos = jnp.cos(ang)[:, :, None, :]
    sin = jnp.sin(ang)[:, :, None, :]
    xf = x.astype(jnp.float32)
    x1, x2 = xf[..., : d // 2], xf[..., d // 2:]
    return jnp.concatenate([x1 * cos - x2 * sin, x2 * cos + x1 * sin], axis=-1).astype(x.dtype)

def dsa_sparse_attention(q, k, v, iq, ik, iw):
    B, S, H, dh = q.shape
    topk = min(TOPK_MAX, S // 4)
    n_blk = S // Q_BLOCK
    key_pos = jnp.arange(S)
    neg = jnp.finfo(jnp.float32).min
    scale = HEAD_DIM ** -0.5

    def block(i):
        start = i * Q_BLOCK
        qb = lax.dynamic_slice_in_dim(q, start, Q_BLOCK, axis=1)
        iqb = lax.dynamic_slice_in_dim(iq, start, Q_BLOCK, axis=1)
        iwb = lax.dynamic_slice_in_dim(iw, start, Q_BLOCK, axis=1)
        q_pos = start + jnp.arange(Q_BLOCK)
        idx_logits = jnp.einsum('bqhd,bsd->bqhs', iqb, ik).astype(jnp.float32)
        score = jnp.einsum('bqh,bqhs->bqs', iwb.astype(jnp.float32) * IDX_W_SCALE,
                           jax.nn.relu(idx_logits))
        causal = key_pos[None, :] <= q_pos[:, None]
        score = jnp.where(causal[None], score, neg)
        _, sel = lax.top_k(score, topk)
        k_sel = jax.vmap(lambda kk, ii: kk[ii])(k, sel)
        v_sel = jax.vmap(lambda vv, ii: vv[ii])(v, sel)
        logits = jnp.einsum('bqhd,bqkhd->bhqk', qb, k_sel).astype(jnp.float32) * scale
        valid = sel <= q_pos[None, :, None]
        logits = jnp.where(valid[:, None], logits, neg)
        probs = jax.nn.softmax(logits, axis=-1)
        return jnp.einsum('bhqk,bqkhd->bqhd', probs.astype(v.dtype), v_sel)

    out = lax.map(block, jnp.arange(n_blk))
    return jnp.moveaxis(out, 0, 1).reshape(B, S, H * dh)

def short_gated_conv(gate_b, gate_c, x_in, conv_w, conv_b):
    W = x_in.shape[-1]
    y = gate_c * x_in
    conv = lax.conv_general_dilated(
        y, conv_w.astype(y.dtype)[:, None, :],
        window_strides=(1,), padding=[(CONV_WIDTH - 1, 0)],
        dimension_numbers=('NWC', 'WIO', 'NWC'), feature_group_count=W)
    return gate_b * (conv + conv_b)

def stick_breaking_attention(q, k, v):
    B, S, H, dh = q.shape
    n_blk = S // Q_BLOCK
    key_pos = jnp.arange(S)
    scale = HEAD_DIM ** -0.5

    def block(i):
        start = i * Q_BLOCK
        qb = lax.dynamic_slice_in_dim(q, start, Q_BLOCK, axis=1)
        q_pos = start + jnp.arange(Q_BLOCK)
        z = jnp.einsum('bqhd,bshd->bhqs', qb, k).astype(jnp.float32) * scale
        strict = (key_pos[None, :] < q_pos[:, None])[None, None]
        log_beta = jax.nn.log_sigmoid(z)
        log_keep = jnp.where(strict, jax.nn.log_sigmoid(-z), 0.0)
        after = lax.cumsum(log_keep, axis=3, reverse=True) - log_keep
        wts = jnp.where(strict, jnp.exp(log_beta + after), 0.0)
        return jnp.einsum('bhqs,bshd->bqhd', wts.astype(v.dtype), v)

    out = lax.map(block, jnp.arange(n_blk))
    return jnp.moveaxis(out, 0, 1).reshape(B, S, H * dh)

def chunked_spatial_gating(u, v, ln_g, ln_b, w_s, b_s):
    B, S, W = v.shape
    vn = layernorm(v, ln_g, ln_b).reshape(B, S // CHUNK, CHUNK, N_GROUPS, GROUP_DIM)
    mask = jnp.tril(jnp.ones((CHUNK, CHUNK), dtype=w_s.dtype))
    mixed = jnp.einsum('gts,bnsgd->bntgd', w_s * mask, vn) + b_s.T[None, None, :, :, None]
    return u * mixed.reshape(B, S, W)

def hybrid_layer(x, p_i, positions, g_pre, w_in, conv_w, conv_b, ln_g, ln_b,
                 w_spatial, b_spatial, b_merge, w_branch, w_out, g_post, w_ple, w_ple_gate):
    B, S, _ = x.shape
    h = rmsnorm(x, g_pre)
    proj = jnp.einsum('bsd,dc->bsc', h, w_in)
    (a_q, a_k, a_v, a_iq, a_ik, a_iw, b_b, b_c, b_x, c_q, c_k, c_v,
     d_u, d_v, gate_paths, merge_logits) = _split_cols(proj, IN_SPLITS)

    heads = lambda t: t.reshape(B, S, N_HEADS, HEAD_DIM)
    iq = rope(a_iq.reshape(B, S, N_IDX_HEADS, IDX_DIM), positions)
    ik = rope(a_ik[:, :, None, :], positions)[:, :, 0, :]
    o_a = dsa_sparse_attention(rope(heads(a_q), positions), rope(heads(a_k), positions),
                               heads(a_v), iq, ik, a_iw)
    o_b = short_gated_conv(b_b, b_c, b_x, conv_w, conv_b)
    o_c = stick_breaking_attention(heads(c_q), heads(c_k), heads(c_v))
    o_d = chunked_spatial_gating(d_u, d_v, ln_g, ln_b, w_spatial, b_spatial)

    o = jnp.stack([o_a, o_b, o_c, o_d], axis=2)
    o = o * jax.nn.silu(gate_paths.reshape(B, S, N_BRANCHES, BRANCH_WIDTH))
    z = jnp.einsum('bsnw,nwd->bsnd', o, w_branch)
    g = jax.nn.sigmoid((merge_logits + b_merge).reshape(B, S, N_BRANCHES, D_MODEL))
    merged = jnp.sum(g * z, axis=2)
    y = jnp.einsum('bsd,de->bse', merged, w_out)
    x = x + rmsnorm(y, g_post)
    ple = jnp.einsum('bsp,pd->bsd', p_i, w_ple)
    x = x + ple * jax.nn.sigmoid(jnp.einsum('bsd,de->bse', x, w_ple_gate))
    return x

def first_inputs(seed: int = 0) -> dict:
    key = jax.random.key(seed)
    ks = jax.random.split(key, 20)
    nrm = lambda k, shape, s: jax.random.normal(k, shape, jnp.float32) * s
    W = BRANCH_WIDTH
    return {
        "x": nrm(ks[0], (BATCH, SEQ, D_MODEL), 1.0),
        "p": nrm(ks[1], (DEPTH, BATCH, SEQ, PLE_DIM), 1.0),
        "positions": jnp.broadcast_to(jnp.arange(SEQ, dtype=jnp.int32), (BATCH, SEQ)),
        "g_pre": 1.0 + nrm(ks[2], (DEPTH, D_MODEL), 0.02),
        "w_in": nrm(ks[3], (DEPTH, D_MODEL, IN_COLS), D_MODEL ** -0.5),
        "conv_w": nrm(ks[4], (DEPTH, CONV_WIDTH, W), CONV_WIDTH ** -0.5),
        "conv_b": nrm(ks[5], (DEPTH, W), 0.02),
        "ln_g": 1.0 + nrm(ks[6], (DEPTH, W), 0.02),
        "ln_b": nrm(ks[7], (DEPTH, W), 0.02),
        "w_spatial": nrm(ks[8], (DEPTH, N_GROUPS, CHUNK, CHUNK), CHUNK ** -0.5),
        "b_spatial": 1.0 + nrm(ks[9], (DEPTH, N_GROUPS, CHUNK), 0.02),
        "b_merge": nrm(ks[10], (DEPTH, N_BRANCHES * D_MODEL), 0.02),
        "w_branch": nrm(ks[11], (DEPTH, N_BRANCHES, W, D_MODEL), W ** -0.5),
        "w_out": nrm(ks[12], (DEPTH, D_MODEL, D_MODEL), D_MODEL ** -0.5),
        "g_post": 1.0 + nrm(ks[13], (DEPTH, D_MODEL), 0.02),
        "w_ple": nrm(ks[14], (DEPTH, PLE_DIM, D_MODEL), PLE_DIM ** -0.5),
        "w_ple_gate": nrm(ks[15], (DEPTH, D_MODEL, D_MODEL), D_MODEL ** -0.5),
    }

def first_block(x, p, positions, g_pre, w_in, conv_w, conv_b, ln_g, ln_b, w_spatial, b_spatial,
              b_merge, w_branch, w_out, g_post, w_ple, w_ple_gate):
    for i in range(DEPTH):
        x = hybrid_layer(x, p[i], positions, g_pre[i], w_in[i], conv_w[i], conv_b[i], ln_g[i], ln_b[i],
                         w_spatial[i], b_spatial[i], b_merge[i], w_branch[i], w_out[i], g_post[i],
                         w_ple[i], w_ple_gate[i])
    return x


_first_inputs = first_inputs


def first_inputs(seed=0):
    import zlib

    import numpy as np

    out = dict(_first_inputs(seed))
    spreads = {}
    factors = {'conv_b': 4.47,
     'ln_g': 6.564,
     'ln_b': 6.502,
     'b_spatial': 4.808,
     'b_merge': 6.69,
     'g_post': 2.745}
    for name, (base, spread) in spreads.items():
        noise = np.random.default_rng([zlib.crc32(name.encode()), seed]).standard_normal(out[name].shape)
        drawn = base * np.exp(spread * noise) if base else spread * noise
        out[name] = __import__('jax').numpy.asarray(drawn.astype(out[name].dtype))
    for name, factor in factors.items():
        out[name] = (out[name] * factor).astype(out[name].dtype)
    return out


_narrow_inputs = first_inputs


def first_inputs(seed=0):

    out = dict(_narrow_inputs(seed))
    wider = {'conv_b': 3.05, 'ln_g': 3.52, 'ln_b': 3.46, 'b_spatial': 3.27}
    for name, times in wider.items():
        mean = out[name].mean()
        out[name] = (mean + times * (out[name] - mean)).astype(out[name].dtype)
    return out


DEPTH_2 = 1

A_HEADS = 16
A_HEAD_DIM = 64
A_WIDTH = A_HEADS * A_HEAD_DIM
DILATED_PATTERNS = ((128, 1), (512, 4), (2048, 16))
N_BUCKETS = 32
MAX_EXACT = N_BUCKETS // 2
MAX_DISTANCE = 2048
M_HEADS = 4
M_WIDTH = 2 * D_MODEL
M_HEAD_DIM = M_WIDTH // M_HEADS
CONV_K = 4
QKV_BLOCK = 4
CHUNK_2 = 64
N_IN = 4 * A_WIDTH + 3 * M_WIDTH + 2 * D_MODEL
SPLIT_POINTS = (A_WIDTH, 2 * A_WIDTH, 3 * A_WIDTH, 4 * A_WIDTH, 4 * A_WIDTH + M_WIDTH, 4 * A_WIDTH + 2 * M_WIDTH, 4 * A_WIDTH + 3 * M_WIDTH)


def rmsnorm_2(x, g):
    xf = x.astype(jnp.float32)
    y = xf * lax.rsqrt(jnp.mean(xf * xf, axis=-1, keepdims=True) + EPS)
    return (y * g.astype(jnp.float32)).astype(x.dtype)

def t5_bucket(dist):
    large = MAX_EXACT + (jnp.log(jnp.maximum(dist, MAX_EXACT).astype(jnp.float32) / MAX_EXACT)
                         / math.log(MAX_DISTANCE / MAX_EXACT) * (N_BUCKETS - MAX_EXACT)).astype(jnp.int32)
    return jnp.where(dist < MAX_EXACT, dist, jnp.minimum(large, N_BUCKETS - 1))

def dilated_band_attention(q, k, v, rel_bias, window, dilation):
    B, S, H, dh = q.shape
    band = window // dilation
    span = band * dilation
    s_pad = -(-S // span) * span
    L = s_pad // dilation
    nb = L // band

    def to_blocks(t):
        t = jnp.pad(t, ((0, 0), (0, s_pad - S), (0, 0), (0, 0)))
        t = t.reshape(B, L, dilation, H, dh).transpose(0, 2, 3, 1, 4)
        return t.reshape(B, dilation, H, nb, band, dh)

    def with_prev(t):
        prev = jnp.pad(t, ((0, 0), (0, 0), (0, 0), (1, 0), (0, 0), (0, 0)))[:, :, :, :-1]
        return jnp.concatenate([prev, t], axis=4)

    qb = to_blocks(q)
    kc = with_prev(to_blocks(k))
    vc = with_prev(to_blocks(v))
    logits = jnp.einsum('brhnqc,brhnkc->brhnqk', qb, kc, preferred_element_type=jnp.float32) * (dh ** -0.5)
    qi = jnp.arange(band)[:, None]
    kj = jnp.arange(2 * band)[None, :]
    delta = qi + band - kj
    bias = rel_bias.astype(jnp.float32)[t5_bucket(jnp.clip(delta, 0, band) * dilation)]
    bias = jnp.transpose(bias, (2, 0, 1))[:, None]
    key_pos = jnp.arange(nb)[:, None, None] * band + kj[None] - band
    valid = (delta >= 0) & (delta <= band) & (key_pos >= 0)
    logits = jnp.where(valid, logits + bias, -jnp.inf)
    m = jnp.max(logits, axis=-1)
    p = jnp.exp(logits - m[..., None])
    s = jnp.sum(p, axis=-1)
    o = jnp.einsum('brhnqk,brhnkc->brhnqc', p, vc.astype(jnp.float32)) / s[..., None]

    def from_blocks(t):
        t = t.reshape((B, dilation, H, L) + t.shape[5:])
        t = jnp.moveaxis(t, 3, 1)
        return t.reshape((B, s_pad, H) + t.shape[4:])[:, :S]

    return from_blocks(o), from_blocks(m), from_blocks(s)

def dilated_attention(q, k, v, rel_bias):
    B, S, H, dh = q.shape
    outs = [dilated_band_attention(q, k, v, rel_bias, w, d) for (w, d) in DILATED_PATTERNS]
    o = jnp.stack([t[0] for t in outs])
    m = jnp.stack([t[1] for t in outs])
    s = jnp.stack([t[2] for t in outs])
    wgt = jnp.exp(m - jnp.max(m, axis=0, keepdims=True)) * s
    out = jnp.sum(wgt[..., None] * o, axis=0) / jnp.sum(wgt, axis=0)[..., None]
    return out.reshape(B, S, H * dh)

def causal_depthwise_conv(x, w, b):
    S = x.shape[1]
    xp = jnp.pad(x, ((0, 0), (CONV_K - 1, 0), (0, 0)))
    y = b
    for tap in range(CONV_K):
        y = y + xp[:, tap:tap + S] * w[tap]
    return y

def block_diag_proj(x, w):
    B, S, C = x.shape
    return jnp.einsum('bsgi,gio->bsgo', x.reshape(B, S, C // QKV_BLOCK, QKV_BLOCK), w).reshape(B, S, C)

def mlstm_chunkwise(q, k, v, li, lf):
    B, S, H, dh = q.shape
    nc = S // CHUNK_2

    def chunks(t):
        t = t.astype(jnp.float32).reshape((B, nc, CHUNK_2, H) + t.shape[3:])
        return jnp.moveaxis(jnp.moveaxis(t, 1, 0), 3, 2)

    qc, kc, vc = chunks(q), chunks(k) * (dh ** -0.5), chunks(v)
    lic, lfc = chunks(li), chunks(lf)
    tril = jnp.tril(jnp.ones((CHUNK_2, CHUNK_2), dtype=bool))

    def step(carry, xs):
        C, n, m = carry
        qt, kt, vt, it, ft = xs
        b = jnp.cumsum(ft, axis=-1)
        g = b[..., -1]
        D = jnp.where(tril, b[..., :, None] - b[..., None, :] + it[..., None, :], -jnp.inf)
        inter = b + m[..., None]
        m_t = jnp.maximum(inter, jnp.max(D, axis=-1))
        qk = jnp.einsum('bhtd,bhsd->bhts', qt, kt) * jnp.exp(D - m_t[..., None])
        w_inter = jnp.exp(inter - m_t)
        num = w_inter[..., None] * jnp.einsum('bhtd,bhde->bhte', qt, C) + jnp.einsum('bhts,bhse->bhte', qk, vt)
        den = w_inter * jnp.einsum('bhtd,bhd->bht', qt, n) + jnp.sum(qk, axis=-1)
        h = num / jnp.maximum(jnp.abs(den), jnp.exp(-m_t))[..., None]
        to_end = g[..., None] - b + it
        m_new = jnp.maximum(g + m, jnp.max(to_end, axis=-1))
        w_s = jnp.exp(to_end - m_new[..., None])
        decay = jnp.exp(g + m - m_new)
        C_new = decay[..., None, None] * C + jnp.einsum('bhsd,bhse->bhde', kt * w_s[..., None], vt)
        n_new = decay[..., None] * n + jnp.einsum('bhs,bhsd->bhd', w_s, kt)
        return (C_new, n_new, m_new), h

    init = (jnp.zeros((B, H, dh, dh), jnp.float32), jnp.zeros((B, H, dh), jnp.float32), jnp.zeros((B, H), jnp.float32))
    _, h = lax.scan(step, init, (qc, kc, vc, lic, lfc))
    return jnp.transpose(h, (1, 0, 3, 2, 4)).reshape(B, S, H, dh)

def mlstm_branch(x_m, z_m, o_m, conv_w, conv_b, wq, wk, wv, w_if, b_if, head_norm_g, skip):
    B, S, _ = x_m.shape
    x_c = jax.nn.silu(causal_depthwise_conv(x_m, conv_w, conv_b))
    q = block_diag_proj(x_c, wq)
    k = block_diag_proj(x_c, wk)
    v = block_diag_proj(x_m, wv)
    gate_pre = (jnp.concatenate([q, k, v], axis=-1) @ w_if + b_if).astype(jnp.float32)
    li = gate_pre[..., :M_HEADS]
    lf = jax.nn.log_sigmoid(gate_pre[..., M_HEADS:])
    heads = lambda t: t.reshape(B, S, M_HEADS, M_HEAD_DIM)
    h = mlstm_chunkwise(heads(q), heads(k), heads(v), li, lf)
    h = jax.nn.sigmoid(heads(o_m).astype(jnp.float32)) * h
    mu = jnp.mean(h, axis=-1, keepdims=True)
    var = jnp.mean(jnp.square(h - mu), axis=-1, keepdims=True)
    h = (h - mu) * lax.rsqrt(var + EPS) * head_norm_g.astype(jnp.float32).reshape(M_HEADS, M_HEAD_DIM)
    h = h.reshape(B, S, M_WIDTH) + skip * x_c
    return h * jax.nn.silu(z_m)

def second_inputs(seed: int = 0) -> dict:
    key = jax.random.key(seed)
    ks = jax.random.split(key, 20)
    nrm = lambda k, shape, scale: jax.random.normal(k, shape, jnp.float32) * scale
    n_blocks = M_WIDTH // QKV_BLOCK
    x = nrm(ks[0], (BATCH, SEQ, D_MODEL), 1.0)
    norm_in_g = 1.0 + nrm(ks[1], (DEPTH_2, D_MODEL), 0.02)
    w_in = nrm(ks[2], (DEPTH_2, D_MODEL, N_IN), D_MODEL ** -0.5)
    gate_b = nrm(ks[3], (DEPTH_2, 2 * D_MODEL), 0.01)
    conv_w = nrm(ks[4], (DEPTH_2, CONV_K, M_WIDTH), CONV_K ** -0.5)
    conv_b = nrm(ks[5], (DEPTH_2, M_WIDTH), 0.01)
    wq_m = nrm(ks[6], (DEPTH_2, n_blocks, QKV_BLOCK, QKV_BLOCK), QKV_BLOCK ** -0.5)
    wk_m = nrm(ks[7], (DEPTH_2, n_blocks, QKV_BLOCK, QKV_BLOCK), QKV_BLOCK ** -0.5)
    wv_m = nrm(ks[8], (DEPTH_2, n_blocks, QKV_BLOCK, QKV_BLOCK), QKV_BLOCK ** -0.5)
    w_if = nrm(ks[9], (DEPTH_2, 3 * M_WIDTH, 2 * M_HEADS), (3 * M_WIDTH) ** -0.5)
    b_if = jnp.concatenate([nrm(ks[10], (DEPTH_2, M_HEADS), 0.1),
                            jnp.linspace(3.0, 6.0, M_HEADS)[None] + nrm(ks[11], (DEPTH_2, M_HEADS), 0.01)], axis=-1)
    head_norm_g = 1.0 + nrm(ks[12], (DEPTH_2, M_WIDTH), 0.02)
    skip_m = 1.0 + nrm(ks[13], (DEPTH_2, M_WIDTH), 0.02)
    w_pa = nrm(ks[14], (DEPTH_2, A_WIDTH, D_MODEL), A_WIDTH ** -0.5)
    w_pb = nrm(ks[15], (DEPTH_2, M_WIDTH, D_MODEL), M_WIDTH ** -0.5)
    w_out = nrm(ks[16], (DEPTH_2, D_MODEL, D_MODEL), D_MODEL ** -0.5)
    rel_bias = nrm(ks[17], (N_BUCKETS, A_HEADS), 0.3)
    norm_out_g = 1.0 + nrm(ks[18], (D_MODEL,), 0.02)
    return {'x': x, 'norm_in_g': norm_in_g, 'w_in': w_in, 'gate_b': gate_b, 'conv_w': conv_w, 'conv_b': conv_b,
            'wq_m': wq_m, 'wk_m': wk_m, 'wv_m': wv_m, 'w_if': w_if, 'b_if': b_if, 'head_norm_g': head_norm_g,
            'skip_m': skip_m, 'w_pa': w_pa, 'w_pb': w_pb, 'w_out': w_out, 'rel_bias': rel_bias, 'norm_out_g': norm_out_g}

def second_block(x, norm_in_g, w_in, gate_b, conv_w, conv_b, wq_m, wk_m, wv_m, w_if, b_if, head_norm_g,
              skip_m, w_pa, w_pb, w_out, rel_bias, norm_out_g):
    B, S, _ = x.shape
    h = x
    for layer in range(DEPTH_2):
        xn = rmsnorm_2(h, norm_in_g[layer])
        proj = xn @ w_in[layer]
        q_a, k_a, v_a, z_a, x_m, z_m, o_m, gates = jnp.split(proj, SPLIT_POINTS, axis=-1)
        to_heads = lambda t: t.reshape(B, S, A_HEADS, A_HEAD_DIM)
        y_a = dilated_attention(to_heads(q_a), to_heads(k_a), to_heads(v_a), rel_bias)
        y_a = (y_a * jax.nn.silu(z_a)) @ w_pa[layer]
        y_m = mlstm_branch(x_m, z_m, o_m, conv_w[layer], conv_b[layer], wq_m[layer], wk_m[layer], wv_m[layer],
                           w_if[layer], b_if[layer], head_norm_g[layer], skip_m[layer]) @ w_pb[layer]
        g = jax.nn.sigmoid(gates.astype(jnp.float32) + gate_b[layer])
        g_a, g_m = jnp.split(g, 2, axis=-1)
        merged = g_a * y_a + g_m * y_m
        h = h + (merged @ w_out[layer]).astype(h.dtype)
    return rmsnorm_2(h, norm_out_g)


_first_inputs_2 = second_inputs


def second_inputs(seed=0):
    import zlib

    import numpy as np

    out = dict(_first_inputs_2(seed))
    spreads = {}
    factors = {'norm_in_g': 3.524,
     'gate_b': 8.0,
     'conv_b': 8.0,
     'head_norm_g': 8.0,
     'skip_m': 8.0,
     'rel_bias': 4.517,
     'norm_out_g': 2.91}
    for name, (base, spread) in spreads.items():
        noise = np.random.default_rng([zlib.crc32(name.encode()), seed]).standard_normal(out[name].shape)
        drawn = base * np.exp(spread * noise) if base else spread * noise
        out[name] = jnp.asarray(drawn.astype(out[name].dtype))
    for name, factor in factors.items():
        out[name] = (out[name] * factor).astype(out[name].dtype)
    return out


_narrow_inputs_2 = second_inputs


def second_inputs(seed=0):

    out = dict(_narrow_inputs_2(seed))
    wider = {'gate_b': 3.94, 'head_norm_g': 8.89, 'skip_m': 3.4, 'norm_out_g': 3.27}
    for name, times in wider.items():
        mean = out[name].mean()
        out[name] = (mean + times * (out[name] - mean)).astype(out[name].dtype)
    return out


def setup_inputs(seed=0):
    out = dict(first_inputs(seed))
    for name, value in second_inputs(seed + 1).items():
        if name != "x":
            out[name + "_2"] = value
    return out


def reference(
    x, p, positions, g_pre, w_in, conv_w, conv_b, ln_g, ln_b, w_spatial, b_spatial, b_merge,
    w_branch, w_out, g_post, w_ple, w_ple_gate, norm_in_g_2, w_in_2, gate_b_2, conv_w_2,
    conv_b_2, wq_m_2, wk_m_2, wv_m_2, w_if_2, b_if_2, head_norm_g_2, skip_m_2, w_pa_2, w_pb_2,
    w_out_2, rel_bias_2, norm_out_g_2,
):
    x = first_block(
        x, p, positions, g_pre, w_in, conv_w, conv_b, ln_g, ln_b, w_spatial, b_spatial, b_merge,
        w_branch, w_out, g_post, w_ple, w_ple_gate,
    )
    return second_block(
        x, norm_in_g_2, w_in_2, gate_b_2, conv_w_2, conv_b_2, wq_m_2, wk_m_2, wv_m_2, w_if_2,
        b_if_2, head_norm_g_2, skip_m_2, w_pa_2, w_pb_2, w_out_2, rel_bias_2, norm_out_g_2,
    )


_drawn_inputs = setup_inputs


def setup_inputs(seed=0):
    import zlib

    import numpy as np

    out = dict(_drawn_inputs(seed))
    spreads = {}
    factors = {}
    for name, (base, spread) in spreads.items():
        noise = np.random.default_rng([zlib.crc32(name.encode()), seed]).standard_normal(out[name].shape)
        drawn = base * np.exp(spread * noise) if base else spread * noise
        out[name] = jnp.asarray(drawn.astype(out[name].dtype))
    for name, factor in factors.items():
        out[name] = (out[name] * factor).astype(out[name].dtype)
    return out
```

```python
P = 128
WIDTH = 256
CHUNK = 8 * 260
PROJECTIONS = ["aq", "ak", "idx", "av", "cq", "ck", "cv", "dv", "du", "bc", "bx", "bb", "g1", "g3", "g2", "g0"]


def layer_chunks():
    ch = [("proj", n) for n in PROJECTIONS]
    for d in range(8):
        ch += [("logits", (d, 0)), ("logits", (d, 1)), ("branch", d)]
    ch += [("out", e) for e in range(4)]
    ch += [("ple", 0), ("ple", 1)]
    return ch + [("pgate", e) for e in range(4)]


def attention_chunks():
    ch = [("q", 0), ("k", 0), ("v", 0)]
    for i in range(3):
        ch += [("q", i + 1), ("k", i + 1), ("v", i + 1), ("z", i)]
    ch += [("ga", 0), ("ga", 1), ("ga", 2), ("z", 3), ("ga", 3)]
    return ch + [("pa", d) for d in range(4)]


def head_chunks(h):
    return [("om", 2 * h), ("om", 2 * h + 1), ("zm", 2 * h), ("zm", 2 * h + 1), ("pb", 2 * h), ("pb", 2 * h + 1)]


def tail_chunks():
    return [("gm", d) for d in range(4)] + [("fo", d) for d in range(4)]


def columns(chunk):
    kind, i = chunk
    return {"branch": 8 * P, "ple": 8 * P}.get(kind, CHUNK if i == "idx" else 8 * WIDTH)


def build_program(nc, a):
    from contextlib import ExitStack

    import concourse.bass as bass
    from concourse import mybir

    ALU = mybir.AluOpType
    ACT = mybir.ActivationFunctionType
    F32 = mybir.dt.float32
    F32R = mybir.dt.float32r
    I32 = mybir.dt.int32
    ds = bass.ds

    DEPTH = a["par1"].shape[1]
    D = a["xT"].shape[1] * P
    S = a["xT"].shape[2]
    KT = D // P
    TT = S // P
    W = 256
    EPS = 1e-6
    NEG_SCORE = -3.0e38
    MARK = -3.3e38
    NEG = -1.0e30

    PROJ = PROJECTIONS
    TOKEN_MAJOR = ("av", "cv", "dv")
    CH = layer_chunks()
    CH_B, CH_C, CH_D, CH_E = attention_chunks(), [("xm", 0), ("xm", 1)], head_chunks(0), tail_chunks()
    NCH = len(CH)
    assert NCH % 2 == 0
    SLOT = CHUNK
    COLUMNS = [columns(c) for c in CH]

    order = [("ssx", 4)]
    order += [("rotq0", 4), ("rotq1", 5), ("rotk0", 6), ("rotk1", 7), ("roti0", 4), ("roti1", 5)]
    order += [("iw", 6)]
    order += [(("idx", tt, h), 4 + h) for tt in (3, 2, 1) for h in range(4)]
    for h in range(4):
        if h == 2:
            order += [(("dmix", 0), 4), (("dmix", 1), 5)]
        order += [(("Z", h, j), 4 + j) for j in range(3)]
        order += [(("Sx", h, j), 4 + j) for j in range(3)] + [(("CO", h), 7)]
    for tt in range(4):
        order += [(("L", tt, 0), 4), (("L", tt, 1), 5), (("T", tt, 0), 6), (("L", tt, 2), 4),
                  (("T", tt, 1), 6), (("L", tt, 3), 5), (("T", tt, 2), 6), (("T", tt, 3), 6),
                  (("AO", tt), 7)]
    order += [("ssy", 6)]
    order_b = [("ssx", 4)]
    for i in range(4):
        for m in range(4):
            order_b += [(("L", m, 0, i), 4), (("L", m, 1, i), 5), (("T", m, 0, i), 6), (("L", m, 2, i), 4),
                        (("T", m, 1, i), 6), (("L", m, 3, i), 5), (("T", m, 2, i), 6), (("T", m, 3, i), 6),
                        (("AO", m, i), 7)]
    order_c = []
    for t in range(4):
        order_c += [(("fold", t), 4), (("qm", t), 4), (("km", t), 5), (("vm", t), 6)]
    order_g = [("gates", 7), ("f", 4), ("cols", 5)]
    order_d = [("M", 7)] + [(("sc", j), 4 + j) for j in range(3)] + [("den", 7)]
    order_d += [(("num", tt), 4 + tt % 2) for tt in range(4)] + [(("hT", tt), 6 + tt % 2) for tt in range(4)]
    order_e = [("ssf", 4)]

    class Phase:
        before = None

        def __init__(self, chunks, side, rounds=1):
            p = Phase.before
            self.chunks, self.rounds, self.n = chunks, rounds, len(chunks)
            self.c0 = p.c0 + p.rounds * p.n if p else 0
            self.g0 = p.g0 + p.rounds * p.ng if p else 0
            self.groups, g = [], 0
            for kind, i in chunks:
                k = 4 if kind in ("branch", "ple", "pb") else 2
                self.groups.append(list(range(g, g + k)))
                g += k
            self.ng = g
            self.before_first = p.last_groups if p else (0, 0)
            self.last_groups = self.groups[-1] if chunks else p.last_groups
            assert g % 4 == 0 and len(chunks) % 2 == 0 and self.c0 % 2 == 0, (g, len(chunks))
            self.b0 = {b: p.b0[b] + p.rounds * p.nb[b] if p else 1 for b in range(4, 8)}
            self.side, self.nb = {}, {b: 0 for b in range(4, 8)}
            for key, b in side:
                self.side[key] = (b, self.nb[b])
                self.nb[b] += 1
            Phase.before = self

    LAYERS = Phase(CH, order, DEPTH)
    ATTN = Phase(CH_B, order_b)
    MPROJ = Phase(CH_C, order_c, 4)
    MGATE = Phase([], order_g)
    MHEAD = Phase(CH_D, order_d, 4)
    TAIL = Phase(CH_E, order_e)
    now = [LAYERS]
    GROUPS, NCH = LAYERS.groups, LAYERS.n

    ctx = ExitStack()
    with ctx:
        top = [(nc.sbuf_base + 31) // 32 * 32]

        def place(name, shape, dt=F32, at=None):
            size = 4
            for n in shape[1:]:
                size *= n
            if at is None:
                at = top[0]
                top[0] += (size + 31) // 32 * 32
            t = nc.alloc_sbuf_tensor_at(name, shape, dt, offset=at)
            addr[name] = at
            return t

        addr = {}
        xT = place("xT", [P, KT, S])
        h_hi = place("h_hi", [P, KT, S], F32R)
        h_lo = place("h_lo", [P, KT, S], F32R)
        w_raw = place("w_raw", [P, 2, SLOT])
        w_hi = place("w_hi", [P, 2, SLOT], F32R)
        w_lo = place("w_lo", [P, 2, SLOT], F32R)
        par2 = place("par2", [P, 144])
        bif = place("bif", [8, 1])
        mask4 = place("mask4", [P, 32])
        consts = place("consts", [P, 12, P])
        (ident, ones, trilT, trilT_add, rot64, rot32, tri_neg, tri_add, trisT, trisT_add, upinc_neg,
         ones_neg) = (consts[:, i, :] for i in range(12))
        R2 = addr["consts"] + 4 * P * 4
        cos64 = place("cos64", [P, S])
        sin64 = place("sin64", [P, S])
        cos32 = place("cos32", [P, S])
        sin32 = place("sin32", [P, S])
        NPAR = 56
        pall = place("pall", [P, DEPTH * NPAR])
        pcur = place("pcur", [P, NPAR])
        lngb = place("lngb", [P, DEPTH, 2, W])
        bsp = place("bsp", [P, DEPTH, 2, P])
        U = place("U", [P, KT, S])
        aq = place("aq", [P, 2, S])
        ak = place("ak", [P, 2, S])
        av = place("av", [P, TT, W])
        cq = place("cq", [P, 2, S])
        ck = place("ck", [P, 2, S])
        cv = place("cv", [P, TT, W])
        keep = place("keep", [P, 9 * P])
        rstd = place("rstd", [P, S])
        small = place("small", [P, 64])
        stats = place("stats", [P, TT, 8])
        sp = place("sp", [P, 10 * P])
        wt = place("wt", [P, 10 * P])
        o_hi = place("o_hi", [P, KT, S], F32R)
        o_lo = place("o_lo", [P, KT, S], F32R)
        assert top[0] <= nc.sbuf_usable_end, (top[0], nc.sbuf_usable_end)
        eb = addr["o_hi"]
        raw = place("raw", [P, 6, S], at=eb)
        rt = place("rt", [P, 2, S], at=eb + 12288)
        relu = place("relu", [P, 4, S], at=eb + 16384)
        iqk = place("iqk", [P, 2, S], at=eb + 24576)
        dvt = place("dvt", [P, TT, W], at=eb + 28672)
        az = place("az", [P, 10 * P], at=eb)
        ws = place("ws", [P, 4, P], at=eb + 8192)
        cvt = place("cvt", [P, 2, S], at=eb + 16384)
        probs = place("probs", [P, 2, S], at=addr["sp"])
        probT = place("probT", [P, 2, S], at=addr["sp"] + 4096)
        th = place("th", [P, 4, S], at=addr["sp"])
        mtmp = place("mtmp", [P, 1, S], at=addr["sp"] + 8192)
        ptok = place("ptok", [P, 2, S], at=addr["aq"])
        pT_hi = place("pT_hi", [P, 2, S], F32R, at=addr["cq"])
        pT_lo = place("pT_lo", [P, 2, S], F32R, at=addr["ck"])
        sq = place("sq", [P, KT, S], at=eb)
        embedded = place("embedded", [P, KT, S], at=eb + 16384)
        posb = place("posb", [P, S], I32, at=eb)
        ang = place("ang", [P, 4, S], at=eb + 2048)
        onehot = place("onehot", [32, 640], at=addr["U"])
        rel = place("rel", [32, 16], at=addr["U"] + 2560)
        lnmult = place("lnmult", [16, 640], at=addr["U"] + 4096)
        biasv = place("biasv", [16, 640], at=addr["U"] + 8192)
        freq = place("freq", [P, 4], at=addr["small"])

        turns = place("turns", [P, S], at=eb + 10240)


        KB = 1024
        y_hi = place("y_hi", [P, KT, S], F32R, at=R2)
        y_lo = place("y_lo", [P, KT, S], F32R, at=R2 + 16 * KB)
        sq2 = place("sq2", [P, KT, S], at=R2)
        qkv = place("qkv", [P, 2, 3, 2 * S], at=R2 + 32 * KB)
        rstd2 = place("rstd2", [P, S], at=R2 + 44 * KB)
        ybuf = place("ybuf", [P, 2, S], at=R2 + 56 * KB)
        zt = place("zt", [P, 2, S], at=R2 + 60 * KB)
        mst = place("mst", [P, 2, S], at=R2 + 64 * KB)
        probs2 = place("probs2", [P, 2, S], at=R2 + 68 * KB)
        probT2 = place("probT2", [P, 2, S], at=R2 + 72 * KB)
        small2 = place("small2", [P, 64], at=R2 + 76 * KB)
        assert R2 + 76 * KB + 256 <= nc.sbuf_usable_end
        xm = place("xm", [P, 2, 2, S], at=R2)
        xc = place("xc", [P, 2, 2, S], at=R2 + 8 * KB)
        q2 = place("q2", [P, 2, 2, S], at=R2 + 16 * KB)
        k2 = place("k2", [P, 2, 2, S], at=R2 + 24 * KB)
        cth = place("cth", [P, 2, S], at=R2 + 48 * KB)
        v2 = place("v2", [P, 2, TT, W], at=R2 + 56 * KB)
        wraw = place("wraw", [P, 2, 3, 16, 4], at=R2 + 64 * KB)
        wif = place("wif", [P, 48, 8], at=R2 + 64 * KB + 1536)
        bd = place("bd", [P, 4, 3, P], at=R2 + 64 * KB + 3072)
        bdT = place("bdT", [P, 2, 3, P], at=R2 + 64 * KB + 9216)
        gt = place("gt", [8, 4, S], at=R2 + 48 * KB)
        yacc = place("yacc", [P, KT, S], at=R2)
        qh = place("qh", [P, 4, S], at=R2 + 16 * KB)
        kh = place("kh", [P, 4, S], at=R2 + 24 * KB)
        vh = place("vh", [P, TT, S], at=R2 + 32 * KB)
        xch = place("xch", [P, 4, S], at=R2 + 40 * KB)
        pm = place("pm", [P, 10 * P], at=R2 + 48 * KB)
        yh_hi = place("yh_hi", [P, 4, S], F32R, at=R2 + 56 * KB)
        yh_lo = place("yh_lo", [P, 4, S], F32R, at=R2 + 64 * KB)
        hstats = place("hstats", [P, TT, 8], at=R2 + 72 * KB)
        negM = place("negM", [4, S], at=R2 + 73 * KB)
        negM_h = place("negM_h", [4, S], at=R2 + 53 * KB)
        mrg = place("mrg", [P, KT, S], at=R2 + 16 * KB)
        sqf = place("sqf", [P, KT, S], at=R2 + 32 * KB)
        th2 = place("th2", [P, 4, S], at=R2 + 48 * KB)
        rstd3 = place("rstd3", [P, S], at=R2 + 56 * KB)
        bias_s = nc.dram_tensor("bias_s", [16, 640], F32, kind="Internal").ap()
        skew_s = nc.dram_tensor("skew_s", [16, P, 640], F32, kind="Internal").ap()
        m_s = nc.dram_tensor("m_s", [P, KT, S], F32, kind="Internal").ap()
        q_s, k_s, xc_s = (nc.dram_tensor(n, [P, 16, S], F32, kind="Internal").ap() for n in ("q_s", "k_s", "xc_s"))
        v_s = nc.dram_tensor("v_s", [P, TT, 4 * S], F32, kind="Internal").ap()

        const_loads = [(consts[:, :, :], a["consts"]), (freq[:, 0:2], a["freq"]), (pall[:, :], a["par1"].rearrange("p l n -> p (l n)")),
                       (par2[:, :], a["par2"]), (onehot[:, :], a["onehot"]), (rel[:, :], a["rel_bias"]), (lnmult[:, :], a["lnmult"]),
                       (bif[:, :], a["b_if"]), (mask4[:, :], a["mask4"]), (posb[:, :], a["positions"][0:1, :].broadcast_to((P, S)))]
        for l in range(DEPTH):
            for i, t in enumerate(("ln_g", "ln_b")):
                const_loads.append((lngb[:, l, i, :], a[t][l:l + 1, :].broadcast_to((P, W))))
            for g in range(4):
                const_loads.append((bsp[64 * (g % 2):64 * (g % 2) + 64, l, g // 2, :],
                                    a["b_spatial"][l, g:g + 1, :].broadcast_to((64, P))))
        NCONST = len(const_loads)
        SETUP_ANGLES, SETUP_DVE = 20, 20
        N_IN0, N_OUT0, HEAD_G, SKIP, GATE_B, CONV_B, CONV_W = 0, 8, 16, 32, 48, 64, 80

        banks = [ctx.enter_context(nc.psum_tensor(f"bank{b}", [P, 512], F32)) for b in range(8)]

        def sem(name):
            return ctx.enter_context(nc.semaphore(name))

        w_landed = [sem(f"w_landed{i}") for i in range(2)]
        w_rounded = sem("w_rounded")
        w_split = sem("w_split")
        full = [sem(f"full{b}") for b in range(8)]
        emptied = [sem(f"emptied{b}") for b in range(8)]
        const_in = sem("const_in")
        bias_product, bias_stored, skewed = sem("bias_product"), sem("bias_stored"), sem("skewed")
        mst_in = [sem("mst_in0"), sem("mst_in1")]
        bd_in = sem("bd_in")
        pexp2, pn2 = sem("pexp2"), sem("pn2")
        z_tanh = sem("z_tanh")
        yb_ready, yb_rounded, yb_split = sem("yb_ready"), sem("yb_rounded"), sem("yb_split")
        m_ready = sem("m_ready")
        bd_ready = sem("bd_ready")
        conv_ready, conv_tanh, xc_ready = sem("conv_ready"), sem("conv_tanh"), sem("xc_ready")
        stored = [sem("stored0"), sem("stored1")]
        zero_ready = sem("zero_ready")
        g_rows, g_abs, g_ln, g_neg, g_cols, g_em = (sem(n) for n in ("g_rows", "g_abs", "g_ln", "g_neg", "g_cols", "g_em"))
        mh_ready = sem("mh_ready")
        head_in = sem("head_in")
        e_ready, e_exp = sem("e_ready"), sem("e_exp")
        skipped = sem("skipped")
        hn_var, hn_rstd, hn_ready = sem("hn_var"), sem("hn_rstd"), sem("hn_ready")
        zm_tanh = sem("zm_tanh")
        yh_ready, yh_rounded, yh_split = sem("yh_ready"), sem("yh_rounded"), sem("yh_split")
        mrg_in = sem("mrg_in")
        fm_ready = sem("fm_ready")
        xo_ready = sem("xo_ready")
        out_ready = sem("out_ready")
        x_in = sem("x_in")
        relu_step = sem("relu_step")
        setup_dve = sem("setup_dve")
        setup_act = sem("setup_act")
        pcur_ready = sem("pcur_ready")
        x_ready = sem("x_ready")
        sq_ready = sem("sq_ready")
        var_ready = sem("var_ready")
        rstd_ready = sem("rstd_ready")
        h_ready = sem("h_ready")
        h_rounded = sem("h_rounded")
        h_split = sem("h_split")
        rot_ready = sem("rot_ready")
        relu_used = sem("relu_used")
        ws_in = sem("ws_in")
        p_in = sem("p_in")
        vn_ready = sem("vn_ready")
        od_ready = sem("od_ready")
        z_ln = sem("z_ln")
        sp_ready = sem("sp_ready")
        cw_ready = sem("cw_ready")
        cw_exp = sem("cw_exp")
        pexp = sem("pexp")
        pn_ready = sem("pn_ready")
        th_ready = sem("th_ready")
        o_f32 = sem("o_f32")
        o_rounded = sem("o_rounded")
        o_split = sem("o_split")
        merged = sem("merged")
        pt_rounded = sem("pt_rounded")
        pt_split = sem("pt_split")
        ws_ready = sem("ws_ready")
        dve_step = sem("dve_step")
        act_step = sem("act_step")
        y_out = sem("y_out")

        block = ctx.enter_context(nc.Block())

        WOFF = [0, 4 * P, 7 * P, 9 * P]
        KOFF = {3: 0, 2: 4 * P, 1: 7 * P}
        G_PRE, G_POST, BM, CW, CB = 0, 8, 16, 48, 54

        def wait_full(eng, l, key, back=0):
            b, n = now[0].side[key]
            eng.wait_ge(full[b], l * now[0].nb[b] + (now[0].b0[b] + n + 1 - back * now[0].nb[b]))
            return banks[b]

        def wait_empty(eng, l, key):
            b, n = now[0].side[key]
            eng.wait_ge(emptied[b], l * now[0].nb[b] + (now[0].b0[b] + n))
            return banks[b]

        def wait_emptied(eng, l, key):
            b, n = now[0].side[key]
            eng.wait_ge(emptied[b], l * now[0].nb[b] + (now[0].b0[b] + n + 1))

        def acc_count(l, g, n):
            return l * (now[0].ng // 4) + ((now[0].g0 + g) // 4 + n + 1)

        def acc_full(eng, l, g):
            eng.wait_ge(full[g % 4], acc_count(l, g, 1))
            return banks[g % 4]

        def acc_empty(eng, l, g):
            eng.wait_ge(emptied[g % 4], acc_count(l, g, 0))
            return banks[g % 4]

        def acc_emptied(eng, l, g):
            eng.wait_ge(emptied[g % 4], acc_count(l, g, 1))

        def chunk_count(l, c, n=1):
            return l * now[0].n + (now[0].c0 + c + n)

        def split_count(l, c, n=1):
            return chunk_count(l, c, n + 2)


        def second_loads(sp_, load):
            def bias_of(n):
                src = bass.AP(tensor=skew_s.tensor, offset=n * P * 640 + 127, ap=[[639, P], [1, S]])
                sp_.dma_start(mst[:, n % 2, :], src).then_inc(mst_in[n % 2], 16)

            now[0] = ATTN
            for c in range(ATTN.n):
                load(0, c)
                if c == 1:
                    sp_.wait_ge(x_ready, DEPTH * 8 + 8)
                    sp_.wait_ge(skewed, 16)
                    bias_of(0)
                    bias_of(1)
                n = c - 2
                if 2 <= n < 16:
                    wait_emptied(sp_, 0, ("L", (n - 2) % 4, 3, (n - 2) // 4))
                    bias_of(n)
                if c == 20:
                    now[0] = ATTN
                    wait_full(sp_, 0, ("AO", 3, 3))
                    sp_.dma_start(wraw[:, :, :, :, :], a["wqkv"]).then_inc(bd_in, 16)
                    sp_.dma_start(wif[:, :, :], a["w_if"]).then_inc(bd_in, 16)
            now[0] = MPROJ
            with sp_.Fori(0, MPROJ.rounds) as r:
                load(r, 0)
                load(r, 1)
            now[0] = MHEAD
            with sp_.Fori(0, MHEAD.rounds) as h:
                for c in range(MHEAD.n):
                    load(h, c)
            now[0] = TAIL
            for c in range(TAIL.n):
                load(0, c)
            now[0] = LAYERS

        def second_products(pe, product, weights, act, part):
            now[0] = ATTN
            wait_empty(pe, 0, "ssx")
            for k in range(KT):
                pe.wait_ge(sq_ready, DEPTH * 16 + k + 1)
                last = pe.matmul(banks[4][:, :], ones, sq2[:, k, :], start=k == 0, stop=k == KT - 1)
            last.then_inc(full[4], 1)

            def logits(i, m, tt):
                out = wait_empty(pe, 0, ("L", m, tt, i))
                rows = slice(64 * (m % 2), 64 * (m % 2) + 64)
                o = (m // 2) * S
                pe.matmul(out[:, 0:(tt + 1) * P], qkv[rows, i % 2, 0, o + tt * P:o + (tt + 1) * P],
                          qkv[rows, i % 2, 1, o:o + (tt + 1) * P], start=True, stop=True).then_inc(full[4 + tt % 2], 1)

            def turn(i, m, tt):
                out = wait_empty(pe, 0, ("T", m, tt, i))
                pe.wait_ge(pn2, 16 * i + 4 * m + tt + 1)
                for j in range(tt + 1):
                    last = pe.transpose(out[:, j * P:(j + 1) * P], probs2[:, tt % 2, j * P:(j + 1) * P], ident)
                last.then_inc(full[6], 1)

            def values(i, m, tt):
                if tt == 0:
                    wait_empty(pe, 0, ("AO", m, i))
                wait_emptied(pe, 0, ("T", m, tt, i))
                rows = slice(64 * (m % 2), 64 * (m % 2) + 64)
                for j in range(tt + 1):
                    last = pe.matmul(banks[7][rows, tt * P:(tt + 1) * P], qkv[:, i % 2, 2, j * W + 64 * m:j * W + 64 * m + 64],
                                     probT2[:, tt % 2, j * P:(j + 1) * P], start=j == 0, stop=j == tt)
                if tt == 3:
                    last.then_inc(full[7], 1)

            for c in range(ATTN.n):
                if ATTN.chunks[c] == ("pa", 0):
                    pe.wait_ge(yb_split, 8)
                for s in range(8):
                    part(0, c, s)
                    if 3 <= c < 19:
                        i, m = (c - 3) // 4, (c - 3) % 4
                        if s == 0:
                            if m == 0:
                                for cc in ((1, 2) if i == 0 else (c - 3, c - 2)):
                                    for g in ATTN.groups[cc]:
                                        acc_emptied(pe, 0, g)
                            logits(i, m, 0)
                            logits(i, m, 1)
                        if s == 2:
                            turn(i, m, 0)
                            logits(i, m, 2)
                        if s == 3:
                            turn(i, m, 1)
                            values(i, m, 0)
                            logits(i, m, 3)
                        if s == 4:
                            turn(i, m, 2)
                            values(i, m, 1)
                        if s == 5:
                            turn(i, m, 3)
                            values(i, m, 2)
                        if s == 6:
                            values(i, m, 3)

            def tile_step(r, t, step):
                u, b = t // 2, t % 2
                if step == 0:
                    out = wait_empty(pe, r, ("fold", t))
                    pe.wait_ge(bd_ready, r * 4 + (t + 1))
                    for m in range(3):
                        last = pe.matmul(out[:, 8 * (m // 2):8 * (m // 2) + 8], bdT[:, b, m, :],
                                         wif[:, ds(4 * r + (16 * m + t), 1), :].rearrange("p o c -> p (o c)"),
                                         start=m != 1, stop=m != 0)
                    last.then_inc(full[4], 1)
                if step == 1:
                    pe.wait_ge(xc_ready, r * 4 + (t + 1))
                    for m, key in ((0, "qm"), (1, "km")):
                        out = wait_empty(pe, r, (key, t))
                        pe.matmul(out[:, :], bd[:, t, m, :], xc[:, u, b, :], start=True, stop=True).then_inc(full[4 + m], 1)
                if step == 2:
                    wait_emptied(pe, r, ("fold", t))
                    for n, x in ((0, xc), (8, xm)):
                        pe.matmul(banks[7][0:8, :], small2[:, 16 * b + n:16 * b + n + 8], x[:, u, b, :],
                                  start=False, stop=False, skip_group_check=True)
                if step == 3:
                    out = wait_empty(pe, r, ("vm", t))
                    for tt in range(TT):
                        last = pe.matmul(out[:, tt * P:(tt + 1) * P], xm[:, u, b, tt * P:(tt + 1) * P], bd[:, t, 2, :],
                                         start=True, stop=True)
                    last.then_inc(full[6], 1)

            now[0] = MGATE
            wait_empty(pe, 0, "gates")
            pe.wait_ge(zero_ready, 1)
            pe.matmul(banks[7][0:8, :], small2[:, 32:40], xT[:, 0, :], start=True, stop=False, skip_group_check=True)
            now[0] = MPROJ
            for s in range(8):
                part(0, 0, s)
            with pe.Fori(0, MPROJ.rounds - 1) as r:
                for s in range(8):
                    part(r, 1, s)
                    tile_step(r, s // 4, s % 4)
                for s in range(8):
                    part(r + 1, 0, s)
                    tile_step(r, 2 + s // 4, s % 4)
            r = MPROJ.rounds - 1
            for s in range(8):
                part(r, 1, s)
                tile_step(r, s // 4, s % 4)
            for s in range(8):
                tile_step(r, 2 + s // 4, s % 4)
            now[0] = MGATE
            pe.matmul(banks[7][0:8, :], small2[:, 32:40], xT[:, 0, :], start=False, stop=True,
                      skip_group_check=True).then_inc(full[7], 1)
            wait_emptied(pe, 0, "gates")
            out = wait_empty(pe, 0, "f")
            pe.matmul(out[0:4, :], ident[0:8, 4:8], gt[0:8, 0, :], start=True, stop=True).then_inc(full[4], 1)
            out = wait_empty(pe, 0, "cols")
            pe.wait_ge(g_neg, 1)
            for n, t in ((0, 1), (16, 3)):
                for tt in range(TT):
                    last = pe.transpose(out[:, n + 4 * tt:n + 4 * tt + 4], gt[0:4, t, tt * P:(tt + 1) * P], ident[0:4, 0:4])
            last.then_inc(full[5], 1)

            now[0] = MHEAD

            def scores(h, bank):
                out = wait_empty(pe, h, ("sc", bank))
                js = (2, 3) if bank == 2 else (bank,)
                for j in js:
                    o = out[:, WOFF[j] - WOFF[js[0]]:WOFF[j] - WOFF[js[0]] + S - j * P]
                    for e in range(4):
                        last = pe.matmul(o, kh[:, e, j * P:(j + 1) * P], qh[:, e, j * P:S], start=e == 0, stop=e == 3)
                last.then_inc(full[4 + bank], 1)

            def weight_of(j, tt):
                return pm[:, WOFF[j] + (tt - j) * P:WOFF[j] + (tt - j + 1) * P]

            def denominators(h):
                for bank in range(3):
                    wait_emptied(pe, h, ("sc", bank))
                out = wait_empty(pe, h, "den")
                for tt in range(TT):
                    for j in range(tt + 1):
                        last = pe.matmul(out[:, tt:tt + 1], weight_of(j, tt), ones[:, 0:1], start=j == 0, stop=j == tt)
                last.then_inc(full[7], 1)

            def numerators(h, tt):
                out = wait_empty(pe, h, ("num", tt))
                for j in range(tt + 1):
                    last = pe.matmul(out[:, :], weight_of(j, tt), vh[:, j, :], start=j == 0, stop=j == tt)
                last.then_inc(full[4 + tt % 2], 1)

            def turn_h(h, tt):
                out = wait_empty(pe, h, ("hT", tt))
                pe.wait_ge(hn_ready, h * 4 + (tt + 1))
                for e in range(4):
                    last = pe.transpose(out[:, e * P:(e + 1) * P], qh[:, tt, e * P:(e + 1) * P], ident)
                last.then_inc(full[6 + tt % 2], 1)

            def head(h):
                for c in range(4):
                    for s in range(8):
                        part(h, c, s)
                        if c == 0 and s == 0:
                            out = wait_empty(pe, h, "M")
                            pe.wait_ge(mh_ready, h + 1)
                            pe.matmul(out[:, :], ones[0:4, :], negM_h[:, :],
                                      start=True, stop=True).then_inc(full[7], 1)
                        if c == 0 and 1 <= s <= 3:
                            if s == 1:
                                pe.wait_ge(head_in, h * 64 + 64)
                            scores(h, s - 1)
                        if c == 1 and s == 6:
                            denominators(h)
                        if c == 2 and s in (0, 1, 3, 4):
                            numerators(h, {0: 0, 1: 1, 3: 2, 4: 3}[s])
                        if c == 3 and 2 <= s <= 5:
                            turn_h(h, s - 2)
                for c in (4, 5):
                    pe.wait_ge(w_split, split_count(h, c))
                    for k in range(4):
                        if c == 4:
                            pe.wait_ge(yh_split, h * 4 + (k + 1))
                        for n, g in enumerate(MHEAD.groups[c]):
                            if k == 0:
                                acc_empty(pe, h, g)
                            last = product(banks[g % 4][:, :], [(weights(c, k * S + n * P, P), (yh_hi[:, k, :], yh_lo[:, k, :]))],
                                           k == 0, k == 3)
                            if k == 3:
                                last.then_inc(full[g % 4], 1)

            with pe.Fori(0, MHEAD.rounds - 1) as h:
                head(h)
            head(MHEAD.rounds - 1)

            now[0] = TAIL
            for c in range(TAIL.n):
                for s in range(8):
                    part(0, c, s)
            wait_empty(pe, 0, "ssf")
            for k in range(KT):
                pe.wait_ge(sq_ready, DEPTH * 16 + 8 + k + 1)
                last = pe.matmul(banks[4][:, :], ones, sqf[:, k, :], start=k == 0, stop=k == KT - 1)
            last.then_inc(full[4], 1)
            now[0] = LAYERS

        def second_scalar(act, round_weights):
            def evacuate(l, g, dst, func=ACT.Copy, scale=1.0, bias=0.0):
                src = acc_full(act, l, g)
                act.activation(dst, src[:, 0:S], func, scale=scale, bias=bias).then_inc(emptied[g % 4], 1)

            def move(l, key, dst, src, scale=1.0):
                wait_full(act, l, key)
                act.activation(dst, src, ACT.Copy, scale=scale).then_inc(emptied[now[0].side[key][0]], 1)

            now[0] = ATTN
            act.wait_ge(x_ready, DEPTH * 8 + 8)
            for k in range(KT):
                act.activation(sq2[:, k, :], xT[:, k, :], ACT.Square).then_inc(sq_ready, 1)
            act.wait_ge(var_ready, DEPTH * 3 + 1)
            act.activation(rstd2[:, :], rstd2[:, :], ACT.Sqrt).then_inc(rstd_ready, 1)
            for k in range(KT):
                act.wait_ge(h_ready, DEPTH * 16 + k + 1)
                act.activation(h_hi[:, k, :], sq2[:, k, :], ACT.Copy).then_inc(h_rounded, 1)

            def exps(i, m, tt):
                wait_emptied(act, 0, ("L", m, tt, i))
                n = (tt + 1) * P
                act.activation(probs2[:, tt % 2, 0:n], probs2[:, tt % 2, 0:n], ACT.Exp, scale=-1.0,
                               bias=small2[:, tt:tt + 1], accum_out=small2[:, 4 + tt:5 + tt]).then_inc(pexp2, 1)

            def turned(i, m, tt):
                n = (tt + 1) * P
                move(0, ("T", m, tt, i), probT2[:, tt % 2, 0:n], banks[6][:, 0:n])

            def project(c, b):
                kind, i = ATTN.chunks[c]
                g = ATTN.groups[c][b]
                if kind in "qkv":
                    evacuate(0, g, qkv[:, i % 2, "qkv".index(kind), b * S:(b + 1) * S], scale=0.125 if kind == "q" else 1.0)
                elif kind == "z":
                    src = acc_full(act, 0, g)
                    if i > 0:
                        act.wait_ge(yb_ready, 2 * (i - 1) + b + 1)
                    act.activation(zt[:, b, :], src[:, :], ACT.Tanh, scale=0.5).then_inc(z_tanh, 1)
                elif kind == "ga":
                    evacuate(0, g, gate_tile(2 * i + b), ACT.Tanh, 0.5, par2[:, GATE_B + 2 * i + b:GATE_B + 2 * i + b + 1])

            for c in range(ATTN.n):
                if 3 <= c < 19:
                    i, m = (c - 3) // 4, (c - 3) % 4
                    exps(i, m, 0)
                    exps(i, m, 1)
                    turned(i, m, 0)
                    exps(i, m, 2)
                    turned(i, m, 1)
                    project(c, 0)
                    exps(i, m, 3)
                    turned(i, m, 2)
                    turned(i, m, 3)
                    rows = slice(64 * (m % 2), 64 * (m % 2) + 64)
                    if i > 0:
                        act.wait_ge(yb_split, 2 * i)
                    move(0, ("AO", m, i), ybuf[rows, m // 2, :], banks[7][rows, :])
                    project(c, 1)
                else:
                    project(c, 0)
                    project(c, 1)
                if c + 2 < ATTN.n:
                    round_weights(0, c + 2)
                else:
                    now[0] = MPROJ
                    round_weights(0, c + 2 - ATTN.n)
                    now[0] = ATTN
                if 3 <= c < 19 and m == 3:
                    for b in range(2):
                        act.wait_ge(yb_ready, 2 * i + b + 1)
                        act.activation(y_hi[:, 2 * i + b, :], ybuf[:, b, :], ACT.Copy).then_inc(yb_rounded, 1)
                if ATTN.chunks[c][0] == "pa":
                    d = ATTN.chunks[c][1]
                    act.wait_ge(m_ready, 2 * d + 2)
                    for b in range(2):
                        act.dma_start(m_s[:, 2 * d + b, :], gate_tile(2 * d + b)).then_inc(stored[b], 16)

            now[0] = MPROJ

            def conv_in(r, u, b):
                evacuate(r, MPROJ.groups[u][b], xm[:, u, b, :])

            def conv_out(r, t):
                act.wait_ge(conv_ready, r * 4 + (t + 1))
                act.activation(cth[:, t % 2, :], xc[:, t // 2, t % 2, :], ACT.Tanh).then_inc(conv_tanh, 1)

            def fold_move(r, t):
                b = t % 2
                move(r, ("fold", t), small2[:, 16 * b:16 * b + 16], banks[4][:, 0:16])

            def qk_moves(r, t):
                u, b = t // 2, t % 2
                if b == 0:
                    act.wait_ge(stored[u], r * 64 + 64)
                move(r, ("qm", t), q2[:, u, b, :], banks[4][:, :])
                move(r, ("km", t), k2[:, u, b, :], banks[5][:, :])

            def v_move(r, t):
                u, b = t // 2, t % 2
                move(r, ("vm", t), v2[:, u, :, b * P:(b + 1) * P], banks[6][:, :].rearrange("p (t n) -> p t n", t=TT))

            def store(r, u):
                for key in ("qm", "km", "vm"):
                    wait_emptied(act, r, (key, 2 * u + 1))
                for dst, src in ((q_s, q2), (k_s, k2), (xc_s, xc)):
                    act.dma_start(dst[:, ds(4 * r + 2 * u, 2), :], src[:, u, :, :]).then_inc(stored[u], 16)
                act.dma_start(v_s[:, :, ds(4 * r * P + 2 * u * P, 2 * P)], v2[:, u, :, :]).then_inc(stored[u], 16)

            def chunk_moves(r, t0, rr, u):
                fold_move(r, t0)
                round_next(r, t0 // 2)
                qk_moves(r, t0)
                v_move(r, t0)
                if rr is not None:
                    conv_in(rr, u, 0)
                fold_move(r, t0 + 1)
                qk_moves(r, t0 + 1)
                if rr is not None:
                    conv_out(rr, 2 * u)
                    conv_in(rr, u, 1)
                v_move(r, t0 + 1)
                store(r, t0 // 2)
                if rr is not None:
                    conv_out(rr, 2 * u + 1)

            def round_next(r, u):
                if isinstance(r, int) and r == MPROJ.rounds - 1:
                    now[0] = MHEAD
                    round_weights(0, u)
                    now[0] = MPROJ
                else:
                    round_weights(r + 1, u)

            conv_in(0, 0, 0)
            conv_in(0, 0, 1)
            conv_out(0, 0)
            conv_out(0, 1)
            with act.Fori(0, MPROJ.rounds - 2) as r:
                chunk_moves(r, 0, r, 1)
                chunk_moves(r, 2, r + 1, 0)
            r = MPROJ.rounds - 2
            chunk_moves(r, 0, r, 1)
            chunk_moves(r, 2, r + 1, 0)
            r = MPROJ.rounds - 1
            chunk_moves(r, 0, r, 1)
            chunk_moves(r, 2, None, None)
            now[0] = MGATE
            wait_full(act, 0, "f")
            act.activation(gt[0:4, 1, :], banks[4][0:4, :], ACT.Abs).then_inc(g_abs, 1)
            act.wait_ge(g_abs, 1)
            act.activation(gt[0:4, 1, :], gt[0:4, 1, :], ACT.Exp, scale=-1.0).then_inc(g_abs, 1)
            act.wait_ge(g_abs, 2)
            act.activation(gt[0:4, 1, :], gt[0:4, 1, :], ACT.Ln, bias=1.0).then_inc(g_ln, 1)
            wait_emptied(act, 0, "cols")
            act.activation(small2[:, 16:32], small2[:, 16:32], ACT.Exp).then_inc(g_em, 1)

            now[0] = MHEAD

            def load_head(h):
                for dst, src in ((qh, q_s), (kh, k_s), (xch, xc_s)):
                    act.dma_start(dst[:, :, :], src[:, ds(4 * h, 4), :]).then_inc(head_in, 16)
                act.dma_start(vh[:, :, :], v_s[:, :, ds(h * S, S)]).then_inc(head_in, 16)

            def head(h, last=False):
                act.wait_ge(head_in, h * 64 + 64)
                for e in range(4):
                    act.activation(xch[:, e, :], xch[:, e, :], ACT.Copy,
                                   scale=par2[:, ds(4 * h + (SKIP + e), 1)]).then_inc(skipped, 1)
                act.wait_ge(e_ready, h + 1)
                act.activation(pm[:, :], pm[:, :], ACT.Exp).then_inc(e_exp, 1)
                wait_full(act, h, ("sc", 2))
                for c in range(2):
                    for b in range(2):
                        g = MHEAD.groups[c][b]
                        src = acc_full(act, h, g)
                        act.activation(qh[:, 2 * b:2 * b + 2, c * W:(c + 1) * W], src[:, :].rearrange("p (t n) -> p t n", t=2),
                                       ACT.Tanh, scale=0.5).then_inc(emptied[g % 4], 1)
                    round_weights(h, c + 2)
                for c in (2, 3):
                    for b in range(2):
                        g = MHEAD.groups[c][b]
                        src = acc_full(act, h, g)
                        act.activation(kh[:, 2 * (c - 2) + b, :], src[:, :], ACT.Tanh, scale=0.5).then_inc(zm_tanh, 1)
                        if c == 2 and b == 1:
                            act.wait_ge(hn_var, h + 1)
                            act.activation(small2[:, 48:52], small2[:, 48:52], ACT.Sqrt).then_inc(hn_rstd, 1)
                    if c == 2:
                        round_weights(h, 4)
                for e in range(4):
                    act.wait_ge(yh_ready, h * 4 + (e + 1))
                    act.activation(yh_hi[:, e, :], xch[:, e, :], ACT.Copy).then_inc(yh_rounded, 1)
                round_weights(h, 5)
                if not last:
                    act.wait_ge(yh_split, h * 4 + 4)
                    load_head(h + 1)
                    round_weights(h + 1, 0)
                    round_weights(h + 1, 1)
                else:
                    now[0] = TAIL
                    act.wait_ge(yh_split, h * 4 + 4)
                    act.dma_start(mrg[:, :, :], m_s).then_inc(mrg_in, 16)
                    round_weights(0, 0)
                    round_weights(0, 1)

            for u in range(2):
                act.wait_ge(stored[u], MPROJ.rounds * 64 + 64)
            load_head(0)
            with act.Fori(0, MHEAD.rounds - 1) as h:
                head(h)
            head(MHEAD.rounds - 1, True)

            now[0] = TAIL
            for d in range(4):
                for b in range(2):
                    if d >= 2:
                        act.wait_ge(fm_ready, 2 * (d - 2) + b + 1)
                    n = GATE_B + 8 + 2 * d + b
                    evacuate(0, TAIL.groups[d][b], th2[:, 2 * (d % 2) + b, :], ACT.Tanh, 0.5, par2[:, n:n + 1])
                round_weights(0, d + 2)
            for k in range(KT):
                act.wait_ge(fm_ready, k + 1)
                act.activation(h_hi[:, k, :], yacc[:, k, :], ACT.Copy).then_inc(h_rounded, 1)
            for d in range(4):
                for b in range(2):
                    k = 2 * d + b
                    act.wait_ge(xo_ready, k + 1)
                    act.activation(sqf[:, k, :], xT[:, k, :], ACT.Square).then_inc(sq_ready, 1)
                if d < 2:
                    round_weights(0, d + 6)
            act.wait_ge(var_ready, DEPTH * 3 + 2)
            act.activation(rstd3[:, :], rstd3[:, :], ACT.Sqrt).then_inc(rstd_ready, 1)
            for k in range(KT):
                act.wait_ge(out_ready, k + 1)
                act.dma_start(a["out"][:, k, :], yacc[:, k, :]).then_inc(y_out, 16)
            act.wait_ge(y_out, 16 * KT)
            now[0] = LAYERS

        def gate_tile(d):
            n = d // 2
            return qkv[:, 0, n, (d % 2) * S:(d % 2 + 1) * S] if n < 3 else qkv[:, 1, 0, (d % 2) * S:(d % 2 + 1) * S]

        def second_vector(dve):
            step = [0]

            def begin():
                step[0] = 0
                dve.sem_clear(dve_step)

            def link(ins):
                step[0] += 1
                ins.then_inc(dve_step, 1)
                dve.wait_ge(dve_step, step[0])

            def inverse_mean(key, t):
                src = wait_full(dve, 0, key)
                dve.tensor_scalar(t[:, :], src[:, :], 1.0 / D, EPS, ALU.mult, ALU.add).then_inc(emptied[4], 1)
                wait_emptied(dve, 0, key)
                dve.reciprocal(t[:, :], t[:, :]).then_inc(var_ready, 1)

            now[0] = ATTN
            begin()
            inverse_mean("ssx", rstd2)
            dve.wait_ge(rstd_ready, DEPTH * 3 + 1)
            for k in range(KT):
                dve.scalar_tensor_tensor(sq2[:, k, :], xT[:, k, :], par2[:, N_IN0 + k:N_IN0 + k + 1], rstd2[:, :],
                                         ALU.mult, ALU.mult).then_inc(h_ready, 1)

            def biased(i, m, tt):
                src = wait_full(dve, 0, ("L", m, tt, i))
                n = 4 * i + m
                if tt == 0:
                    dve.wait_ge(mst_in[n % 2], 16 * (n // 2 + 1))
                if tt >= 2:
                    wait_full(dve, 0, ("T", m, tt - 2, i))
                elif n > 0:
                    wait_full(dve, 0, ("T", (n - 1) % 4, tt + 2, (n - 1) // 4))
                w = (tt + 1) * P
                dve.tensor_tensor_reduce(probs2[:, tt % 2, 0:w], src[:, 0:w], mst[:, n % 2, S - w:S], -1.0, 3.0e38,
                                         ALU.add, ALU.min, small2[:, tt:tt + 1]).then_inc(emptied[4 + tt % 2], 1)

            def normalize(i, m, tt):
                w = (tt + 1) * P
                dve.wait_ge(pexp2, 16 * i + 4 * m + tt + 1)
                link(dve.reciprocal(small2[:, 8 + tt:9 + tt], small2[:, 4 + tt:5 + tt]))
                dve.tensor_scalar(probs2[:, tt % 2, 0:w], probs2[:, tt % 2, 0:w], small2[:, 8 + tt:9 + tt], None,
                                  ALU.mult).then_inc(pn2, 1)

            for c in range(ATTN.n):
                kind, j = ATTN.chunks[c]
                if 3 <= c < 19:
                    i, m = (c - 3) // 4, (c - 3) % 4
                    biased(i, m, 0)
                    biased(i, m, 1)
                    normalize(i, m, 0)
                    biased(i, m, 2)
                    normalize(i, m, 1)
                    if m == 3:
                        zg = ATTN.groups[c]
                        dve.wait_ge(z_tanh, 2 * i + 1)
                        dve.scalar_tensor_tensor(zt[:, 0, :], zt[:, 0, :], 1.0, banks[zg[0] % 4][:, :], ALU.add, ALU.mult)\
                           .then_inc(emptied[zg[0] % 4], 1)
                    biased(i, m, 3)
                    normalize(i, m, 2)
                    normalize(i, m, 3)
                    if m == 3:
                        dve.wait_ge(z_tanh, 2 * i + 2)
                        dve.scalar_tensor_tensor(zt[:, 1, :], zt[:, 1, :], 1.0, banks[zg[1] % 4][:, :], ALU.add, ALU.mult)\
                           .then_inc(emptied[zg[1] % 4], 1)
                        wait_emptied(dve, 0, ("AO", m, i))
                        for b in range(2):
                            acc_emptied(dve, 0, zg[b])
                            dve.scalar_tensor_tensor(ybuf[:, b, :], ybuf[:, b, :], 0.5, zt[:, b, :], ALU.mult,
                                                     ALU.mult).then_inc(yb_ready, 1)
                if kind == "pa":
                    for b in range(2):
                        d = 2 * j + b
                        g = ATTN.groups[c][b]
                        src = acc_full(dve, 0, g)
                        link(dve.scalar_tensor_tensor(gate_tile(d), gate_tile(d), 1.0, src[:, :], ALU.add, ALU.mult))
                        dve.sem_inc(emptied[g % 4], 1)
                        dve.sem_inc(m_ready, 1)

            now[0] = MPROJ
            dve.memset(small2[:, 32:40], 0.0).then_inc(zero_ready, 1)
            dve.wait_ge(bd_in, 32)

            def blocks(r, t):
                b = t % 2
                if b == 0:
                    wait_full(dve, r, ("vm", t + 1), back=1)
                wait_full(dve, r, ("fold", (t - 2) % 4), back=int(t < 2))
                for m in range(3):
                    for n, out in ((0, bd[:, t, m, :]), (1, bdT[:, b, m, :])):
                        w = wraw[:, n, m, ds(4 * r + t, 1), :].broadcast_to((P, 32, 4))
                        ins = dve.tensor_tensor(out.rearrange("p (g o) -> p g o", o=4),
                                                mask4[:, :].unsqueeze(2).broadcast_to((P, 32, 4)), w, ALU.mult)
                ins.then_inc(bd_ready, 1)

            def conv(r, t):
                u, b = t // 2, t % 2
                o, x = xc[:, u, b, :], xm[:, u, b, :]
                acc_emptied(dve, r, MPROJ.groups[u][b])
                if b == 0:
                    dve.wait_ge(stored[u], r * 64 + 64)

                def par(n):
                    return par2[:, ds(4 * r + (n + t), 1)]

                link(dve.tensor_scalar(o, x, par(CONV_W + 48), par(CONV_B), ALU.mult, ALU.add))
                for k in range(3):
                    n = 3 - k
                    ins = dve.scalar_tensor_tensor(o[:, n:S], x[:, 0:S - n], par(CONV_W + 16 * k), o[:, n:S], ALU.mult, ALU.add)
                    if k < 2:
                        link(ins)
                    else:
                        ins.then_inc(conv_ready, 1)
                dve.wait_ge(conv_tanh, r * 4 + (t + 1))
                dve.scalar_tensor_tensor(o, cth[:, b, :], 1.0, o, ALU.add, ALU.mult).then_inc(xc_ready, 1)

            with dve.Fori(0, MPROJ.rounds) as r:
                begin()
                for t in range(4):
                    blocks(r, t)
                    conv(r, t)

            now[0] = MGATE
            begin()
            wait_full(dve, 0, "gates")
            dve.tensor_scalar(gt[0:8, 0, :], banks[7][0:8, :], bif[:, 0:1], None, ALU.add).then_inc(emptied[7], 1)
            wait_emptied(dve, 0, "gates")
            dve.wait_ge(g_ln, 1)
            dve.scalar_tensor_tensor(gt[0:4, 2, :], banks[4][0:4, :], 0.0, gt[0:4, 1, :], ALU.min, ALU.subtract)\
               .then_inc(emptied[4], 1)
            wait_emptied(dve, 0, "f")
            link(dve.tensor_tensor_scan(gt[0:4, 3, :], ones[0:4, 0:1].broadcast_to((4, S)), gt[0:4, 2, :], 0.0, ALU.mult, ALU.add))
            link(dve.tensor_tensor(gt[0:4, 1, :], gt[0:4, 0, :], gt[0:4, 3, :], ALU.subtract))
            link(dve.tensor_tensor_scan(gt[0:4, 2, :], gt[0:4, 1, :], gt[0:4, 1, :], 0.0, ALU.max, ALU.max))
            dve.scalar_tensor_tensor(gt[0:4, 3, :], gt[0:4, 3, :], -1.0, gt[0:4, 2, :], ALU.mult, ALU.subtract).then_inc(g_neg, 1)
            link(dve.tensor_scalar(negM[:, :], gt[0:4, 2, :], -1.0, None, ALU.mult))
            wait_full(dve, 0, "cols")
            dve.tensor_copy(small2[:, 0:32], banks[5][:, 0:32]).then_inc(emptied[5], 1)
            wait_emptied(dve, 0, "cols")
            for u in range(2):
                dve.wait_ge(stored[u], MPROJ.rounds * 64 + 64)
            link(dve.memset(yacc[:, :, :], 0.0))
            dve.wait_ge(g_em, 1)

            now[0] = MHEAD

            def head(h):
                begin()
                dve.tensor_scalar(negM_h[:, :], negM[:, :], ident[0:4, ds(h, 1)], None, ALU.mult).then_inc(mh_ready, 1)
                src = wait_full(dve, h, "M")
                for j in range(TT):
                    ins = dve.tensor_scalar(pm[:, WOFF[j]:WOFF[j] + S - j * P], src[:, j * P:S],
                                            small2[:, ds(h + 4 * j, 1)], 0.0, ALU.add, ALU.min)
                    if j == 3:
                        ins.then_inc(emptied[7], 1)
                wait_emptied(dve, h, "M")
                for j in range(TT):
                    ins = dve.tensor_tensor(pm[:, WOFF[j]:WOFF[j] + P], pm[:, WOFF[j]:WOFF[j] + P], trilT_add, ALU.add)
                    if j == 3:
                        ins.then_inc(e_ready, 1)
                dve.wait_ge(e_exp, h + 1)
                for bank in range(3):
                    src = wait_full(dve, h, ("sc", bank))
                    n = (512, 384, 384)[bank]
                    o = pm[:, WOFF[bank]:WOFF[bank] + n]
                    dve.scalar_tensor_tensor(o, src[:, 0:n], 512.0 ** -0.5, o, ALU.mult, ALU.mult).then_inc(emptied[4 + bank], 1)
                wait_full(dve, h, "den")
                d, r = small2[:, 40:44], small2[:, 44:48]
                dve.tensor_copy(d, banks[7][:, 0:4]).then_inc(emptied[7], 1)
                wait_emptied(dve, h, "den")
                link(dve.scalar_tensor_tensor(r, d, -1.0, d, ALU.mult, ALU.max))
                em = small2[:, 16:32].rearrange("p (t h) -> p t h", h=4)[:, :, ds(h, 1)].rearrange("p t o -> p (t o)")
                link(dve.tensor_tensor(r, r, em, ALU.max))
                link(dve.reciprocal(r, r))
                link(dve.tensor_scalar(r, r, 0.5, None, ALU.mult))
                for tt in range(TT):
                    src = wait_full(dve, h, ("num", tt))
                    if tt == 0:
                        for c in (0, 1):
                            for g in MHEAD.groups[c]:
                                acc_emptied(dve, h, g)
                    dve.scalar_tensor_tensor(qh[:, tt, :], qh[:, tt, :], 1.0, src[:, :], ALU.add, ALU.mult)\
                       .then_inc(emptied[4 + tt % 2], 1)
                    wait_emptied(dve, h, ("num", tt))
                    link(dve.bn_stats(hstats[:, tt, 0:6], qh[:, tt, :]))
                    link(dve.bn_aggr(hstats[:, tt, 6:8], hstats[:, tt, 0:6]))
                    if tt == 1:
                        silu_z(h, 2, 0)
                v = small2[:, 48:52]
                link(dve.tensor_tensor(v, hstats[:, :, 7], r, ALU.mult))
                link(dve.tensor_tensor(v, v, r, ALU.mult))
                link(dve.tensor_scalar(v, v, EPS, None, ALU.add))
                dve.reciprocal(v, v).then_inc(hn_var, 1)
                silu_z(h, 2, 1)
                dve.wait_ge(hn_rstd, h + 1)
                link(dve.tensor_tensor(v, v, r, ALU.mult))
                for tt in range(TT):
                    dve.tensor_scalar(qh[:, tt, :], qh[:, tt, :], hstats[:, tt, 6:7], v[:, tt:tt + 1], ALU.subtract,
                                      ALU.mult).then_inc(hn_ready, 1)
                silu_z(h, 3, 0)
                dve.wait_ge(skipped, h * 4 + 4)
                for tt in range(TT):
                    src = wait_full(dve, h, ("hT", tt))
                    for e in range(4):
                        o = xch[:, e, tt * P:(tt + 1) * P]
                        ins = dve.scalar_tensor_tensor(o, src[:, e * P:(e + 1) * P], par2[:, ds(4 * h + (HEAD_G + e), 1)], o,
                                                       ALU.mult, ALU.add)
                        if e == 3:
                            ins.then_inc(emptied[6 + tt % 2], 1)
                    wait_emptied(dve, h, ("hT", tt))
                silu_z(h, 3, 1)
                for e in range(4):
                    dve.scalar_tensor_tensor(xch[:, e, :], xch[:, e, :], 0.5, kh[:, e, :], ALU.mult, ALU.mult).then_inc(yh_ready, 1)
                for c in (4, 5):
                    for n, g in enumerate(MHEAD.groups[c]):
                        d = 4 * (c - 4) + n
                        src = acc_full(dve, h, g)
                        dve.tensor_tensor(yacc[:, d, :], src[:, :], yacc[:, d, :], ALU.add).then_inc(emptied[g % 4], 1)
                        acc_emptied(dve, h, g)

            def silu_z(h, c, b):
                g = MHEAD.groups[c][b]
                e = 2 * (c - 2) + b
                dve.wait_ge(zm_tanh, h * 4 + (e + 1))
                dve.scalar_tensor_tensor(kh[:, e, :], kh[:, e, :], 1.0, banks[g % 4][:, :], ALU.add, ALU.mult)\
                   .then_inc(emptied[g % 4], 1)
                acc_emptied(dve, h, g)

            with dve.Fori(0, MHEAD.rounds - 1) as h:
                head(h)
            head(MHEAD.rounds - 1)

            now[0] = TAIL
            begin()
            dve.wait_ge(mrg_in, 16)
            for k in range(KT):
                acc_emptied(dve, 0, TAIL.groups[k // 2][k % 2])
                link(dve.scalar_tensor_tensor(yacc[:, k, :], th2[:, k % 4, :], 1.0, yacc[:, k, :], ALU.add, ALU.mult))
                dve.tensor_tensor(yacc[:, k, :], yacc[:, k, :], mrg[:, k, :], ALU.add).then_inc(fm_ready, 1)
            for k in range(KT):
                g = TAIL.groups[4 + k // 2][k % 2]
                src = acc_full(dve, 0, g)
                link(dve.scalar_tensor_tensor(xT[:, k, :], src[:, :], 0.5, xT[:, k, :], ALU.mult, ALU.add))
                dve.sem_inc(emptied[g % 4], 1)
                dve.sem_inc(xo_ready, 1)
            inverse_mean("ssf", rstd3)
            dve.wait_ge(rstd_ready, DEPTH * 3 + 2)
            for k in range(KT):
                dve.scalar_tensor_tensor(yacc[:, k, :], xT[:, k, :], par2[:, N_OUT0 + k:N_OUT0 + k + 1], rstd3[:, :],
                                         ALU.mult, ALU.mult).then_inc(out_ready, 1)
            now[0] = LAYERS

        def second_pool(pool, split_weights):
            def split(dst, src, hi, rounded, n, signal):
                pool.wait_ge(rounded, n)
                pool.tensor_tensor(dst, src, hi, ALU.subtract).then_inc(signal, 1)

            now[0] = ATTN
            for k in range(KT):
                split(h_lo[:, k, :], sq2[:, k, :], h_hi[:, k, :], h_rounded, DEPTH * 24 + k + 1, h_split)
            for c in range(ATTN.n):
                if c + 2 < ATTN.n:
                    split_weights(0, c + 2)
                if 3 <= c < 19 and (c - 3) % 4 == 3:
                    i = (c - 3) // 4
                    for b in range(2):
                        split(y_lo[:, 2 * i + b, :], ybuf[:, b, :], y_hi[:, 2 * i + b, :], yb_rounded, 2 * i + b + 1, yb_split)
            now[0] = MPROJ
            with pool.Fori(0, MPROJ.rounds) as r:
                split_weights(r, 0)
                split_weights(r, 1)
            now[0] = MHEAD

            def head(h, last=False):
                for c in range(2, 5):
                    split_weights(h, c)
                for e in range(4):
                    split(yh_lo[:, e, :], xch[:, e, :], yh_hi[:, e, :], yh_rounded, h * 4 + (e + 1), yh_split)
                split_weights(h, 5)
                if last:
                    now[0] = TAIL
                    split_weights(0, 0)
                    split_weights(0, 1)
                else:
                    split_weights(h + 1, 0)
                    split_weights(h + 1, 1)

            split_weights(0, 0)
            split_weights(0, 1)
            with pool.Fori(0, MHEAD.rounds - 1) as h:
                head(h)
            head(MHEAD.rounds - 1, True)
            for c in range(2, 6):
                split_weights(0, c)
            for k in range(KT):
                split(h_lo[:, k, :], yacc[:, k, :], h_hi[:, k, :], h_rounded, DEPTH * 24 + 8 + k + 1, h_split)
            for c in (6, 7):
                split_weights(0, c)
            now[0] = LAYERS

        @block.sync
        def _(sp_):
            def load(l, c):
                slot, n = c % 2, columns(now[0].chunks[c])
                sp_.wait_ge(w_split, split_count(l, c, -1))
                src = a["stream"][ds(l * now[0].n + (now[0].c0 + c), 1), :, 0:n].rearrange("o p n -> p (o n)")
                sp_.dma_start(w_raw[:, slot, 0:n], src).then_inc(w_landed[slot], 16)

            with sp_.Fori(0, DEPTH) as l:
                for c in range(NCH):
                    load(l, c)
                    if c == 4:
                        sp_.wait_ge(rot_ready, l * 6 + 6)
                        sp_.dma_start(ws[:, :, :], a["wsT"][:, ds(l, 1), :, :].rearrange("s o g t -> s (o g) t")).then_inc(ws_in, 16)
                    if c == 18:
                        sp_.wait_ge(full[7], l * LAYERS.nb[7] + (LAYERS.nb[7] + 1))
                        sp_.dma_start(ptok[:, :, :], a["pT"][:, ds(l, 1), :, :].rearrange("p o i t -> p (o i) t")).then_inc(p_in, 16)
            second_loads(sp_, load)

        @block.tensor
        def _(pe):
            def product(out, pairs, start, stop):
                n = 3 * len(pairs)
                i = 0
                for (a_hi, a_lo), (b_hi, b_lo) in pairs:
                    for lhsT, rhs in ((a_hi, b_hi), (a_hi, b_lo), (a_lo, b_hi)):
                        last = pe.matmul(out, lhsT, rhs, start=start and i == 0, stop=stop and i == n - 1)
                        i += 1
                return last

            def weights(c, col, n):
                return w_hi[:, c % 2, col:col + n], w_lo[:, c % 2, col:col + n]

            def act(k, cols=slice(0, S)):
                return h_hi[:, k, cols], h_lo[:, k, cols]

            def part(l, c, s):
                kind, i = now[0].chunks[c]
                if s == 0:
                    pe.wait_ge(w_split, split_count(l, c))
                b = s // 4
                g = now[0].groups[c][b]
                if s % 4 == 0:
                    acc_empty(pe, l, g)
                acc = banks[g % 4]
                if i in TOKEN_MAJOR or kind in ("v", "om"):
                    tt, half = 2 * b + s % 4 // 2, s % 2
                    last = product(acc[:, (tt % 2) * W:(tt % 2 + 1) * W],
                                   [(act(k, slice(tt * P, (tt + 1) * P)), weights(c, k * W, W))
                                    for k in range(4 * half, 4 * half + 4)], half == 0, half == 1)
                else:
                    stride = 260 if i == "idx" else W
                    for k in (2 * (s % 4), 2 * (s % 4) + 1):
                        first = {("proj", "aq"): 0, ("out", 0): 8, ("pgate", 0): 16, ("q", 0): DEPTH * 24,
                                 ("fo", 0): DEPTH * 24 + 8}.get((kind, i))
                        if s < 4 and first is not None:
                            pe.wait_ge(h_split, l * 24 + (first + k + 1))
                        x = (y_hi[:, k, :], y_lo[:, k, :]) if kind == "pa" else act(k)
                        last = product(acc[:, :], [(weights(c, k * stride + b * P, P), x)], k == 0, k == KT - 1)
                if s % 4 == 3:
                    last.then_inc(full[g % 4], 1)

            def rotate(l, key, mat, src):
                out = wait_empty(pe, l, key)
                pe.matmul(out[:, :], mat, src, start=True, stop=True).then_inc(full[now[0].side[key][0]], 1)

            def index_logits(l, tt):
                n = (tt + 1) * P
                for h in range(4):
                    out = wait_empty(pe, l, ("idx", tt, h))
                    rows = slice(32 * h, 32 * h + 32)
                    pe.matmul(out[:, 0:n], iqk[rows, 0, tt * P:(tt + 1) * P], iqk[rows, 1, 0:n],
                              start=True, stop=True).then_inc(full[4 + h], 1)

            def c_scores(l, h, what):
                rows = slice(64 * (h % 2), 64 * (h % 2) + 64)
                i = h // 2
                for bank in range(3):
                    out = wait_empty(pe, l, (what, h, bank))
                    js = (2, 3) if bank == 2 else (bank,)
                    for j in js:
                        o = out[:, WOFF[j] - WOFF[js[0]]:WOFF[j] - WOFF[js[0]] + S - j * P]
                        last = pe.matmul(o, ck[rows, i, j * P:(j + 1) * P], cq[rows, i, j * P:S],
                                         start=True, stop=what == "Z")
                        if what == "Sx":
                            for jj in range(j, TT):
                                last = pe.matmul(o[:, (jj - j) * P:], upinc_neg if jj == j else ones_neg,
                                                 sp[:, WOFF[jj]:WOFF[jj] + S - jj * P], start=False, stop=jj == TT - 1)
                    last.then_inc(full[4 + bank], 1)

            def c_values(l, h):
                out = wait_empty(pe, l, ("CO", h))
                rows = slice(64 * (h % 2), 64 * (h % 2) + 64)
                for j in range(TT):
                    last = pe.matmul(out[rows, j * P:S], cv[:, j, 64 * h:64 * h + 64],
                                     wt[:, WOFF[j]:WOFF[j] + S - j * P], start=j == 0, stop=j == TT - 1)
                last.then_inc(full[7], 1)

            def d_mix(l):
                pe.wait_ge(ws_ready, l + 1)
                pe.wait_ge(vn_ready, l + 1)
                for i in range(2):
                    out = wait_empty(pe, l, ("dmix", i))
                    for g in (2 * i, 2 * i + 1):
                        rows = slice(64 * (g % 2), 64 * (g % 2) + 64)
                        for tt in range(TT):
                            last = pe.matmul(out[rows, tt * P:(tt + 1) * P], dvt[:, tt, 64 * g:64 * g + 64],
                                             ws[:, g, :], start=True, stop=True)
                    last.then_inc(full[4 + i], 1)

            def a_logits(l, tt, h):
                out = wait_empty(pe, l, ("L", tt, h))
                rows = slice(64 * (h % 2), 64 * (h % 2) + 64)
                pe.matmul(out[:, 0:(tt + 1) * P], aq[rows, h // 2, tt * P:(tt + 1) * P],
                          ak[rows, h // 2, 0:(tt + 1) * P], start=True, stop=True).then_inc(full[4 + h % 2], 1)

            def a_transpose(l, tt, h):
                out = wait_empty(pe, l, ("T", tt, h))
                pe.wait_ge(pn_ready, l * 16 + (4 * tt + h + 1))
                for j in range(tt + 1):
                    last = pe.transpose(out[:, j * P:(j + 1) * P], probs[:, h % 2, j * P:(j + 1) * P], ident)
                last.then_inc(full[6], 1)

            def a_values(l, tt, h):
                if h == 0:
                    wait_empty(pe, l, ("AO", tt))
                wait_emptied(pe, l, ("T", tt, h))
                rows = slice(64 * (h % 2), 64 * (h % 2) + 64)
                for j in range(tt + 1):
                    last = pe.matmul(banks[7][rows, (h // 2) * P:(h // 2 + 1) * P], av[:, j, 64 * h:64 * h + 64],
                                     probT[:, h % 2, j * P:(j + 1) * P], start=j == 0, stop=j == tt)
                if h == 3:
                    last.then_inc(full[7], 1)

            def side(l, c, s):
                if c == 1 and s == 0:
                    for i in range(2):
                        acc_emptied(pe, l, GROUPS[0][i])
                        rotate(l, f"rotq{i}", rot64, raw[:, i, :])
                if c == 2 and s == 0:
                    for i in range(2):
                        acc_emptied(pe, l, GROUPS[1][i])
                        rotate(l, f"rotk{i}", rot64, raw[:, 2 + i, :])
                if c == 2 and s == 7:
                    out = wait_empty(pe, l, "iw")
                    for tt in range(TT):
                        last = product(out[:, 4 * tt:4 * tt + 4],
                                       [(act(k, slice(tt * P, (tt + 1) * P)), weights(2, k * 260 + 256, 4))
                                        for k in range(KT)], True, True)
                    last.then_inc(full[6], 1)
                if c == 3 and s == 0:
                    for i in range(2):
                        acc_emptied(pe, l, GROUPS[2][i])
                        rotate(l, f"roti{i}", rot32, raw[:, 4 + i, :])
                if c == 4 and s in (0, 3, 6):
                    if s == 0:
                        pe.wait_ge(rot_ready, l * 6 + 6)
                    index_logits(l, 3 - s // 3)
                if 8 <= c < 12:
                    h = c - 8
                    if s == 0:
                        if h == 2:
                            d_mix(l)
                        if h == 0:
                            for g in (GROUPS[5] + GROUPS[6]):
                                acc_emptied(pe, l, g)
                        c_scores(l, h, "Z")
                    if s == 4:
                        pe.wait_ge(sp_ready, l * 4 + (h + 1))
                        c_scores(l, h, "Sx")
                    if s == 7:
                        pe.wait_ge(cw_exp, l * 4 + (h + 1))
                        c_values(l, h)
                if 12 <= c < 16:
                    tt = c - 12
                    if s == 0:
                        a_logits(l, tt, 0)
                        a_logits(l, tt, 1)
                    if s == 2:
                        a_transpose(l, tt, 0)
                        a_logits(l, tt, 2)
                    if s == 3:
                        a_transpose(l, tt, 1)
                        a_values(l, tt, 0)
                        a_logits(l, tt, 3)
                    if s == 4:
                        a_transpose(l, tt, 2)
                        a_values(l, tt, 1)
                    if s == 5:
                        a_transpose(l, tt, 3)
                        a_values(l, tt, 2)
                    if s == 6:
                        a_values(l, tt, 3)
                if 40 < c < 44 and s in (1, 5):
                    sum_squares_y(l, 2 * (c - 41) + s // 4)

            def sum_squares_y(l, e):
                if e == 0:
                    wait_empty(pe, l, "ssy")
                pe.wait_ge(sq_ready, l * 16 + (8 + e + 1))
                last = pe.matmul(banks[6][:, :], ones, sq[:, e, :], start=e == 0, stop=e == KT - 1)
                if e == KT - 1:
                    last.then_inc(full[6], 1)

            def branches(l, c):
                pe.wait_ge(w_split, split_count(l, c))
                if c == 18:
                    pe.wait_ge(o_split, l * 8 + 8)
                for n, g in enumerate(GROUPS[c]):
                    acc_empty(pe, l, g)
                    product(banks[g % 4][:, :], [(weights(c, (2 * n + kk) * P, P),
                                                  (o_hi[:, 2 * n + kk, :], o_lo[:, 2 * n + kk, :]))
                                                 for kk in range(2)], True, True).then_inc(full[g % 4], 1)

            def embedding(l, c):
                pe.wait_ge(w_split, split_count(l, c))
                if c == 44:
                    pe.wait_ge(pt_split, l * 2 + 2)
                for b, g in enumerate(GROUPS[c]):
                    acc_empty(pe, l, g)
                    product(banks[g % 4][:, :], [(weights(c, kk * S + b * P, P), (pT_hi[:, kk, :], pT_lo[:, kk, :]))
                                                 for kk in range(2)], True, True).then_inc(full[g % 4], 1)

            for b in range(8):
                pe.sem_inc(full[b], 1)
            pe.wait_ge(const_in, 16 * NCONST)
            pe.matmul(banks[0][0:16, :], rel[:, :], onehot[:, 0:512], start=True, stop=True)
            pe.matmul(banks[1][0:16, 0:128], rel[:, :], onehot[:, 512:640], start=True, stop=True).then_inc(bias_product, 1)
            pe.wait_ge(setup_dve, 3)
            with pe.Fori(0, DEPTH) as l:
                wait_empty(pe, l, "ssx")
                for k in range(KT):
                    pe.wait_ge(sq_ready, l * 16 + (k + 1))
                    last = pe.matmul(banks[4][:, :], ones, U[:, k, :], start=k == 0, stop=k == KT - 1)
                last.then_inc(full[4], 1)
                for c, (kind, i) in enumerate(CH):
                    if kind == "branch":
                        branches(l, c)
                    elif kind == "ple":
                        embedding(l, c)
                    else:
                        for s in range(8):
                            part(l, c, s)
                            side(l, c, s)
                    if c == 43:
                        sum_squares_y(l, 6)
                        sum_squares_y(l, 7)
            second_products(pe, product, weights, act, part)

        @block.scalar
        def _(act):
            for k in range(KT):
                act.dma_start(xT[:, k, :], a["xT"][:, k, :]).then_inc(x_in, 16)
            for dst, src in const_loads:
                act.dma_start(dst, src).then_inc(const_in, 16)
            act.wait_ge(setup_dve, SETUP_ANGLES)
            for i, t in enumerate((sin64, cos64, sin32, cos32)):
                act.activation(t[:, :], ang[:, i, :], ACT.Sin).then_inc(setup_act, 1)

            def round_weights(l, c):
                slot = c % 2
                act.wait_ge(w_landed[slot], (l * (now[0].n // 2) + ((now[0].c0 + c) // 2 + 1)) * 16)
                start = now[0].groups[c][0]
                between = now[0].groups[c - 1] if c else now[0].before_first if type(l) is int and l == 0 else now[0].groups[-1]
                before = start - len(between) - 1
                act.wait_ge(full[before % 4], acc_count(l, before, 1))
                n = columns(now[0].chunks[c])
                act.activation(w_hi[:, slot, 0:n], w_raw[:, slot, 0:n], ACT.Copy).then_inc(w_rounded, 1)

            def round_ahead(l, c):
                if c < NCH:
                    round_weights(l, c)
                else:
                    round_weights(l + 1, c - NCH)

            def evacuate(l, g, dst, scale=1.0):
                src = acc_full(act, l, g)
                act.activation(dst, src[:, :], ACT.Copy, scale=scale).then_inc(emptied[g % 4], 1)

            def move_side(l, key, dst, src, func=ACT.Copy, scale=1.0):
                wait_full(act, l, key)
                act.activation(dst, src, func, scale=scale).then_inc(emptied[now[0].side[key][0]], 1)

            def square_root(l, n, t):
                act.wait_ge(var_ready, l * 3 + n)
                act.activation(t, t, ACT.Sqrt).then_inc(rstd_ready, 1)

            def round_tile(l, k, first, src):
                act.activation(h_hi[:, k, :], src, ACT.Copy).then_inc(h_rounded, 1)

            def a_exp(l, tt, h):
                wait_emptied(act, l, ("L", tt, h))
                n = (tt + 1) * P
                act.activation(probs[:, h % 2, 0:n], probs[:, h % 2, 0:n], ACT.Exp, scale=-1.0,
                               bias=small[:, 24 + h:25 + h], accum_out=small[:, 28 + h:29 + h]).then_inc(pexp, 1)

            def a_move(l, tt, h):
                move_side(l, ("T", tt, h), probT[:, h % 2, 0:(tt + 1) * P], banks[6][:, 0:(tt + 1) * P])

            def index_relu(l, tt):
                for h in range(4):
                    if tt < 3:
                        act.wait_ge(relu_used, l * 12 + (4 * (2 - tt) + h + 1))
                    n = (tt + 1) * P
                    move_side(l, ("idx", tt, h), relu[:, h, 0:n], banks[4 + h][:, 0:n], ACT.Relu)

            def c_exp(l, h):
                act.wait_ge(cw_ready, l * 4 + (h + 1))
                act.activation(wt[:, :], wt[:, :], ACT.Exp).then_inc(cw_exp, 1)

            def gate_tanh(l, c, b):
                g = GROUPS[c][b]
                src = acc_full(act, l, g)
                if c > 12:
                    act.wait_ge(o_f32, l * 8 + 2 * (c - 12))
                act.activation(cvt[:, b, :], src[:, :], ACT.Tanh, scale=0.5).then_inc(th_ready, 1)

            def round_branch(l, c):
                n = int(CH[c][1][1])
                for b in range(2):
                    act.wait_ge(o_f32, l * 8 + (2 * (c - 12) + b + 1))
                    act.activation(o_hi[:, 2 * n + b, :], U[:, 2 * n + b, :], ACT.Copy).then_inc(o_rounded, 1)

            act.wait_ge(bias_stored, 16)
            round_weights(0, 0)
            round_weights(0, 1)
            with act.Fori(0, DEPTH) as l:
                act.wait_ge(x_ready, l * 8 + 8)
                for k in range(KT):
                    act.activation(U[:, k, :], xT[:, k, :], ACT.Square).then_inc(sq_ready, 1)
                square_root(l, 1, rstd[:, :])
                for k in range(KT):
                    act.wait_ge(h_ready, l * 16 + (k + 1))
                    round_tile(l, k, 0, U[:, k, :])
                for c in range(16):
                    name = CH[c][1]
                    g0, g1 = GROUPS[c]
                    if c == 9:
                        square_root(l, 2, small[:, 16:20])
                    if 8 <= c < 12:
                        h = c - 8
                        for bank in range(3):
                            src = wait_full(act, l, ("Z", h, bank))
                            n = (512, 384, 384)[bank]
                            o = WOFF[bank]
                            act.activation(az[:, o:o + n], src[:, 0:n], ACT.Abs).then_inc(act_step, 1)
                        act.wait_ge(act_step, l * 16 + (4 * h + 3))
                        act.activation(az[:, :], az[:, :], ACT.Exp, scale=-1.0).then_inc(act_step, 1)
                        act.wait_ge(act_step, l * 16 + (4 * h + 4))
                        act.activation(az[:, :], az[:, :], ACT.Ln, bias=1.0).then_inc(z_ln, 1)
                    if 12 <= c:
                        tt = c - 12
                        a_exp(l, tt, 0)
                        a_exp(l, tt, 1)
                        a_move(l, tt, 0)
                        a_exp(l, tt, 2)
                        a_move(l, tt, 1)
                    dst = {"aq": raw[:, 0:2, :], "ak": raw[:, 2:4, :], "idx": raw[:, 4:6, :], "cq": cq, "ck": ck,
                           "du": U[:, 6:8, :], "bc": U[:, 2:4, :]}.get(name)
                    if name in TOKEN_MAJOR:
                        t = {"av": av, "cv": cv, "dv": dvt}[name]
                        for b in range(2):
                            evacuate(l, GROUPS[c][b], t[:, 2 * b:2 * b + 2, :].rearrange("p t n -> p (t n)"))
                    elif dst is not None:
                        for b in range(2):
                            if c == 4:
                                index_relu(l, 3 - b)
                            if 8 <= c < 12 and b == 1:
                                c_exp(l, c - 8)
                            evacuate(l, GROUPS[c][b], dst[:, b, :], scale=0.125 if name in ("aq", "cq") else 1.0)
                    elif c >= 12:
                        gate_tanh(l, c, 0)
                        a_exp(l, tt, 3)
                        a_move(l, tt, 2)
                        a_move(l, tt, 3)
                        move_side(l, ("AO", tt), U[:, 0:2, tt * P:(tt + 1) * P],
                                  banks[7][:, 0:2 * P].rearrange("p (i t) -> p i t", i=2))
                        gate_tanh(l, c, 1)
                    else:
                        c_exp(l, c - 8)
                    if name == "idx":
                        move_side(l, "iw", small[:, 0:16], banks[6][:, 0:16], scale=(4 * 32) ** -0.5)
                    if c == 4:
                        index_relu(l, 1)
                    if 8 <= c < 12:
                        h = c - 8
                        rows = slice(64 * (h % 2), 64 * (h % 2) + 64)
                        move_side(l, ("CO", h), U[rows, 4 + h // 2, :], banks[7][rows, :])
                    round_weights(l, c + 2)
                    if c >= 13:
                        round_branch(l, c - 1)
                round_branch(l, 15)
                for d in range(KT):
                    c = 16 + 3 * d
                    for n in range(4):
                        g = GROUPS[c + n // 2][n % 2]
                        src = acc_full(act, l, g)
                        if n == 0 and d > 0:
                            act.wait_ge(merged, l * 8 + d)
                        act.activation(th[:, n, :], src[:, :], ACT.Tanh, scale=0.5,
                                       bias=pcur[:, BM + 8 * n + d:BM + 8 * n + d + 1]).then_inc(emptied[g % 4], 1)
                        if n % 2:
                            round_weights(l, c + n // 2 + 2)
                    if d == 2:
                        act.wait_ge(p_in, l * 16 + 16)
                        for i in range(2):
                            act.activation(pT_hi[:, i, :], ptok[:, i, :], ACT.Copy).then_inc(pt_rounded, 1)
                    if d < 7:
                        round_weights(l, c + 4)
                for k in range(KT):
                    act.wait_ge(merged, l * 8 + (k + 1))
                    round_tile(l, k, 8, U[:, k, :])
                round_weights(l, 41)
                for c in range(40, 44):
                    for b, g in enumerate(GROUPS[c]):
                        e = 2 * (c - 40) + b
                        src = acc_full(act, l, g)
                        act.activation(sq[:, e, :], src[:, :], ACT.Square).then_inc(sq_ready, 1)
                        act.activation(U[:, e, :], src[:, :], ACT.Copy).then_inc(emptied[g % 4], 1)
                    round_weights(l, c + 2)
                square_root(l, 3, rstd[:, :])
                for k in range(KT):
                    evacuate(l, GROUPS[44 + k // 4][k % 4], embedded[:, k, :])
                    if k == 3:
                        round_weights(l, 46)
                    if k >= 4:
                        act.wait_ge(h_ready, l * 16 + (8 + k - 3))
                        round_tile(l, k - 4, 16, xT[:, k - 4, :])
                for k in range(4, KT):
                    act.wait_ge(h_ready, l * 16 + (8 + k + 1))
                    round_tile(l, k, 16, xT[:, k, :])
                round_weights(l, 47)
                for e in range(4):
                    for b, g in enumerate(GROUPS[46 + e]):
                        src = acc_full(act, l, g)
                        if e > 0:
                            act.wait_ge(x_ready, l * 8 + (8 + 2 * (e - 1) + b + 1))
                        act.activation(th[:, b, :], src[:, :], ACT.Tanh, scale=0.5).then_inc(emptied[g % 4], 1)
                    round_ahead(l, 48 + e)
            second_scalar(act, round_weights)

        @block.vector
        def _(dve):
            setup = [0]

            def sstep(ins):
                setup[0] += 1
                ins.then_inc(setup_dve, 1)
                dve.wait_ge(setup_dve, setup[0])

            for b in range(8):
                dve.sem_inc(emptied[b], 1)
            dve.wait_ge(const_in, 16 * NCONST)
            sstep(dve.tensor_scalar(par2[:, GATE_B:144], par2[:, GATE_B:144], 0.5, None, ALU.mult))
            dve.wait_ge(bias_product, 1)
            sstep(dve.tensor_tensor(biasv[:, 0:512], banks[0][0:16, :], lnmult[:, 0:512], ALU.add))
            sstep(dve.tensor_tensor(biasv[:, 512:640], banks[1][0:16, 0:128], lnmult[:, 512:640], ALU.add))
            pos = ang[:, 3, :]
            sstep(dve.tensor_copy(pos, posb[:, :]))
            ROUND = 1.5 * 2 ** 23
            for i in range(2):
                r, q = ang[:, 2 * i, :], turns[:, :]
                sstep(dve.tensor_scalar(r, pos, freq[:, i:i + 1], None, ALU.mult))
                sstep(dve.tensor_scalar(q, r, 0.15915494309189535, ROUND, ALU.mult, ALU.add))
                sstep(dve.tensor_scalar(q, q, ROUND, None, ALU.subtract))
                sstep(dve.scalar_tensor_tensor(r, q, -6.28125, r, ALU.mult, ALU.add))
                sstep(dve.scalar_tensor_tensor(r, q, -0.0019353071795864769, r, ALU.mult, ALU.add))
                sstep(dve.tensor_scalar(r, r, 3.1415925, -3.1415925, ALU.min, ALU.max))
            for i in range(2):
                r, c = ang[:, 2 * i, :], ang[:, 2 * i + 1, :]
                sstep(dve.scalar_tensor_tensor(c, r, -1.0, r, ALU.mult, ALU.max))
                sstep(dve.tensor_scalar(c, c, -1.0, 1.5707963267948966, ALU.mult, ALU.add))
            assert setup[0] == SETUP_ANGLES, setup
            dve.wait_ge(x_in, 16 * KT)
            for k in range(KT):
                dve.sem_inc(x_ready, 1)
            dve.wait_ge(setup_act, 4)

            steps = [0]

            def link(ins):
                steps[0] += 1
                ins.then_inc(dve_step, 1)
                dve.wait_ge(dve_step, steps[0])

            def inverse_mean(l, key, scale):
                src = wait_full(dve, l, key)
                dve.tensor_scalar(rstd[:, :], src[:, :], scale, EPS, ALU.mult, ALU.add).then_inc(emptied[now[0].side[key][0]], 1)
                wait_emptied(dve, l, key)
                dve.reciprocal(rstd[:, :], rstd[:, :]).then_inc(var_ready, 1)

            def rope(l, key, n, dst, src, cos, sin):
                rot = wait_full(dve, l, key)
                dve.tensor_tensor(rt[:, 0, :], src, cos[:, :], ALU.mult).then_inc(relu_step, 1)
                dve.tensor_tensor(rt[:, 1, :], rot[:, :], sin[:, :], ALU.mult).then_inc(emptied[now[0].side[key][0]], 1)
                dve.wait_ge(relu_step, l * 6 + (n + 1))
                wait_emptied(dve, l, key)
                dve.tensor_tensor(dst, rt[:, 0, :], rt[:, 1, :], ALU.add).then_inc(rot_ready, 1)
                dve.wait_ge(rot_ready, l * 6 + (n + 1))

            def index_scores(l, tt):
                n = (tt + 1) * P
                kp = keep[:, KOFF[tt]:KOFF[tt] + n]
                for h in range(4):
                    i = 4 * (3 - tt) + h
                    wait_emptied(dve, l, ("idx", tt, h))
                    w = small[:, 4 * tt + h:4 * tt + h + 1]
                    if h == 0:
                        dve.tensor_scalar(kp, relu[:, h, 0:n], w, None, ALU.mult).then_inc(relu_used, 1)
                    else:
                        dve.scalar_tensor_tensor(kp, relu[:, h, 0:n], w, kp, ALU.mult, ALU.add).then_inc(relu_used, 1)
                    dve.wait_ge(relu_used, l * 12 + (i + 1))
                link(dve.tensor_tensor(kp[:, n - P:n], kp[:, n - P:n], tri_neg, ALU.add))

            def top_keys(tt, rounds=range(P // 8)):
                n = (tt + 1) * P
                kp = keep[:, KOFF[tt]:KOFF[tt] + n]
                top8 = small[:, 36:44]
                for r in rounds:
                    link(dve.max(top8, kp))
                    link(dve.match_replace(kp, top8, kp, MARK))
                if rounds[-1] == P // 8 - 1:
                    link(dve.tensor_scalar(kp, kp, -3.1e38, NEG, ALU.is_gt, ALU.mult))

            def layer_norm(l):
                for g in GROUPS[7]:
                    acc_emptied(dve, l, g)
                for tt in range(TT):
                    link(dve.bn_stats(stats[:, tt, 0:6], dvt[:, tt, :]))
                    link(dve.bn_aggr(stats[:, tt, 6:8], stats[:, tt, 0:6]))
                link(dve.tensor_scalar(small[:, 16:20], stats[:, :, 7], EPS, None, ALU.add))
                dve.reciprocal(small[:, 16:20], small[:, 16:20]).then_inc(var_ready, 1)

            def layer_norm_apply(l):
                dve.wait_ge(rstd_ready, l * 3 + 2)
                for tt in range(TT):
                    v = dvt[:, tt, :]
                    link(dve.tensor_scalar(v, v, stats[:, tt, 6:7], small[:, 16 + tt:17 + tt], ALU.subtract, ALU.mult))
                    link(dve.tensor_tensor(v, v, lngb[:, ds(l, 1), 0, :].rearrange("p o n -> p (o n)"), ALU.mult))
                    ins = dve.tensor_tensor(v, v, lngb[:, ds(l, 1), 1, :].rearrange("p o n -> p (o n)"), ALU.add)
                    if tt < 3:
                        link(ins)
                    else:
                        ins.then_inc(vn_ready, 1)

            def d_weights(l):
                dve.wait_ge(ws_in, l * 16 + 16)
                dve.tensor_tensor(ws[:, :, :], ws[:, :, :], trilT.unsqueeze(1).broadcast_to((P, 4, P)),
                                  ALU.mult).then_inc(ws_ready, 1)

            def d_output(l):
                for g in GROUPS[8]:
                    acc_emptied(dve, l, g)
                for i in range(2):
                    src = wait_full(dve, l, ("dmix", i))
                    bias = bsp[:, ds(l, 1), i, :].broadcast_to((P, TT, P))
                    dve.tensor_tensor(rt[:, i, :].rearrange("p (t c) -> p t c", t=TT),
                                      src[:, :].rearrange("p (t c) -> p t c", t=TT), bias, ALU.add).then_inc(emptied[4 + i], 1)
                    wait_emptied(dve, l, ("dmix", i))
                    link(dve.tensor_tensor(U[:, 6 + i, :], rt[:, i, :], U[:, 6 + i, :], ALU.mult))

            def z_pieces(js):
                return [(WOFF[j], WOFF[j] - WOFF[js[0]], S - j * P) for j in js]

            def c_softplus(l, h):
                dve.wait_ge(z_ln, l * 4 + (h + 1))
                for bank in range(3):
                    n = (512, 384, 384)[bank]
                    o = WOFF[bank]
                    dve.scalar_tensor_tensor(sp[:, o:o + n], banks[4 + bank][:, 0:n], 0.0, az[:, o:o + n],
                                             ALU.max, ALU.add).then_inc(emptied[4 + bank], 1)
                for bank in range(3):
                    wait_emptied(dve, l, ("Z", h, bank))
                for j in range(TT):
                    ins = dve.tensor_tensor(sp[:, WOFF[j]:WOFF[j] + P], sp[:, WOFF[j]:WOFF[j] + P], trisT, ALU.mult)
                    if j == 3:
                        ins.then_inc(sp_ready, 1)

            def c_weights(l, h):
                for bank in range(3):
                    src = wait_full(dve, l, ("Sx", h, bank))
                    n = (512, 384, 384)[bank]
                    o = WOFF[bank]
                    dve.tensor_scalar(wt[:, o:o + n], src[:, 0:n], 0.0, None, ALU.min).then_inc(emptied[4 + bank], 1)
                for bank in range(3):
                    wait_emptied(dve, l, ("Sx", h, bank))
                for j in range(TT):
                    ins = dve.tensor_tensor(wt[:, WOFF[j]:WOFF[j] + P], wt[:, WOFF[j]:WOFF[j] + P], trisT_add, ALU.add)
                    if j == 3:
                        ins.then_inc(cw_ready, 1)

            def b_gate_x(l):
                for g in GROUPS[9]:
                    acc_emptied(dve, l, g)
                for b, g in enumerate(GROUPS[10]):
                    src = acc_full(dve, l, g)
                    dve.tensor_tensor(U[:, 2 + b, :], U[:, 2 + b, :], src[:, :], ALU.mult).then_inc(emptied[g % 4], 1)
                    acc_emptied(dve, l, g)

            def b_conv(l):
                for b in range(2):
                    y, o = U[:, 2 + b, :], cvt[:, b, :]
                    w = [pcur[:, CW + 2 * k + b:CW + 2 * k + b + 1] for k in range(3)]
                    link(dve.tensor_scalar(o, y, w[2], pcur[:, CB + b:CB + b + 1], ALU.mult, ALU.add))
                    link(dve.scalar_tensor_tensor(o[:, 1:S], y[:, 0:S - 1], w[1], o[:, 1:S], ALU.mult, ALU.add))
                    link(dve.scalar_tensor_tensor(o[:, 2:S], y[:, 0:S - 2], w[0], o[:, 2:S], ALU.mult, ALU.add))
                for b, g in enumerate(GROUPS[11]):
                    src = acc_full(dve, l, g)
                    dve.tensor_tensor(U[:, 2 + b, :], cvt[:, b, :], src[:, :], ALU.mult).then_inc(emptied[g % 4], 1)
                    acc_emptied(dve, l, g)

            def a_max(l, tt, h):
                src = wait_full(dve, l, ("L", tt, h))
                n = (tt + 1) * P
                if h >= 2:
                    wait_full(dve, l, ("T", tt, h - 2))
                elif tt > 0:
                    wait_full(dve, l, ("T", tt - 1, h + 2))
                link(dve.memset(small[:, 24 + h:25 + h], 0.0))
                mask = keep[:, KOFF[tt]:KOFF[tt] + n] if tt else tri_add
                dve.tensor_tensor_reduce(probs[:, h % 2, 0:n], src[:, 0:n], mask, -1.0, 3.0e38, ALU.add, ALU.min,
                                         small[:, 24 + h:25 + h]).then_inc(emptied[4 + h % 2], 1)

            def a_norm(l, tt, h):
                n = (tt + 1) * P
                dve.wait_ge(pexp, l * 16 + (4 * tt + h + 1))
                link(dve.reciprocal(small[:, 32 + h:33 + h], small[:, 28 + h:29 + h]))
                dve.tensor_scalar(probs[:, h % 2, 0:n], probs[:, h % 2, 0:n], small[:, 32 + h:33 + h], None,
                                  ALU.mult).then_inc(pn_ready, 1)

            def gate(l, c, b):
                n, g = int(CH[c][1][1]), GROUPS[c][b]
                dve.wait_ge(th_ready, l * 8 + (2 * (c - 12) + b + 1))
                dve.scalar_tensor_tensor(cvt[:, b, :], cvt[:, b, :], 1.0, banks[g % 4][:, :], ALU.add, ALU.mult)\
                   .then_inc(emptied[g % 4], 1)
                acc_emptied(dve, l, g)
                o = U[:, 2 * n + b, :]
                dve.scalar_tensor_tensor(o, o, 0.5, cvt[:, b, :], ALU.mult, ALU.mult).then_inc(o_f32, 1)

            with dve.Fori(0, DEPTH) as l:
                steps[0] = 0
                dve.sem_clear(dve_step)
                dve.wait_ge(x_ready, l * 8 + 8)
                link(dve.tensor_copy(pcur[:, :], pall[:, ds(l * NPAR, NPAR)]))
                link(dve.tensor_scalar(pcur[:, G_POST:CW], pcur[:, G_POST:CW], 0.5, None, ALU.mult))
                inverse_mean(l, "ssx", 1.0 / D)
                dve.wait_ge(rstd_ready, l * 3 + 1)
                for k in range(KT):
                    dve.scalar_tensor_tensor(U[:, k, :], xT[:, k, :], pcur[:, G_PRE + k:G_PRE + k + 1], rstd[:, :],
                                             ALU.mult, ALU.mult).then_inc(h_ready, 1)
                for i in range(2):
                    rope(l, f"rotq{i}", i, aq[:, i, :], raw[:, i, :], cos64, sin64)
                for i in range(2):
                    rope(l, f"rotk{i}", 2 + i, ak[:, i, :], raw[:, 2 + i, :], cos64, sin64)
                for i in range(2):
                    rope(l, f"roti{i}", 4 + i, iqk[:, i, :], raw[:, 4 + i, :], cos32, sin32)
                wait_emptied(dve, l, "iw")
                for tt in (3, 2, 1):
                    index_scores(l, tt)
                top_keys(3)
                top_keys(2, range(0, 8))
                c_softplus(l, 0)
                top_keys(2, range(8, 10))
                c_weights(l, 0)
                layer_norm(l)
                top_keys(1, range(0, 4))
                c_softplus(l, 1)
                layer_norm_apply(l)
                c_weights(l, 1)
                top_keys(1, range(4, 8))
                d_weights(l)
                d_output(l)
                c_softplus(l, 2)
                top_keys(2, range(10, 12))
                c_weights(l, 2)
                top_keys(1, range(8, 12))
                b_gate_x(l)
                c_softplus(l, 3)
                top_keys(2, range(12, 14))
                c_weights(l, 3)
                top_keys(1, range(12, 16))
                top_keys(2, range(14, 16))
                b_conv(l)
                for c in range(12, 16):
                    tt = c - 12
                    a_max(l, tt, 0)
                    a_max(l, tt, 1)
                    a_norm(l, tt, 0)
                    a_max(l, tt, 2)
                    a_norm(l, tt, 1)
                    a_max(l, tt, 3)
                    a_norm(l, tt, 2)
                    if c == 15:
                        a_norm(l, tt, 3)
                        wait_emptied(dve, l, ("AO", tt))
                        gate(l, c, 0)
                    elif c == 14:
                        gate(l, c, 0)
                        a_norm(l, tt, 3)
                    else:
                        gate(l, c, 0)
                        a_norm(l, tt, 3)
                    gate(l, c, 1)
                for d in range(KT):
                    c = 16 + 3 * d
                    if d == 3:
                        for i in range(2):
                            dve.wait_ge(pt_rounded, l * 2 + (i + 1))
                            dve.tensor_tensor(pT_lo[:, i, :], ptok[:, i, :], pT_hi[:, i, :], ALU.subtract).then_inc(pt_split, 1)
                    for n, g in enumerate(GROUPS[c + 2]):
                        acc_emptied(dve, l, GROUPS[c + n // 2][n % 2])
                        src = acc_full(dve, l, g)
                        dst = U[:, d, :] if n == 0 else mtmp[:, 0, :]
                        dve.scalar_tensor_tensor(dst, th[:, n, :], 1.0, src[:, :], ALU.add, ALU.mult)\
                           .then_inc(emptied[g % 4], 1)
                        acc_emptied(dve, l, g)
                        if n > 0:
                            ins = dve.tensor_tensor(U[:, d, :], U[:, d, :], mtmp[:, 0, :], ALU.add)
                            if n < 3:
                                link(ins)
                            else:
                                ins.then_inc(merged, 1)
                inverse_mean(l, "ssy", 0.25 / D)
                dve.wait_ge(rstd_ready, l * 3 + 3)
                for k in range(KT):
                    link(dve.scalar_tensor_tensor(U[:, k, :], U[:, k, :], pcur[:, G_POST + k:G_POST + k + 1],
                                                  rstd[:, :], ALU.mult, ALU.mult))
                    dve.tensor_tensor(xT[:, k, :], xT[:, k, :], U[:, k, :], ALU.add).then_inc(h_ready, 1)
                for e in range(4):
                    for b in range(2):
                        k = 2 * e + b
                        if e == 0 and b == 0:
                            for g in GROUPS[45]:
                                acc_emptied(dve, l, g)
                        acc_emptied(dve, l, GROUPS[46 + e][b])
                        link(dve.scalar_tensor_tensor(U[:, k, :], th[:, b, :], 1.0, embedded[:, k, :], ALU.add, ALU.mult))
                        dve.wait_ge(h_split, l * 24 + 24)
                        dve.scalar_tensor_tensor(xT[:, k, :], U[:, k, :], 0.5, xT[:, k, :], ALU.mult, ALU.add)\
                           .then_inc(x_ready, 1)
            second_vector(dve)

        @block.gpsimd
        def _(pool):
            def split_weights(l, c):
                pool.wait_ge(w_rounded, chunk_count(l, c))
                n = columns(now[0].chunks[c])
                pool.tensor_tensor(w_lo[:, c % 2, 0:n], w_raw[:, c % 2, 0:n], w_hi[:, c % 2, 0:n],
                                   ALU.subtract).then_inc(w_split, 1)

            def split_tiles(l, first, src):
                for k in range(KT):
                    pool.wait_ge(h_rounded, l * 24 + (first + k + 1))
                    pool.tensor_tensor(h_lo[:, k, :], src[:, k, :], h_hi[:, k, :], ALU.subtract).then_inc(h_split, 1)

            def split_branch(l, c):
                n = int(CH[c][1][1])
                for b in range(2):
                    i = 2 * n + b
                    pool.wait_ge(o_rounded, l * 8 + (2 * (c - 12) + b + 1))
                    pool.tensor_tensor(o_lo[:, i, :], U[:, i, :], o_hi[:, i, :], ALU.subtract).then_inc(o_split, 1)

            pool.sem_inc(w_split, 2)
            pool.wait_ge(setup_dve, 3)
            pool.dma_start(bias_s, biasv[:, :]).then_inc(bias_stored, 16)
            pool.wait_ge(bias_stored, 16)
            pool.dma_start(skew_s, bias_s.unsqueeze(1).broadcast_to((16, P, 640))).then_inc(skewed, 16)
            split_weights(0, 0)
            split_weights(0, 1)
            with pool.Fori(0, DEPTH) as l:
                split_tiles(l, 0, U)
                for c in range(2, 41):
                    split_weights(l, c)
                    if 15 <= c <= 17:
                        split_branch(l, c - 3)
                    if c == 17:
                        split_branch(l, 15)
                split_tiles(l, 8, U)
                for c in range(41, 47):
                    split_weights(l, c)
                split_tiles(l, 16, xT)
                for c in range(47, NCH):
                    split_weights(l, c)
                split_weights(l + 1, 0)
                split_weights(l + 1, 1)
            second_pool(pool, split_weights)


def program_inputs(x, p, positions, g_pre, w_in, conv_w, conv_b, ln_g, ln_b, w_spatial, b_spatial, b_merge, w_branch,
                   w_out, g_post, w_ple, w_ple_gate, norm_in_g_2, w_in_2, gate_b_2, conv_w_2, conv_b_2, wq_m_2, wk_m_2,
                   wv_m_2, w_if_2, b_if_2, head_norm_g_2, skip_m_2, w_pa_2, w_pb_2, w_out_2, rel_bias_2, norm_out_g_2):
    import numpy as np
    C = WIDTH

    def tiles(w, cols, kt=8):
        return np.ascontiguousarray(w[:, cols].reshape(kt, P, -1).transpose(1, 0, 2)).reshape(P, -1)

    def columns_of(*vectors):
        return np.concatenate([np.asarray(v).reshape(-1, P) for v in vectors]).T

    depth = w_in.shape[0]
    off = {"aq": 0, "ak": C, "av": 2 * C}
    iq = 3 * C
    ik, iw = iq + 128, iq + 160
    off.update({n: iq + 164 + j * C for j, n in enumerate(("bb", "bc", "bx", "cq", "ck", "cv", "du", "dv", "g0", "g1", "g2", "g3"))})
    merge = off["g3"] + C
    D, IN2 = 1024, {"q": 0, "k": 1024, "v": 2048, "z": 3072, "xm": 4096, "zm": 6144, "om": 8192, "ga": 10240, "gm": 11264}

    def block(kind, i, l):
        r = np.arange
        if kind == "proj":
            if i == "idx":
                return tiles(w_in[l], np.concatenate([r(iq, iq + 128)] + [r(ik, ik + 32)] * 4 + [r(iw, iw + 4)]))
            return tiles(w_in[l], r(off[i], off[i] + C))
        if kind == "logits":
            d, half = i
            return tiles(w_in[l], np.concatenate([r(merge + n * D + d * P, merge + n * D + (d + 1) * P) for n in (2 * half, 2 * half + 1)]))
        if kind == "branch":
            return tiles(w_branch[l].reshape(-1, D), r(i * P, (i + 1) * P))
        if kind in ("out", "pgate", "pa", "fo"):
            w = {"out": w_out, "pgate": w_ple_gate, "pa": w_pa_2, "fo": w_out_2}[kind][l]
            return tiles(w, r(i * C, (i + 1) * C))
        if kind == "ple":
            return tiles(w_ple[l], r(i * 512, (i + 1) * 512), 2)
        if kind == "pb":
            h, half = i // 2, i % 2
            return tiles(w_pb_2[0][h * 512:(h + 1) * 512], r(half * 512, (half + 1) * 512), 4)
        return tiles(w_in_2[0], r(IN2[kind] + i * C, IN2[kind] + (i + 1) * C))

    chunks = [(k, i, l) for l in range(depth) for k, i in layer_chunks()]
    rest = attention_chunks() + [("xm", j) for j in range(8)] + [c for h in range(4) for c in head_chunks(h)] + tail_chunks()
    chunks += [(k, i, 0) for k, i in rest]
    stream = np.zeros((len(chunks), P, CHUNK), np.float32)
    for n, (k, i, l) in enumerate(chunks):
        b = block(k, i, l)
        stream[n, :, :b.shape[1]] = b

    def diagonal_blocks(w):
        return w.reshape(16, P, 4).transpose(1, 0, 2)

    t = lambda w: np.ascontiguousarray(w.transpose(0, 2, 1))
    wqkv = np.stack([np.stack([diagonal_blocks(f(w[0])) for w in (wq_m_2, wk_m_2, wv_m_2)], 1) for f in (lambda w: w, t)], 1)
    arrays = {
        "stream": stream,
        "xT": x[0].T.reshape(8, P, -1).transpose(1, 0, 2),
        "pT": p[:, 0].transpose(2, 0, 1).reshape(2, P, depth, -1).transpose(1, 2, 0, 3),
        "positions": positions,
        "par1": np.stack([columns_of(g_pre[l], g_post[l], b_merge[l], conv_w[l], conv_b[l]) for l in range(depth)], 1),
        "ln_g": ln_g, "ln_b": ln_b, "b_spatial": b_spatial,
        "wsT": w_spatial.transpose(3, 0, 1, 2),
        "par2": columns_of(norm_in_g_2[0], norm_out_g_2, head_norm_g_2[0], skip_m_2[0], gate_b_2[0], conv_b_2[0], conv_w_2[0]),
        "wqkv": wqkv,
        "w_if": w_if_2[0].reshape(48, P, 8).transpose(1, 0, 2),
        "b_if": b_if_2[0].reshape(8, 1),
        "rel_bias": rel_bias_2,
    }
    arrays.update(host_constants())
    return {k: np.ascontiguousarray(v) for k, v in arrays.items()}


def host_constants():
    import math
    import numpy as np
    dist = 511 - np.arange(640)
    large = 16 + (np.log(np.maximum(dist, 16).astype(np.float32) / np.float32(16)) / np.float32(math.log(2048 / 16))
                  * np.float32(16)).astype(np.int32)
    bucket = np.where(dist < 16, dist, np.minimum(large, 31))
    times = (dist <= 128).astype(int) + (dist % 4 == 0) + (dist % 16 == 0)
    times[dist < 0] = 0
    onehot = ((np.arange(32)[:, None] == bucket[None, :]) & (dist >= 0)).astype(np.float32)
    lnmult = np.where(times > 0, np.log(np.maximum(times, 1).astype(np.float32)), np.float32(-1e30)).astype(np.float32)
    lnmult = np.ascontiguousarray(np.broadcast_to(lnmult, (16, 640)))
    i = np.arange(P)
    part, col = i[:, None], i[None, :]
    rot = []
    for half in (32, 16):
        m = np.zeros((P, P), np.float32)
        for j in range(P):
            if j % (2 * half) < half:
                m[j + half, j] = -1.0
            else:
                m[j - half, j] = 1.0
        rot.append(m)
    f = np.float32
    mats = [np.eye(P, dtype=f), np.ones((P, P), f), (part <= col).astype(f), np.where(part <= col, f(0), f(-1e30)),
            rot[0], rot[1], np.where(col > part, f(-3.0e38), f(0)), np.where(col > part, f(-1e30), f(0)),
            (part < col).astype(f), np.where(part < col, f(0), f(-1e30)),
            -(part >= col).astype(f), -np.ones((P, P), f)]
    consts = np.ascontiguousarray(np.stack(mats, 1).astype(f))
    freq = np.stack([f(10000.0) ** (-(np.arange(0, d, 2, dtype=f) / f(d)))[i % (d // 2)] for d in (64, 32)], 1).astype(f)
    mask4 = (part // 4 == np.arange(32)[None, :]).astype(f)
    return {"consts": consts, "freq": freq, "mask4": mask4, "onehot": onehot, "lnmult": lnmult}


def kernel(**inputs):
    import numpy as np
    import concourse.bacc as bacc
    from concourse import mybir
    from concourse.bass_utils import run_bass_kernel_spmd

    nc = bacc.Bacc("TRN2", target_bir_lowering=False, num_devices=1)
    arrays = {f"in_{k}_dram": v for k, v in program_inputs(**{k: np.asarray(v) for k, v in inputs.items()}).items()}
    a = {n[3:-5]: nc.dram_tensor(n, v.shape, mybir.dt.from_np(v.dtype), kind="ExternalInput").ap() for n, v in arrays.items()}
    kt, tokens = a["xT"].shape[1:]
    a["out"] = nc.dram_tensor("out_0_dram", (P, kt, tokens), mybir.dt.float32, kind="ExternalOutput").ap()
    build_program(nc, a)
    out = run_bass_kernel_spmd(nc, [arrays], core_ids=[0]).results[0]["out_0_dram"]
    return out.transpose(2, 1, 0).reshape(1, tokens, kt * P)
```

```python
P = 128
WIDTH = 256
CHUNK = 8 * 260
PROJECTIONS = ["aq", "ak", "idx", "av", "cq", "ck", "cv", "dv", "du", "bc", "bx", "bb", "g1", "g3", "g2", "g0"]


def layer_chunks():
    ch = [("proj", n) for n in PROJECTIONS]
    for d in range(8):
        ch += [("logits", (d, 0)), ("logits", (d, 1)), ("branch", d)]
    ch += [("out", e) for e in range(4)]
    ch += [("ple", 0), ("ple", 1)]
    return ch + [("pgate", e) for e in range(4)]


def attention_chunks():
    ch = [("q", 0), ("k", 0), ("v", 0)]
    for i in range(3):
        ch += [("q", i + 1), ("k", i + 1), ("v", i + 1), ("z", i)]
    ch += [("ga", 0), ("ga", 1), ("ga", 2), ("z", 3), ("ga", 3)]
    return ch + [("pa", d) for d in range(4)]


def head_chunks(h):
    return [("om", 2 * h), ("om", 2 * h + 1), ("zm", 2 * h), ("zm", 2 * h + 1), ("pb", 2 * h), ("pb", 2 * h + 1)]


def tail_chunks():
    return [("gm", d) for d in range(4)] + [("fo", d) for d in range(4)]


def columns(chunk):
    kind, i = chunk
    return {"branch": 8 * P, "ple": 8 * P}.get(kind, CHUNK if i == "idx" else 8 * WIDTH)


def build_program(nc, a):
    from contextlib import ExitStack

    import concourse.bass as bass
    from concourse import mybir

    ALU = mybir.AluOpType
    ACT = mybir.ActivationFunctionType
    F32 = mybir.dt.float32
    F32R = mybir.dt.float32r
    I32 = mybir.dt.int32
    ds = bass.ds

    DEPTH = a["par1"].shape[1] - 1
    D = a["xT"].shape[1] * P
    S = a["xT"].shape[2]
    KT = D // P
    TT = S // P
    W = 256
    EPS = 1e-6
    NEG_SCORE = -3.0e38
    MARK = -3.3e38
    NEG = -1.0e30

    TOKEN_MAJOR = ("av", "cv", "dv")
    CH = layer_chunks()
    CH_B, CH_C, CH_D, CH_E = attention_chunks(), [("xm", 0), ("xm", 1)], head_chunks(0), tail_chunks()
    NCH = len(CH)
    assert NCH % 2 == 0

    order = [("ssx", 4), ("rsx", 5)]
    order += [("rotq0", 4), ("rotq1", 5), ("rotk0", 6), ("rotk1", 7), ("roti0", 4), ("roti1", 5)]
    order += [("iw", 6), ("iwT", 7)]
    order += [(("idx", tt, h), 4 + h) for tt in (3, 2, 1) for h in range(4)]
    for h in range(4):
        order += [(("Z", h, j), 4 + j) for j in range(3)]
        order += [(("CO", h - 1), 7)] if h else []
        order += [(("dmix", 0), 7), (("dmix", 1), 7)] if h == 3 else []
        order += [(("Sx", h, j), 4 + j) for j in range(3)]
    order += [(("CO", 3), 7)]
    for tt in range(4):
        order += [(("L", tt, 0), 4), (("L", tt, 1), 5), (("T", tt, 0), 6), (("L", tt, 2), 4),
                  (("T", tt, 1), 6), (("L", tt, 3), 5), (("T", tt, 2), 6), (("T", tt, 3), 6),
                  (("AO", tt), 7)]
    order += [("ssy", 6), ("rsy", 7)]
    order_b = [("ssx", 4), ("rsx", 5)]
    for i in range(4):
        for m in range(4):
            order_b += [(("L", m, 0, i), 4), (("L", m, 1, i), 5), (("T", m, 0, i), 6), (("L", m, 2, i), 4),
                        (("T", m, 1, i), 6), (("L", m, 3, i), 5), (("T", m, 2, i), 6), (("T", m, 3, i), 6),
                        (("AO", m, i), 7)]
    order_c = []
    for t in range(4):
        order_c += [(("fold", t), 4), (("qm", t), 4), (("km", t), 5), (("vm", t), 6)]
    order_g = [("gates", 7), ("f", 4), ("cols", 5)]
    order_d = [("M", 7)] + [(("sc", j), 4 + j) for j in range(3)] + [("den", 7)]
    order_d += [(("num", tt), 4 + tt % 2) for tt in range(4)] + [(("hT", tt), 6 + tt % 2) for tt in range(4)]
    order_e = [("ssf", 4), ("rsf", 5)]

    class Phase:
        before = None

        def __init__(self, chunks, side, rounds=1):
            p = Phase.before
            self.chunks, self.rounds, self.n = chunks, rounds, len(chunks)
            self.c0 = p.c0 + p.rounds * p.n if p else 0
            self.g0 = p.g0 + p.rounds * p.ng if p else 0
            self.groups, g = [], 0
            for kind, i in chunks:
                k = 4 if kind in ("branch", "ple", "pb") else 2
                self.groups.append(list(range(g, g + k)))
                g += k
            self.ng = g
            self.before_first = p.last_groups if p else (0, 0)
            self.last_groups = self.groups[-1] if chunks else p.last_groups
            assert g % 4 == 0 and len(chunks) % 2 == 0 and self.c0 % 2 == 0, (g, len(chunks))
            self.b0 = {b: p.b0[b] + p.rounds * p.nb[b] if p else 1 for b in range(4, 8)}
            self.side, self.nb = {}, {b: 0 for b in range(4, 8)}
            for key, b in side:
                self.side[key] = (b, self.nb[b])
                self.nb[b] += 1
            Phase.before = self

    LAYERS = Phase(CH, order, DEPTH)
    ATTN = Phase(CH_B, order_b)
    MPROJ = Phase(CH_C, order_c, 4)
    MGATE = Phase([], order_g)
    MHEAD = Phase(CH_D, order_d, 4)
    TAIL = Phase(CH_E, order_e)
    now = [LAYERS]
    GROUPS, NCH = LAYERS.groups, LAYERS.n

    ctx = ExitStack()
    with ctx:
        top = [(nc.sbuf_base + 31) // 32 * 32]

        def place(name, shape, dt=F32, at=None):
            size = 4
            for n in shape[1:]:
                size *= n
            if at is None:
                at = top[0]
                top[0] += (size + 31) // 32 * 32
            t = nc.alloc_sbuf_tensor_at(name, shape, dt, offset=at)
            addr[name] = at
            return t

        addr = {}
        xT = place("xT", [P, KT, S])
        h_hi = place("h_hi", [P, KT, S], F32R)
        h_lo = place("h_lo", [P, KT, S], F32R)
        w_raw = place("w_raw", [P, 2, CHUNK])
        w_hi = place("w_hi", [P, 2, CHUNK], F32R)
        w_lo = place("w_lo", [P, 2, CHUNK], F32R)
        par2 = place("par2", [P, 144])
        bif = place("bif", [8, 1])
        mask4 = place("mask4", [P, 32])
        consts = place("consts", [P, 12, P])
        (ident, ones, trilT, trilT_add, rot64, rot32, tri_neg, tri_add, trisT, trisT_add, upinc_neg,
         ones_neg) = (consts[:, i, :] for i in range(12))
        R2 = addr["consts"] + 4 * P * 4
        cos64 = place("cos64", [P, S])
        sin64 = place("sin64", [P, S])
        cos32 = place("cos32", [P, S])
        sin32 = place("sin32", [P, S])
        NPAR = 56
        pall = place("pall", [P, (DEPTH + 1) * NPAR])
        pcur = place("pcur", [P, NPAR])
        lngb = place("lngb", [P, DEPTH, 2, W])
        bsp = place("bsp", [P, DEPTH, 2, P])
        U = place("U", [P, KT, S])
        aq = place("aq", [P, 2, S])
        ak = place("ak", [P, 2, S])
        av = place("av", [P, TT, W])
        cq = place("cq", [P, 2, S])
        ck = place("ck", [P, 2, S])
        cv = place("cv", [P, TT, W])
        keep = place("keep", [P, 9 * P])
        diag = place("diag", [P, S])
        small = place("small", [P, 64])
        stats = place("stats", [P, TT, 8])
        sp = place("sp", [P, 10 * P])
        wt = place("wt", [P, 10 * P])
        o_hi = place("o_hi", [P, KT, S], F32R)
        o_lo = place("o_lo", [P, KT, S], F32R)
        assert top[0] <= nc.sbuf_usable_end, (top[0], nc.sbuf_usable_end)
        eb = addr["o_hi"]
        raw = place("raw", [P, 6, S], at=eb)
        rt = place("rt", [P, 2, S], at=eb + 12288)
        relu = place("relu", [P, 4, S], at=eb + 16384)
        iqk = place("iqk", [P, 2, S], at=eb + 24576)
        dvt = place("dvt", [P, TT, W], at=eb + 28672)
        az = place("az", [P, 10 * P], at=eb)
        ws = place("ws", [P, 4, P], at=eb + 8192)
        cvt = place("cvt", [P, 2, S], at=eb + 16384)
        probs = place("probs", [P, 2, S], at=addr["sp"])
        probT = place("probT", [P, 2, S], at=addr["sp"] + 4096)
        th = place("th", [P, 4, S], at=addr["sp"])
        mtmp = place("mtmp", [P, 1, S], at=addr["sp"] + 8192)
        ptok = place("ptok", [P, 2, S], at=addr["aq"])
        pT_hi = place("pT_hi", [P, 2, S], F32R, at=addr["cq"])
        pT_lo = place("pT_lo", [P, 2, S], F32R, at=addr["ck"])
        sq = place("sq", [P, KT, S], at=eb)
        embedded = place("embedded", [P, KT, S], at=eb + 16384)
        posb = place("posb", [P, S], I32, at=addr["wt"])
        ang = place("ang", [P, 4, S], at=eb + 24576)
        onehot = place("onehot", [32, 640], at=eb + 12288)
        rel = place("rel", [32, 16], at=eb + 14848)
        lnmult = place("lnmult", [16, 640], at=eb + 15360)
        biasv = place("biasv", [16, 640], at=eb + 18432)
        freq = place("freq", [P, 4], at=addr["small"])

        turns = place("turns", [P, S], at=addr["sp"])

        KB = 1024
        y_hi = place("y_hi", [P, KT, S], F32R, at=R2)
        y_lo = place("y_lo", [P, KT, S], F32R, at=R2 + 16 * KB)
        qkv = place("qkv", [P, 2, 3, 2 * S], at=R2 + 32 * KB)
        ybuf = place("ybuf", [P, 2, S], at=R2 + 56 * KB)
        zt = place("zt", [P, 2, S], at=R2 + 60 * KB)
        mst = place("mst", [P, 2, S], at=R2 + 64 * KB)
        probs2 = place("probs2", [P, 2, S], at=R2 + 68 * KB)
        probT2 = place("probT2", [P, 2, S], at=R2 + 72 * KB)
        small2 = place("small2", [P, 64], at=R2 + 76 * KB)
        assert R2 + 76 * KB + 256 <= nc.sbuf_usable_end
        xm = place("xm", [P, 2, 2, S], at=R2)
        xc = place("xc", [P, 2, 2, S], at=R2 + 8 * KB)
        q2 = place("q2", [P, 2, 2, S], at=R2 + 16 * KB)
        k2 = place("k2", [P, 2, 2, S], at=R2 + 24 * KB)
        cth = place("cth", [P, 2, S], at=R2 + 48 * KB)
        v2 = place("v2", [P, 2, TT, W], at=R2 + 56 * KB)
        wraw = place("wraw", [P, 2, 3, 16, 4], at=R2 + 64 * KB)
        wif = place("wif", [P, 48, 8], at=R2 + 64 * KB + 1536)
        bd = place("bd", [P, 4, 3, P], at=R2 + 64 * KB + 3072)
        bdT = place("bdT", [P, 2, 3, P], at=R2 + 64 * KB + 9216)
        gt = place("gt", [8, 4, S], at=R2 + 48 * KB)
        yacc = place("yacc", [P, KT, S], at=R2)
        qh = place("qh", [P, 4, S], at=R2 + 16 * KB)
        kh = place("kh", [P, 4, S], at=R2 + 24 * KB)
        vh = place("vh", [P, TT, S], at=R2 + 32 * KB)
        xch = place("xch", [P, 4, S], at=R2 + 40 * KB)
        pm = place("pm", [P, 10 * P], at=R2 + 48 * KB)
        yh_hi = place("yh_hi", [P, 4, S], F32R, at=R2 + 56 * KB)
        yh_lo = place("yh_lo", [P, 4, S], F32R, at=R2 + 64 * KB)
        hstats = place("hstats", [P, TT, 8], at=R2 + 72 * KB)
        negM = place("negM", [4, S], at=R2 + 73 * KB)
        negM_h = place("negM_h", [4, S], at=R2 + 53 * KB)
        mrg = place("mrg", [P, KT, S], at=R2 + 16 * KB)
        sqf = place("sqf", [P, KT, S], at=R2 + 32 * KB)
        th2 = place("th2", [P, 4, S], at=R2 + 48 * KB)
        m_hi = place("m_hi", [P, KT, S], F32R, at=R2 + 76 * KB + 256)
        m_lo = place("m_lo", [P, KT, S], F32R, at=R2 + 92 * KB + 256)
        assert R2 + 108 * KB + 256 <= nc.sbuf_usable_end
        diag3 = place("diag3", [P, S], at=R2 + 56 * KB)
        bias_s = nc.dram_tensor("bias_s", [16, 640], F32, kind="Internal").ap()
        skew_s = nc.dram_tensor("skew_s", [16, P, 640], F32, kind="Internal").ap()
        m_s = nc.dram_tensor("m_s", [P, KT, S], F32, kind="Internal").ap()
        q_s, k_s, xc_s = (nc.dram_tensor(n, [P, 16, S], F32, kind="Internal").ap() for n in ("q_s", "k_s", "xc_s"))
        v_s = nc.dram_tensor("v_s", [P, TT, 4 * S], F32, kind="Internal").ap()

        first_loads = [(posb[:, :], a["positions"][0:1, :].broadcast_to((P, S))), (freq[:, 0:2], a["freq"]),
                       (onehot[:, :], a["onehot"]), (rel[:, :], a["rel_bias"]), (lnmult[:, :], a["lnmult"])]
        const_loads = [(consts[:, 0:2, :], a["consts"][:, 0:2, :]), (pall[:, :], a["par1"].rearrange("p l n -> p (l n)")),
                       (consts[:, 2:12, :], a["consts"][:, 2:12, :]), (par2[:, :], a["par2"]),
                       (bif[:, :], a["b_if"]), (mask4[:, :], a["mask4"]),
                       (lngb[:, :, :, :].rearrange("p l i w -> p (l i w)"), a["ln_gb"].broadcast_to((P, DEPTH * 2 * W)))]
        for i in range(2):
            const_loads.append((bsp[64 * i:64 * i + 64, :, :, :].rearrange("p l i w -> p (l i w)"),
                                a["b_spatial"][i:i + 1, :].broadcast_to((64, DEPTH * 2 * P))))
        NCONST = len(const_loads)
        SETUP_BIAS, SETUP_ANGLES = 8, 25
        N_OUT0, HEAD_G, SKIP, GATE_B, CONV_B, CONV_W = 8, 16, 32, 48, 64, 80

        banks = [ctx.enter_context(nc.psum_tensor(f"bank{b}", [P, 512], F32)) for b in range(8)]

        def sem(name):
            return ctx.enter_context(nc.semaphore(name))

        w_landed = [sem(f"w_landed{i}") for i in range(2)]
        w_rounded = sem("w_rounded")
        w_split = sem("w_split")
        full = [sem(f"full{b}") for b in range(8)]
        emptied = [sem(f"emptied{b}") for b in range(8)]
        first_in, const_in = sem("first_in"), sem("const_in")
        bias_product, bias_stored, skewed = sem("bias_product"), sem("bias_stored"), sem("skewed")
        mst_in = [sem("mst_in0"), sem("mst_in1")]
        bd_in = sem("bd_in")
        pexp2, pn2 = sem("pexp2"), sem("pn2")
        z_tanh = sem("z_tanh")
        yb_ready, yb_rounded, yb_split = sem("yb_ready"), sem("yb_rounded"), sem("yb_split")
        m_ready = sem("m_ready")
        bd_ready = sem("bd_ready")
        conv_ready, conv_tanh, xc_ready = sem("conv_ready"), sem("conv_tanh"), sem("xc_ready")
        stored = [sem("stored0"), sem("stored1")]
        zero_ready = sem("zero_ready")
        g_abs, g_ln = sem("g_abs"), sem("g_ln")
        g_neg, g_em = sem("g_neg"), sem("g_em")
        yacc_zero = sem("yacc_zero")
        mh_ready = sem("mh_ready")
        qk_in, vx_in = sem("qk_in"), sem("vx_in")
        e_ready, e_exp = sem("e_ready"), sem("e_exp")
        skipped = sem("skipped")
        hn_var, hn_rstd, hn_ready = sem("hn_var"), sem("hn_rstd"), sem("hn_ready")
        zm_tanh = sem("zm_tanh")
        yh_ready, yh_rounded, yh_split = sem("yh_ready"), sem("yh_rounded"), sem("yh_split")
        mrg_in = sem("mrg_in")
        fm_ready = sem("fm_ready")
        out_ready = sem("out_ready")
        x_in = [sem("x_in0"), sem("x_in1")]
        rope_cos = sem("rope_cos")
        setup_dve = sem("setup_dve")
        setup_act = sem("setup_act")
        x_ready = sem("x_ready")
        sq_ready = sem("sq_ready")
        sum_ready = sem("sum_ready")
        diag_ready = sem("diag_ready")
        var_ready = sem("var_ready")
        rstd_ready = sem("rstd_ready")
        h_ready = sem("h_ready")
        h_rounded = sem("h_rounded")
        h_split = sem("h_split")
        rot_ready = sem("rot_ready")
        relu_used = sem("relu_used")
        ws_in = sem("ws_in")
        p_in = sem("p_in")
        vn_ready = sem("vn_ready")
        z_ln = sem("z_ln")
        sp_ready = sem("sp_ready")
        cw_ready = sem("cw_ready")
        cw_exp = sem("cw_exp")
        pexp = sem("pexp")
        pn_ready = sem("pn_ready")
        th_ready = sem("th_ready")
        o_f32 = sem("o_f32")
        o_rounded = sem("o_rounded")
        o_split = sem("o_split")
        merged = sem("merged")
        pt_rounded = sem("pt_rounded")
        pt_split = sem("pt_split")
        ws_ready = sem("ws_ready")
        dve_step = sem("dve_step")
        act_step = sem("act_step")
        y_out = sem("y_out")

        block = ctx.enter_context(nc.Block())

        SUM_AT = 6
        WOFF = [0, 4 * P, 7 * P, 9 * P]
        KOFF = {3: 0, 2: 4 * P, 1: 7 * P}
        G_PRE, G_POST, BM, CW, CB = 0, 8, 16, 48, 54

        def wait_full(eng, l, key, back=0):
            b, n = now[0].side[key]
            eng.wait_ge(full[b], l * now[0].nb[b] + (now[0].b0[b] + n + 1 - back * now[0].nb[b]))
            return banks[b]

        def wait_empty(eng, l, key):
            b, n = now[0].side[key]
            eng.wait_ge(emptied[b], l * now[0].nb[b] + (now[0].b0[b] + n))
            return banks[b]

        def wait_emptied(eng, l, key):
            b, n = now[0].side[key]
            eng.wait_ge(emptied[b], l * now[0].nb[b] + (now[0].b0[b] + n + 1))

        def acc_count(l, g, n):
            return l * (now[0].ng // 4) + ((now[0].g0 + g) // 4 + n + 1)

        def acc_full(eng, l, g):
            eng.wait_ge(full[g % 4], acc_count(l, g, 1))
            return banks[g % 4]

        def acc_empty(eng, l, g):
            eng.wait_ge(emptied[g % 4], acc_count(l, g, 0))
            return banks[g % 4]

        def acc_emptied(eng, l, g):
            eng.wait_ge(emptied[g % 4], acc_count(l, g, 1))

        def halves_count(l, c, half):
            return l * (2 * now[0].n) + (2 * (now[0].c0 + c) + half + 1)

        def split_count(l, c, half=1):
            return l * (2 * now[0].n) + (2 * (now[0].c0 + c) + half + 5)


        def second_loads(sp_, load):
            def bias_of(n):
                src = bass.AP(tensor=skew_s.tensor, offset=n * P * 640 + 127, ap=[[639, P], [1, S]])
                sp_.dma_start(mst[:, n % 2, :], src).then_inc(mst_in[n % 2], 16)

            now[0] = ATTN
            for c in range(ATTN.n):
                load(0, c)
                if c == 1:
                    sp_.wait_ge(h_ready, DEPTH * 16 + 8)
                    sp_.wait_ge(skewed, 16)
                    bias_of(0)
                    bias_of(1)
                n = c - 2
                if 2 <= n < 16:
                    wait_emptied(sp_, 0, ("L", (n - 2) % 4, 3, (n - 2) // 4))
                    bias_of(n)
                if c == 20:
                    now[0] = ATTN
                    wait_full(sp_, 0, ("AO", 3, 3))
                    sp_.dma_start(wraw[:, :, :, :, :], a["wqkv"]).then_inc(bd_in, 16)
                    sp_.dma_start(wif[:, :, :], a["w_if"]).then_inc(bd_in, 16)
            now[0] = MPROJ
            with sp_.Fori(0, MPROJ.rounds) as r:
                load(r, 0)
                load(r, 1)
            now[0] = MHEAD
            with sp_.Fori(0, MHEAD.rounds) as h:
                for c in range(MHEAD.n):
                    load(h, c)
            now[0] = TAIL
            for c in range(TAIL.n):
                load(0, c)
            now[0] = LAYERS

        def second_products(pe, product, weights, act, part, column_sums, spread):
            now[0] = ATTN

            def logits(i, m, tt):
                out = wait_empty(pe, 0, ("L", m, tt, i))
                rows = slice(64 * (m % 2), 64 * (m % 2) + 64)
                o = (m // 2) * S
                pe.matmul(out[:, 0:(tt + 1) * P], qkv[rows, i % 2, 0, o + tt * P:o + (tt + 1) * P],
                          qkv[rows, i % 2, 1, o:o + (tt + 1) * P], start=True, stop=True).then_inc(full[4 + tt % 2], 1)

            def turn(i, m, tt):
                out = wait_empty(pe, 0, ("T", m, tt, i))
                pe.wait_ge(pn2, 16 * i + 4 * m + tt + 1)
                for j in range(tt + 1):
                    last = pe.transpose(out[:, j * P:(j + 1) * P], probs2[:, tt % 2, j * P:(j + 1) * P], ident)
                last.then_inc(full[6], 1)

            def values(i, m, tt):
                if tt == 0:
                    wait_empty(pe, 0, ("AO", m, i))
                wait_emptied(pe, 0, ("T", m, tt, i))
                rows = slice(64 * (m % 2), 64 * (m % 2) + 64)
                for j in range(tt + 1):
                    last = pe.matmul(banks[7][rows, tt * P:(tt + 1) * P], qkv[:, i % 2, 2, j * W + 64 * m:j * W + 64 * m + 64],
                                     probT2[:, tt % 2, j * P:(j + 1) * P], start=j == 0, stop=j == tt)
                if tt == 3:
                    last.then_inc(full[7], 1)

            for c in range(ATTN.n):
                if ATTN.chunks[c] == ("pa", 0):
                    pe.wait_ge(yb_split, 8)
                for s in range(8):
                    part(0, c, s)
                    if 3 <= c < 19:
                        i, m = (c - 3) // 4, (c - 3) % 4
                        if s == 0:
                            if m == 0:
                                for cc in ((1, 2) if i == 0 else (c - 3, c - 2)):
                                    for g in ATTN.groups[cc]:
                                        acc_emptied(pe, 0, g)
                            logits(i, m, 0)
                            logits(i, m, 1)
                        if s == 2:
                            turn(i, m, 0)
                            logits(i, m, 2)
                        if s == 3:
                            turn(i, m, 1)
                            values(i, m, 0)
                            logits(i, m, 3)
                        if s == 4:
                            turn(i, m, 2)
                            values(i, m, 1)
                        if s == 5:
                            turn(i, m, 3)
                            values(i, m, 2)
                        if s == 6:
                            values(i, m, 3)

            def tile_step(r, t, step):
                u, b = t // 2, t % 2
                if step == 0:
                    out = wait_empty(pe, r, ("fold", t))
                    pe.wait_ge(bd_ready, r * 4 + (t + 1))
                    for m in range(3):
                        last = pe.matmul(out[:, 8 * (m // 2):8 * (m // 2) + 8], bdT[:, b, m, :],
                                         wif[:, ds(4 * r + (16 * m + t), 1), :].rearrange("p o c -> p (o c)"),
                                         start=m != 1, stop=m != 0)
                    last.then_inc(full[4], 1)
                if step == 1:
                    pe.wait_ge(xc_ready, r * 4 + (t + 1))
                    for m, key in ((0, "qm"), (1, "km")):
                        out = wait_empty(pe, r, (key, t))
                        pe.matmul(out[:, :], bd[:, t, m, :], xc[:, u, b, :], start=True, stop=True).then_inc(full[4 + m], 1)
                if step == 2:
                    wait_emptied(pe, r, ("fold", t))
                    for n, x in ((0, xc), (8, xm)):
                        pe.matmul(banks[7][0:8, :], small2[:, 16 * b + n:16 * b + n + 8], x[:, u, b, :],
                                  start=False, stop=False, skip_group_check=True)
                if step == 3:
                    out = wait_empty(pe, r, ("vm", t))
                    for tt in range(TT):
                        last = pe.matmul(out[:, tt * P:(tt + 1) * P], xm[:, u, b, tt * P:(tt + 1) * P], bd[:, t, 2, :],
                                         start=True, stop=True)
                    last.then_inc(full[6], 1)

            now[0] = MGATE
            wait_empty(pe, 0, "gates")
            pe.wait_ge(zero_ready, 1)
            pe.matmul(banks[7][0:8, :], small2[:, 32:40], xT[:, 0, :], start=True, stop=False, skip_group_check=True)
            now[0] = MPROJ
            for s in range(8):
                part(0, 0, s)
            with pe.Fori(0, MPROJ.rounds - 1) as r:
                for s in range(8):
                    part(r, 1, s)
                    tile_step(r, s // 4, s % 4)
                for s in range(8):
                    part(r + 1, 0, s)
                    tile_step(r, 2 + s // 4, s % 4)
            r = MPROJ.rounds - 1
            for s in range(8):
                part(r, 1, s)
                tile_step(r, s // 4, s % 4)
            for s in range(8):
                tile_step(r, 2 + s // 4, s % 4)
            now[0] = MGATE
            pe.matmul(banks[7][0:8, :], small2[:, 32:40], xT[:, 0, :], start=False, stop=True,
                      skip_group_check=True).then_inc(full[7], 1)
            AHEAD = 4

            def first_parts(h):
                for s in range(AHEAD):
                    part(h, 0, s)

            wait_emptied(pe, 0, "gates")
            out = wait_empty(pe, 0, "f")
            pe.matmul(out[0:4, :], ident[0:8, 4:8], gt[0:8, 0, :], start=True, stop=True).then_inc(full[4], 1)
            now[0] = MHEAD
            first_parts(0)
            now[0] = MGATE
            out = wait_empty(pe, 0, "cols")
            pe.wait_ge(g_neg, 1)
            for n, t in ((0, 1), (16, 3)):
                for tt in range(TT):
                    last = pe.transpose(out[:, n + 4 * tt:n + 4 * tt + 4], gt[0:4, t, tt * P:(tt + 1) * P], ident[0:4, 0:4])
            last.then_inc(full[5], 1)

            now[0] = MHEAD

            def scores(h, bank):
                out = wait_empty(pe, h, ("sc", bank))
                js = (2, 3) if bank == 2 else (bank,)
                for j in js:
                    o = out[:, WOFF[j] - WOFF[js[0]]:WOFF[j] - WOFF[js[0]] + S - j * P]
                    for e in range(4):
                        last = pe.matmul(o, kh[:, e, j * P:(j + 1) * P], qh[:, e, j * P:S], start=e == 0, stop=e == 3)
                last.then_inc(full[4 + bank], 1)

            def weight_of(j, tt):
                return pm[:, WOFF[j] + (tt - j) * P:WOFF[j] + (tt - j + 1) * P]

            def denominators(h):
                for bank in range(3):
                    wait_emptied(pe, h, ("sc", bank))
                out = wait_empty(pe, h, "den")
                for tt in range(TT):
                    for j in range(tt + 1):
                        last = pe.matmul(out[:, tt:tt + 1], weight_of(j, tt), ones[:, 0:1], start=j == 0, stop=j == tt)
                last.then_inc(full[7], 1)

            def numerators(h, tt):
                if tt == 0:
                    pe.wait_ge(vx_in, h * 32 + 32)
                out = wait_empty(pe, h, ("num", tt))
                for j in range(tt + 1):
                    last = pe.matmul(out[:, :], weight_of(j, tt), vh[:, j, :], start=j == 0, stop=j == tt)
                last.then_inc(full[4 + tt % 2], 1)

            def turn_h(h, tt):
                out = wait_empty(pe, h, ("hT", tt))
                pe.wait_ge(hn_ready, h * 4 + (tt + 1))
                for e in range(4):
                    last = pe.transpose(out[:, e * P:(e + 1) * P], qh[:, tt, e * P:(e + 1) * P], ident)
                last.then_inc(full[6 + tt % 2], 1)

            def head(h):
                for c in range(4):
                    for s in range(AHEAD if c == 0 else 0, 8):
                        part(h, c, s)
                        if c == 0 and s == AHEAD:
                            out = wait_empty(pe, h, "M")
                            pe.wait_ge(mh_ready, h + 1)
                            pe.matmul(out[:, :], ones[0:4, :], negM_h[:, :],
                                      start=True, stop=True).then_inc(full[7], 1)
                        if c == 0 and s > AHEAD:
                            if s == AHEAD + 1:
                                pe.wait_ge(qk_in, h * 32 + 32)
                            scores(h, s - AHEAD - 1)
                        if c == 1 and s == 6:
                            denominators(h)
                        if c == 2 and s in (0, 1, 3, 4):
                            numerators(h, {0: 0, 1: 1, 3: 2, 4: 3}[s])
                        if c == 3 and 2 <= s <= 5:
                            turn_h(h, s - 2)
                for k in range(4):
                    if k % 2 == 0:
                        pe.wait_ge(w_split, split_count(h, 4, k // 2))
                    pe.wait_ge(yh_rounded, h * 4 + (k + 1))
                    for n, g in enumerate(MHEAD.groups[4]):
                        if k == 0:
                            acc_empty(pe, h, g)
                        for i, lhsT in enumerate(weights(4, k * S + n * P, P)):
                            pe.matmul(banks[g % 4][:, :], lhsT, yh_hi[:, k, :], start=k == 0 and i == 0, stop=False)
                for n, g in enumerate(MHEAD.groups[4]):
                    for k in range(4):
                        if n == 0:
                            pe.wait_ge(yh_split, h * 4 + (k + 1))
                        last = pe.matmul(banks[g % 4][:, :], weights(4, k * S + n * P, P)[0], yh_lo[:, k, :],
                                         start=False, stop=k == 3)
                    last.then_inc(full[g % 4], 1)
                pe.wait_ge(w_split, split_count(h, 5))
                for n, g in enumerate(MHEAD.groups[5]):
                    acc_empty(pe, h, g)
                    product(banks[g % 4][:, :], [(weights(5, k * S + n * P, P), (yh_hi[:, k, :], yh_lo[:, k, :]))
                                                 for k in range(4)], True, True).then_inc(full[g % 4], 1)

            with pe.Fori(0, MHEAD.rounds - 1) as h:
                head(h)
                first_parts(h + 1)
            head(MHEAD.rounds - 1)

            now[0] = TAIL
            for c in range(TAIL.n):
                for s in range(8):
                    part(0, c, s)
            column_sums(0, "ssf", sqf[:, KT - 1, :], DEPTH * 2 + 2)
            spread(0, "rsf", diag3, DEPTH * 2 + 2)
            now[0] = LAYERS

        def second_scalar(act, round_weights):
            def evacuate(l, g, dst, func=ACT.Copy, scale=1.0, bias=0.0):
                src = acc_full(act, l, g)
                act.activation(dst, src[:, 0:S], func, scale=scale, bias=bias).then_inc(emptied[g % 4], 1)

            def move(l, key, dst, src, scale=1.0):
                wait_full(act, l, key)
                act.activation(dst, src, ACT.Copy, scale=scale).then_inc(emptied[now[0].side[key][0]], 1)

            now[0] = ATTN
            def exps(i, m, tt):
                wait_emptied(act, 0, ("L", m, tt, i))
                n = (tt + 1) * P
                act.activation(probs2[:, tt % 2, 0:n], probs2[:, tt % 2, 0:n], ACT.Exp, scale=-1.0,
                               bias=small2[:, tt:tt + 1], accum_out=small2[:, 4 + tt:5 + tt]).then_inc(pexp2, 1)

            def turned(i, m, tt):
                n = (tt + 1) * P
                move(0, ("T", m, tt, i), probT2[:, tt % 2, 0:n], banks[6][:, 0:n])

            def project(c, b):
                kind, i = ATTN.chunks[c]
                g = ATTN.groups[c][b]
                if kind in "qkv":
                    evacuate(0, g, qkv[:, i % 2, "qkv".index(kind), b * S:(b + 1) * S], scale=0.125 if kind == "q" else 1.0)
                elif kind == "z":
                    src = acc_full(act, 0, g)
                    if i > 0:
                        act.wait_ge(yb_ready, 2 * (i - 1) + b + 1)
                    act.activation(zt[:, b, :], src[:, :], ACT.Tanh, scale=0.5).then_inc(z_tanh, 1)
                elif kind == "ga":
                    evacuate(0, g, gate_tile(2 * i + b), ACT.Tanh, 0.5, par2[:, GATE_B + 2 * i + b:GATE_B + 2 * i + b + 1])

            for c in range(ATTN.n):
                if 3 <= c < 19:
                    i, m = (c - 3) // 4, (c - 3) % 4
                    exps(i, m, 0)
                    exps(i, m, 1)
                    turned(i, m, 0)
                    exps(i, m, 2)
                    turned(i, m, 1)
                    project(c, 0)
                    exps(i, m, 3)
                    turned(i, m, 2)
                    turned(i, m, 3)
                    rows = slice(64 * (m % 2), 64 * (m % 2) + 64)
                    if i > 0:
                        act.wait_ge(yb_split, 2 * i)
                    move(0, ("AO", m, i), ybuf[rows, m // 2, :], banks[7][rows, :])
                    project(c, 1)
                else:
                    project(c, 0)
                    project(c, 1)
                if c + 2 < ATTN.n:
                    round_weights(0, c + 2)
                else:
                    now[0] = MPROJ
                    round_weights(0, c + 2 - ATTN.n)
                    now[0] = ATTN
                if 3 <= c < 19 and m == 3:
                    for b in range(2):
                        act.wait_ge(yb_ready, 2 * i + b + 1)
                        act.activation(y_hi[:, 2 * i + b, :], ybuf[:, b, :], ACT.Copy).then_inc(yb_rounded, 1)
                if ATTN.chunks[c][0] == "pa":
                    d = ATTN.chunks[c][1]
                    act.wait_ge(m_ready, 2 * d + 2)
                    for b in range(2):
                        act.dma_start(m_s[:, 2 * d + b, :], gate_tile(2 * d + b)).then_inc(stored[b], 16)

            now[0] = MPROJ

            def conv_in(r, u, b):
                evacuate(r, MPROJ.groups[u][b], xm[:, u, b, :])

            def conv_out(r, t):
                act.wait_ge(conv_ready, r * 4 + (t + 1))
                act.activation(cth[:, t % 2, :], xc[:, t // 2, t % 2, :], ACT.Tanh).then_inc(conv_tanh, 1)

            def fold_move(r, t):
                b = t % 2
                move(r, ("fold", t), small2[:, 16 * b:16 * b + 16], banks[4][:, 0:16])

            def qk_moves(r, t):
                u, b = t // 2, t % 2
                if b == 0:
                    act.wait_ge(stored[u], r * 64 + 64)
                move(r, ("qm", t), q2[:, u, b, :], banks[4][:, :])
                move(r, ("km", t), k2[:, u, b, :], banks[5][:, :])

            def v_move(r, t):
                u, b = t // 2, t % 2
                move(r, ("vm", t), v2[:, u, :, b * P:(b + 1) * P], banks[6][:, :].rearrange("p (t n) -> p t n", t=TT))

            def store(r, u):
                for key in ("qm", "km", "vm"):
                    wait_emptied(act, r, (key, 2 * u + 1))
                for dst, src in ((q_s, q2), (k_s, k2), (xc_s, xc)):
                    act.dma_start(dst[:, ds(4 * r + 2 * u, 2), :], src[:, u, :, :]).then_inc(stored[u], 16)
                act.dma_start(v_s[:, :, ds(4 * r * P + 2 * u * P, 2 * P)], v2[:, u, :, :]).then_inc(stored[u], 16)

            def chunk_moves(r, t0, rr, u):
                fold_move(r, t0)
                round_next(r, t0 // 2)
                qk_moves(r, t0)
                v_move(r, t0)
                if rr is not None:
                    conv_in(rr, u, 0)
                fold_move(r, t0 + 1)
                qk_moves(r, t0 + 1)
                if rr is not None:
                    conv_out(rr, 2 * u)
                    conv_in(rr, u, 1)
                v_move(r, t0 + 1)
                store(r, t0 // 2)
                if rr is not None:
                    conv_out(rr, 2 * u + 1)

            def round_next(r, u):
                if isinstance(r, int) and r == MPROJ.rounds - 1:
                    now[0] = MHEAD
                    round_weights(0, u)
                    now[0] = MPROJ
                else:
                    round_weights(r + 1, u)

            conv_in(0, 0, 0)
            conv_in(0, 0, 1)
            conv_out(0, 0)
            conv_out(0, 1)
            with act.Fori(0, MPROJ.rounds - 2) as r:
                chunk_moves(r, 0, r, 1)
                chunk_moves(r, 2, r + 1, 0)
            r = MPROJ.rounds - 2
            chunk_moves(r, 0, r, 1)
            chunk_moves(r, 2, r + 1, 0)
            r = MPROJ.rounds - 1
            chunk_moves(r, 0, r, 1)
            chunk_moves(r, 2, None, None)
            def load_qk(h):
                act.dma_start(qh[:, :, :], q_s[:, ds(4 * h, 4), :]).then_inc(qk_in, 16)
                act.dma_start(kh[:, :, :], k_s[:, ds(4 * h, 4), :]).then_inc(qk_in, 16)

            def load_vx(h):
                act.dma_start(vh[:, :, :], v_s[:, :, ds(h * S, S)]).then_inc(vx_in, 16)
                act.dma_start(xch[:, :, :], xc_s[:, ds(4 * h, 4), :]).then_inc(vx_in, 16)

            now[0] = MGATE
            wait_full(act, 0, "f")
            act.activation(gt[0:4, 1, :], banks[4][0:4, :], ACT.Abs).then_inc(g_abs, 1)
            act.wait_ge(g_abs, 1)
            act.activation(gt[0:4, 1, :], gt[0:4, 1, :], ACT.Exp, scale=-1.0).then_inc(g_abs, 1)
            act.wait_ge(g_abs, 2)
            act.activation(gt[0:4, 1, :], gt[0:4, 1, :], ACT.Ln, bias=1.0).then_inc(g_ln, 1)
            for u in range(2):
                act.wait_ge(stored[u], MPROJ.rounds * 64 + 64)
            load_qk(0)
            load_vx(0)
            wait_emptied(act, 0, "cols")
            act.activation(small2[:, 16:32], small2[:, 16:32], ACT.Exp).then_inc(g_em, 1)

            now[0] = MHEAD

            def round_output(h, e):
                act.wait_ge(yh_ready, h * 4 + (e + 1))
                act.activation(yh_hi[:, e, :], xch[:, e, :], ACT.Copy).then_inc(yh_rounded, 1)

            def head(h, last=False):
                act.wait_ge(vx_in, h * 32 + 32)
                for e in range(4):
                    act.activation(xch[:, e, :], xch[:, e, :], ACT.Copy,
                                   scale=par2[:, ds(4 * h + (SKIP + e), 1)]).then_inc(skipped, 1)
                act.wait_ge(e_ready, h + 1)
                act.activation(pm[:, :], pm[:, :], ACT.Exp).then_inc(e_exp, 1)
                wait_full(act, h, ("sc", 2))
                for c in range(2):
                    for b in range(2):
                        g = MHEAD.groups[c][b]
                        src = acc_full(act, h, g)
                        act.activation(qh[:, 2 * b:2 * b + 2, c * W:(c + 1) * W], src[:, :].rearrange("p (t n) -> p t n", t=2),
                                       ACT.Tanh, scale=0.5).then_inc(emptied[g % 4], 1)
                    round_weights(h, c + 2)
                for c in (2, 3):
                    for b in range(2):
                        if c == 3 and b == 1:
                            round_output(h, 0)
                        g = MHEAD.groups[c][b]
                        src = acc_full(act, h, g)
                        act.activation(kh[:, 2 * (c - 2) + b, :], src[:, :], ACT.Tanh, scale=0.5).then_inc(zm_tanh, 1)
                        if c == 2 and b == 1:
                            act.wait_ge(hn_var, h + 1)
                            act.activation(small2[:, 48:52], small2[:, 48:52], ACT.Sqrt).then_inc(hn_rstd, 1)
                    if c == 2:
                        round_weights(h, 4)
                for e in range(1, 4):
                    round_output(h, e)
                round_weights(h, 5)
                if not last:
                    act.wait_ge(yh_split, h * 4 + 4)
                    load_qk(h + 1)
                    load_vx(h + 1)
                    round_weights(h + 1, 0)
                    round_weights(h + 1, 1)
                else:
                    now[0] = TAIL
                    act.wait_ge(yh_split, h * 4 + 4)
                    act.dma_start(mrg[:, :, :], m_s).then_inc(mrg_in, 16)
                    round_weights(0, 0)
                    round_weights(0, 1)

            with act.Fori(0, MHEAD.rounds - 1) as h:
                head(h)
            head(MHEAD.rounds - 1, True)

            def round_merged(k):
                act.wait_ge(fm_ready, k + 1)
                act.activation(m_hi[:, k, :], yacc[:, k, :], ACT.Copy).then_inc(h_rounded, 1)

            now[0] = TAIL
            for d in range(4):
                for b in range(2):
                    if d >= 2:
                        act.wait_ge(fm_ready, 2 * (d - 2) + b + 1)
                    n = GATE_B + 8 + 2 * d + b
                    evacuate(0, TAIL.groups[d][b], th2[:, 2 * (d % 2) + b, :], ACT.Tanh, 0.5, par2[:, n:n + 1])
                for k in (2 * d - 2, 2 * d - 1) if d else ():
                    round_merged(k)
                if d == 3:
                    round_merged(6)
                    round_merged(7)
                round_weights(0, d + 2)
            for c in (6, 7):
                round_weights(0, c)
            act.wait_ge(var_ready, DEPTH * 3 + 2)
            act.activation(small2[:, 56:60], small2[:, 56:60], ACT.Sqrt).then_inc(rstd_ready, 1)
            for k in range(KT):
                act.wait_ge(out_ready, k + 1)
                act.dma_start(a["out"][:, k, :], yacc[:, k, :]).then_inc(y_out, 16)
            act.wait_ge(y_out, 16 * KT)
            now[0] = LAYERS

        def gate_tile(d):
            n = d // 2
            return qkv[:, 0, n, (d % 2) * S:(d % 2 + 1) * S] if n < 3 else qkv[:, 1, 0, (d % 2) * S:(d % 2 + 1) * S]

        def second_vector(dve, rstd_of, add_square):
            step = [0]

            def begin():
                step[0] = 0
                dve.sem_clear(dve_step)

            def link(ins):
                step[0] += 1
                ins.then_inc(dve_step, 1)
                dve.wait_ge(dve_step, step[0])

            now[0] = ATTN
            begin()

            def biased(i, m, tt):
                src = wait_full(dve, 0, ("L", m, tt, i))
                n = 4 * i + m
                if tt == 0:
                    dve.wait_ge(mst_in[n % 2], 16 * (n // 2 + 1))
                if tt >= 2:
                    wait_full(dve, 0, ("T", m, tt - 2, i))
                elif n > 0:
                    wait_full(dve, 0, ("T", (n - 1) % 4, tt + 2, (n - 1) // 4))
                w = (tt + 1) * P
                dve.tensor_tensor_reduce(probs2[:, tt % 2, 0:w], src[:, 0:w], mst[:, n % 2, S - w:S], -1.0, 3.0e38,
                                         ALU.add, ALU.min, small2[:, tt:tt + 1]).then_inc(emptied[4 + tt % 2], 1)

            def normalize(i, m, tt):
                w = (tt + 1) * P
                dve.wait_ge(pexp2, 16 * i + 4 * m + tt + 1)
                link(dve.reciprocal(small2[:, 8 + tt:9 + tt], small2[:, 4 + tt:5 + tt]))
                dve.tensor_scalar(probs2[:, tt % 2, 0:w], probs2[:, tt % 2, 0:w], small2[:, 8 + tt:9 + tt], None,
                                  ALU.mult).then_inc(pn2, 1)

            for c in range(ATTN.n):
                kind, j = ATTN.chunks[c]
                if 3 <= c < 19:
                    i, m = (c - 3) // 4, (c - 3) % 4
                    biased(i, m, 0)
                    biased(i, m, 1)
                    normalize(i, m, 0)
                    biased(i, m, 2)
                    normalize(i, m, 1)
                    if m == 3:
                        zg = ATTN.groups[c]
                        dve.wait_ge(z_tanh, 2 * i + 1)
                        dve.scalar_tensor_tensor(zt[:, 0, :], zt[:, 0, :], 1.0, banks[zg[0] % 4][:, :], ALU.add, ALU.mult)\
                           .then_inc(emptied[zg[0] % 4], 1)
                    biased(i, m, 3)
                    normalize(i, m, 2)
                    normalize(i, m, 3)
                    if m == 3:
                        dve.wait_ge(z_tanh, 2 * i + 2)
                        dve.scalar_tensor_tensor(zt[:, 1, :], zt[:, 1, :], 1.0, banks[zg[1] % 4][:, :], ALU.add, ALU.mult)\
                           .then_inc(emptied[zg[1] % 4], 1)
                        wait_emptied(dve, 0, ("AO", m, i))
                        for b in range(2):
                            acc_emptied(dve, 0, zg[b])
                            dve.scalar_tensor_tensor(ybuf[:, b, :], ybuf[:, b, :], 0.5, zt[:, b, :], ALU.mult,
                                                     ALU.mult).then_inc(yb_ready, 1)
                if kind == "pa":
                    for b in range(2):
                        d = 2 * j + b
                        g = ATTN.groups[c][b]
                        src = acc_full(dve, 0, g)
                        link(dve.scalar_tensor_tensor(gate_tile(d), gate_tile(d), 1.0, src[:, :], ALU.add, ALU.mult))
                        dve.sem_inc(emptied[g % 4], 1)
                        dve.sem_inc(m_ready, 1)

            now[0] = MPROJ
            dve.memset(small2[:, 32:40], 0.0).then_inc(zero_ready, 1)
            dve.wait_ge(bd_in, 32)

            def blocks(r, t):
                b = t % 2
                if b == 0:
                    wait_full(dve, r, ("vm", t + 1), back=1)
                wait_full(dve, r, ("fold", (t - 2) % 4), back=int(t < 2))
                for m in range(3):
                    for n, out in ((0, bd[:, t, m, :]), (1, bdT[:, b, m, :])):
                        w = wraw[:, n, m, ds(4 * r + t, 1), :].broadcast_to((P, 32, 4))
                        ins = dve.tensor_tensor(out.rearrange("p (g o) -> p g o", o=4),
                                                mask4[:, :].unsqueeze(2).broadcast_to((P, 32, 4)), w, ALU.mult)
                ins.then_inc(bd_ready, 1)

            def conv(r, t):
                u, b = t // 2, t % 2
                o, x = xc[:, u, b, :], xm[:, u, b, :]
                acc_emptied(dve, r, MPROJ.groups[u][b])
                if b == 0:
                    dve.wait_ge(stored[u], r * 64 + 64)

                def par(n):
                    return par2[:, ds(4 * r + (n + t), 1)]

                link(dve.tensor_scalar(o, x, par(CONV_W + 48), par(CONV_B), ALU.mult, ALU.add))
                for k in range(3):
                    n = 3 - k
                    ins = dve.scalar_tensor_tensor(o[:, n:S], x[:, 0:S - n], par(CONV_W + 16 * k), o[:, n:S], ALU.mult, ALU.add)
                    if k < 2:
                        link(ins)
                    else:
                        ins.then_inc(conv_ready, 1)
                dve.wait_ge(conv_tanh, r * 4 + (t + 1))
                dve.scalar_tensor_tensor(o, cth[:, b, :], 1.0, o, ALU.add, ALU.mult).then_inc(xc_ready, 1)

            with dve.Fori(0, MPROJ.rounds) as r:
                begin()
                for t in range(4):
                    blocks(r, t)
                    conv(r, t)

            now[0] = MGATE
            begin()
            wait_full(dve, 0, "gates")
            dve.tensor_scalar(gt[0:8, 0, :], banks[7][0:8, :], bif[:, 0:1], None, ALU.add).then_inc(emptied[7], 1)
            wait_emptied(dve, 0, "gates")
            dve.wait_ge(g_ln, 1)
            dve.scalar_tensor_tensor(gt[0:4, 2, :], banks[4][0:4, :], 0.0, gt[0:4, 1, :], ALU.min, ALU.subtract)\
               .then_inc(emptied[4], 1)
            wait_emptied(dve, 0, "f")
            link(dve.tensor_tensor_scan(gt[0:4, 3, :], ones[0:4, 0:1].broadcast_to((4, S)), gt[0:4, 2, :], 0.0, ALU.mult, ALU.add))
            link(dve.tensor_tensor(gt[0:4, 1, :], gt[0:4, 0, :], gt[0:4, 3, :], ALU.subtract))
            link(dve.tensor_tensor_scan(gt[0:4, 2, :], gt[0:4, 1, :], gt[0:4, 1, :], 0.0, ALU.max, ALU.max))
            dve.scalar_tensor_tensor(gt[0:4, 3, :], gt[0:4, 3, :], -1.0, gt[0:4, 2, :], ALU.mult, ALU.subtract).then_inc(g_neg, 1)
            link(dve.tensor_scalar(negM[:, :], gt[0:4, 2, :], -1.0, None, ALU.mult))
            wait_full(dve, 0, "cols")
            dve.tensor_copy(small2[:, 0:32], banks[5][:, 0:32]).then_inc(emptied[5], 1)
            wait_emptied(dve, 0, "cols")
            dve.wait_ge(g_em, 1)

            now[0] = MHEAD

            def head(h):
                begin()
                dve.tensor_scalar(negM_h[:, :], negM[:, :], ident[0:4, ds(h, 1)], None, ALU.mult).then_inc(mh_ready, 1)
                src = wait_full(dve, h, "M")
                for j in range(TT):
                    ins = dve.tensor_scalar(pm[:, WOFF[j]:WOFF[j] + S - j * P], src[:, j * P:S],
                                            small2[:, ds(h + 4 * j, 1)], 0.0, ALU.add, ALU.min)
                    if j == 3:
                        ins.then_inc(emptied[7], 1)
                wait_emptied(dve, h, "M")
                for j in range(TT):
                    ins = dve.tensor_tensor(pm[:, WOFF[j]:WOFF[j] + P], pm[:, WOFF[j]:WOFF[j] + P], trilT_add, ALU.add)
                    if j == 3:
                        ins.then_inc(e_ready, 1)
                dve.wait_ge(e_exp, h + 1)
                for bank in range(3):
                    src = wait_full(dve, h, ("sc", bank))
                    n = (512, 384, 384)[bank]
                    o = pm[:, WOFF[bank]:WOFF[bank] + n]
                    dve.scalar_tensor_tensor(o, src[:, 0:n], 512.0 ** -0.5, o, ALU.mult, ALU.mult).then_inc(emptied[4 + bank], 1)
                wait_full(dve, h, "den")
                d, r = small2[:, 40:44], small2[:, 44:48]
                dve.tensor_copy(d, banks[7][:, 0:4]).then_inc(emptied[7], 1)
                wait_emptied(dve, h, "den")
                link(dve.scalar_tensor_tensor(r, d, -1.0, d, ALU.mult, ALU.max))
                em = small2[:, 16:32].rearrange("p (t h) -> p t h", h=4)[:, :, ds(h, 1)].rearrange("p t o -> p (t o)")
                link(dve.tensor_tensor(r, r, em, ALU.max))
                link(dve.reciprocal(r, r))
                link(dve.tensor_scalar(r, r, 0.5, None, ALU.mult))
                for tt in range(TT):
                    src = wait_full(dve, h, ("num", tt))
                    if tt == 0:
                        for c in (0, 1):
                            for g in MHEAD.groups[c]:
                                acc_emptied(dve, h, g)
                    dve.scalar_tensor_tensor(qh[:, tt, :], qh[:, tt, :], 1.0, src[:, :], ALU.add, ALU.mult)\
                       .then_inc(emptied[4 + tt % 2], 1)
                    wait_emptied(dve, h, ("num", tt))
                    link(dve.bn_stats(hstats[:, tt, 0:6], qh[:, tt, :]))
                    link(dve.bn_aggr(hstats[:, tt, 6:8], hstats[:, tt, 0:6]))
                    if tt == 1:
                        silu_z(h, 2, 0)
                v = small2[:, 48:52]
                link(dve.tensor_tensor(v, hstats[:, :, 7], r, ALU.mult))
                link(dve.tensor_tensor(v, v, r, ALU.mult))
                link(dve.tensor_scalar(v, v, EPS, None, ALU.add))
                dve.reciprocal(v, v).then_inc(hn_var, 1)
                silu_z(h, 2, 1)
                dve.wait_ge(hn_rstd, h + 1)
                link(dve.tensor_tensor(v, v, r, ALU.mult))
                for tt in range(TT):
                    dve.tensor_scalar(qh[:, tt, :], qh[:, tt, :], hstats[:, tt, 6:7], v[:, tt:tt + 1], ALU.subtract,
                                      ALU.mult).then_inc(hn_ready, 1)
                silu_z(h, 3, 0)
                dve.wait_ge(skipped, h * 4 + 4)
                for tt in range(TT):
                    src = wait_full(dve, h, ("hT", tt))
                    for e in range(4):
                        o = xch[:, e, tt * P:(tt + 1) * P]
                        ins = dve.scalar_tensor_tensor(o, src[:, e * P:(e + 1) * P], par2[:, ds(4 * h + (HEAD_G + e), 1)], o,
                                                       ALU.mult, ALU.add)
                        if e == 3:
                            ins.then_inc(emptied[6 + tt % 2], 1)
                    wait_emptied(dve, h, ("hT", tt))
                for e in range(4):
                    if e == 3:
                        silu_z(h, 3, 1)
                    dve.scalar_tensor_tensor(xch[:, e, :], xch[:, e, :], 0.5, kh[:, e, :], ALU.mult, ALU.mult).then_inc(yh_ready, 1)
                dve.wait_ge(yacc_zero, 1)
                for c in (4, 5):
                    for n, g in enumerate(MHEAD.groups[c]):
                        d = 4 * (c - 4) + n
                        src = acc_full(dve, h, g)
                        dve.tensor_tensor(yacc[:, d, :], src[:, :], yacc[:, d, :], ALU.add).then_inc(emptied[g % 4], 1)
                        acc_emptied(dve, h, g)

            def silu_z(h, c, b):
                g = MHEAD.groups[c][b]
                e = 2 * (c - 2) + b
                dve.wait_ge(zm_tanh, h * 4 + (e + 1))
                dve.scalar_tensor_tensor(kh[:, e, :], kh[:, e, :], 1.0, banks[g % 4][:, :], ALU.add, ALU.mult)\
                   .then_inc(emptied[g % 4], 1)
                acc_emptied(dve, h, g)

            with dve.Fori(0, MHEAD.rounds - 1) as h:
                head(h)
            head(MHEAD.rounds - 1)

            now[0] = TAIL
            begin()
            dve.wait_ge(mrg_in, 16)
            for k in range(KT):
                acc_emptied(dve, 0, TAIL.groups[k // 2][k % 2])
                link(dve.scalar_tensor_tensor(yacc[:, k, :], th2[:, k % 4, :], 1.0, yacc[:, k, :], ALU.add, ALU.mult))
                dve.tensor_tensor(yacc[:, k, :], yacc[:, k, :], mrg[:, k, :], ALU.add).then_inc(fm_ready, 1)
            for k in range(KT):
                g = TAIL.groups[4 + k // 2][k % 2]
                src = acc_full(dve, 0, g)
                link(dve.scalar_tensor_tensor(xT[:, k, :], src[:, :], 0.5, xT[:, k, :], ALU.mult, ALU.add))
                dve.sem_inc(emptied[g % 4], 1)
                add_square(link, k, xT, sqf)
            rstd = rstd_of(0, "ssf", "rsf", 1.0 / D, small2[:, 56:60], diag3, DEPTH * 3 + 2)
            for k in range(KT):
                dve.scalar_tensor_tensor(yacc[:, k, :], xT[:, k, :], par2[:, N_OUT0 + k:N_OUT0 + k + 1], rstd[:, :],
                                         ALU.mult, ALU.mult).then_inc(out_ready, 1)
            now[0] = LAYERS

        def second_pool(pool, split_weights):
            def split(dst, src, hi, rounded, n, signal):
                pool.wait_ge(rounded, n)
                pool.tensor_tensor(dst, src, hi, ALU.subtract).then_inc(signal, 1)

            now[0] = ATTN
            for k in range(KT):
                split(h_lo[:, k, :], U[:, k, :], h_hi[:, k, :], h_rounded, DEPTH * 24 + k + 1, h_split)
            for c in range(ATTN.n):
                if c + 2 < ATTN.n:
                    split_weights(0, c + 2)
                if 3 <= c < 19 and (c - 3) % 4 == 3:
                    i = (c - 3) // 4
                    for b in range(2):
                        split(y_lo[:, 2 * i + b, :], ybuf[:, b, :], y_hi[:, 2 * i + b, :], yb_rounded, 2 * i + b + 1, yb_split)
            now[0] = MPROJ
            with pool.Fori(0, MPROJ.rounds) as r:
                split_weights(r, 0)
                split_weights(r, 1)
            now[0] = MHEAD
            split_weights(0, 0)
            split_weights(0, 1)
            now[0] = MGATE
            wait_full(pool, 0, "gates")
            for u in range(2):
                pool.wait_ge(stored[u], MPROJ.rounds * 64 + 64)
            pool.memset(yacc[:, :, :], 0.0).then_inc(yacc_zero, 1)
            now[0] = MHEAD

            def head(h, last=False):
                for c in range(2, 5):
                    split_weights(h, c)
                for e in range(4):
                    split(yh_lo[:, e, :], xch[:, e, :], yh_hi[:, e, :], yh_rounded, h * 4 + (e + 1), yh_split)
                split_weights(h, 5)
                if last:
                    now[0] = TAIL
                    split_weights(0, 0)
                    split_weights(0, 1)
                else:
                    split_weights(h + 1, 0)
                    split_weights(h + 1, 1)

            with pool.Fori(0, MHEAD.rounds - 1) as h:
                head(h)
            head(MHEAD.rounds - 1, True)
            for c in range(2, 6):
                for k in (2 * c - 6, 2 * c - 5) if c > 2 else ():
                    split(m_lo[:, k, :], yacc[:, k, :], m_hi[:, k, :], h_rounded, DEPTH * 24 + 8 + k + 1, h_split)
                if c == 5:
                    for k in (6, 7):
                        split(m_lo[:, k, :], yacc[:, k, :], m_hi[:, k, :], h_rounded, DEPTH * 24 + 8 + k + 1, h_split)
                split_weights(0, c)
            for c in (6, 7):
                split_weights(0, c)
            now[0] = LAYERS

        @block.sync
        def _(sp_):
            def load(l, c):
                slot, n = c % 2, columns(now[0].chunks[c])
                sp_.wait_ge(w_split, split_count(l, c - 2))
                src = a["stream"][ds(l * now[0].n + (now[0].c0 + c), 1), :, 0:n].rearrange("o p n -> p (o n)")
                sp_.dma_start(w_raw[:, slot, 0:n], src).then_inc(w_landed[slot], 16)

            for dst, src in first_loads:
                sp_.dma_start(dst, src).then_inc(first_in, 16)
            for dst, src in const_loads:
                sp_.dma_start(dst, src).then_inc(const_in, 16)
            with sp_.Fori(0, DEPTH) as l:
                for c in range(NCH):
                    load(l, c)
                    if c == 4:
                        sp_.wait_ge(rot_ready, l * 6 + 6)
                        sp_.dma_start(ws[:, :, :], a["wsT"][:, ds(l, 1), :, :].rearrange("s o g t -> s (o g) t")).then_inc(ws_in, 16)
                    if c == 18:
                        wait_full(sp_, l, ("AO", 3))
                        sp_.dma_start(ptok[:, :, :], a["pT"][:, ds(l, 1), :, :].rearrange("p o i t -> p (o i) t")).then_inc(p_in, 16)
            second_loads(sp_, load)

        @block.tensor
        def _(pe):
            def product(out, pairs, start, stop):
                n = 3 * len(pairs)
                i = 0
                for (a_hi, a_lo), (b_hi, b_lo) in pairs:
                    for lhsT, rhs in ((a_hi, b_hi), (a_hi, b_lo), (a_lo, b_hi)):
                        last = pe.matmul(out, lhsT, rhs, start=start and i == 0, stop=stop and i == n - 1)
                        i += 1
                return last

            def weights(c, col, n):
                return w_hi[:, c % 2, col:col + n], w_lo[:, c % 2, col:col + n]

            def act(k, cols=slice(0, S)):
                return h_hi[:, k, cols], h_lo[:, k, cols]

            def operand(kind, k):
                return {"pa": (y_hi[:, k, :], y_lo[:, k, :]), "fo": (m_hi[:, k, :], m_lo[:, k, :])}.get(kind) or act(k)

            def first_part(l, c, s, first):
                if s < 2:
                    pe.wait_ge(w_split, split_count(l, c, s))
                b, low = s % 4 // 2, s >= 4
                g = now[0].groups[c][b]
                if s in (0, 2):
                    acc_empty(pe, l, g)
                for k in range(4 * (s % 2), 4 * (s % 2) + 4):
                    w = weights(c, k * W + b * P, P)
                    x = operand(now[0].chunks[c][0], k)
                    if s < 2:
                        pe.wait_ge(h_rounded, l * 24 + (first + k + 1))
                    if s in (4, 5):
                        pe.wait_ge(h_split, l * 24 + (first + k + 1))
                    for lhsT in (w[:1] if low else w):
                        last = pe.matmul(banks[g % 4][:, :], lhsT, x[int(low)], start=s in (0, 2) and k == 0 and lhsT is w[0],
                                         stop=low and s % 2 == 1 and k == KT - 1)
                if s in (5, 7):
                    last.then_inc(full[g % 4], 1)

            def part(l, c, s):
                kind, i = now[0].chunks[c]
                token_major = i in TOKEN_MAJOR or kind in ("v", "om")
                first = {("proj", "aq"): 0, ("out", 0): 8, ("pgate", 0): 16, ("q", 0): DEPTH * 24,
                         ("fo", 0): DEPTH * 24 + 8}.get((kind, i))
                if first is not None:
                    first_part(l, c, s, first)
                    return
                if s == 0:
                    pe.wait_ge(w_split, split_count(l, c, 0))
                if s == (1 if token_major else 2):
                    pe.wait_ge(w_split, split_count(l, c, 1))
                b = s // 4
                g = now[0].groups[c][b]
                if s % 4 == 0:
                    acc_empty(pe, l, g)
                acc = banks[g % 4]
                if token_major:
                    tt, half = 2 * b + s % 4 // 2, s % 2
                    last = product(acc[:, (tt % 2) * W:(tt % 2 + 1) * W],
                                   [(act(k, slice(tt * P, (tt + 1) * P)), weights(c, k * W, W))
                                    for k in range(4 * half, 4 * half + 4)], half == 0, half == 1)
                else:
                    stride = 260 if i == "idx" else W
                    for k in (2 * (s % 4), 2 * (s % 4) + 1):
                        x = operand(kind, k)
                        last = product(acc[:, :], [(weights(c, k * stride + b * P, P), x)], k == 0, k == KT - 1)
                if s % 4 == 3:
                    last.then_inc(full[g % 4], 1)

            def rotate(l, key, mat, src):
                out = wait_empty(pe, l, key)
                pe.matmul(out[:, :], mat, src, start=True, stop=True).then_inc(full[now[0].side[key][0]], 1)

            def index_logits(l, tt):
                n = (tt + 1) * P
                for h in range(4):
                    out = wait_empty(pe, l, ("idx", tt, h))
                    rows = slice(32 * h, 32 * h + 32)
                    pe.matmul(out[:, 0:n], iqk[rows, 0, tt * P:(tt + 1) * P], iqk[rows, 1, 0:n],
                              start=True, stop=True).then_inc(full[4 + h], 1)

            def c_scores(l, h, what):
                rows = slice(64 * (h % 2), 64 * (h % 2) + 64)
                i = h // 2
                for bank in range(3):
                    out = wait_empty(pe, l, (what, h, bank))
                    js = (2, 3) if bank == 2 else (bank,)
                    for j in js:
                        o = out[:, WOFF[j] - WOFF[js[0]]:WOFF[j] - WOFF[js[0]] + S - j * P]
                        if what == "Z":
                            last = pe.matmul(o, ck[rows, i, j * P:(j + 1) * P], cq[rows, i, j * P:S],
                                             start=j == js[0], stop=True, skip_group_check=True)
                        else:
                            for jj in range(j, TT):
                                last = pe.matmul(o[:, (jj - j) * P:], upinc_neg if jj == j else ones_neg,
                                                 sp[:, WOFF[jj]:WOFF[jj] + S - jj * P], start=False, stop=jj == TT - 1,
                                                 skip_group_check=True)
                    last.then_inc(full[4 + bank], 1)

            def c_values(l, h):
                out = wait_empty(pe, l, ("CO", h))
                rows = slice(64 * (h % 2), 64 * (h % 2) + 64)
                for j in range(TT):
                    last = pe.matmul(out[rows, j * P:S], cv[:, j, 64 * h:64 * h + 64],
                                     wt[:, WOFF[j]:WOFF[j] + S - j * P], start=j == 0, stop=j == TT - 1)
                last.then_inc(full[7], 1)

            def d_mix(l, i):
                pe.wait_ge(ws_ready, l + 1)
                pe.wait_ge(vn_ready, l + 1)
                out = wait_empty(pe, l, ("dmix", i))
                for g in (2 * i, 2 * i + 1):
                    rows = slice(64 * (g % 2), 64 * (g % 2) + 64)
                    for tt in range(TT):
                        last = pe.matmul(out[rows, tt * P:(tt + 1) * P], dvt[:, tt, 64 * g:64 * g + 64],
                                         ws[:, g, :], start=True, stop=True)
                last.then_inc(full[7], 1)

            def a_logits(l, tt, h):
                out = wait_empty(pe, l, ("L", tt, h))
                rows = slice(64 * (h % 2), 64 * (h % 2) + 64)
                pe.matmul(out[:, 0:(tt + 1) * P], aq[rows, h // 2, tt * P:(tt + 1) * P],
                          ak[rows, h // 2, 0:(tt + 1) * P], start=True, stop=True).then_inc(full[4 + h % 2], 1)

            def a_transpose(l, tt, h):
                out = wait_empty(pe, l, ("T", tt, h))
                pe.wait_ge(pn_ready, l * 16 + (4 * tt + h + 1))
                for j in range(tt + 1):
                    last = pe.transpose(out[:, j * P:(j + 1) * P], probs[:, h % 2, j * P:(j + 1) * P], ident)
                last.then_inc(full[6], 1)

            def a_values(l, tt, h):
                if h == 0:
                    wait_empty(pe, l, ("AO", tt))
                wait_emptied(pe, l, ("T", tt, h))
                rows = slice(64 * (h % 2), 64 * (h % 2) + 64)
                for j in range(tt + 1):
                    last = pe.matmul(banks[7][rows, (h // 2) * P:(h // 2 + 1) * P], av[:, j, 64 * h:64 * h + 64],
                                     probT[:, h % 2, j * P:(j + 1) * P], start=j == 0, stop=j == tt)
                if h == 3:
                    last.then_inc(full[7], 1)

            def side(l, c, s):
                if c == 1 and s == 0:
                    for i in range(2):
                        acc_emptied(pe, l, GROUPS[0][i])
                        rotate(l, f"rotq{i}", rot64, raw[:, i, :])
                if c == 2 and s == 0:
                    for i in range(2):
                        acc_emptied(pe, l, GROUPS[1][i])
                        rotate(l, f"rotk{i}", rot64, raw[:, 2 + i, :])
                if c == 2 and s == 7:
                    out = wait_empty(pe, l, "iw")
                    product(out[0:4, :], [(weights(2, k * 260 + 256, 4), act(k)) for k in range(KT)],
                            True, True).then_inc(full[6], 1)
                if c == 3 and s == 2:
                    wait_emptied(pe, l, "iw")
                    out = wait_empty(pe, l, "iwT")
                    for tt in range(TT):
                        last = pe.matmul(out[:, 4 * tt:4 * tt + 4], diag[0:4, tt * P:(tt + 1) * P], ident[0:4, 0:4],
                                         start=True, stop=True)
                    last.then_inc(full[7], 1)
                if c == 3 and s == 0:
                    for i in range(2):
                        acc_emptied(pe, l, GROUPS[2][i])
                        rotate(l, f"roti{i}", rot32, raw[:, 4 + i, :])
                if c == 4 and s in (0, 3, 6):
                    if s == 0:
                        pe.wait_ge(rot_ready, l * 6 + 6)
                    index_logits(l, 3 - s // 3)
                if 8 <= c < 12:
                    h = c - 8
                    if s == 0:
                        if h == 0:
                            for g in (GROUPS[5] + GROUPS[6]):
                                acc_emptied(pe, l, g)
                        c_scores(l, h, "Z")
                    if h == 3 and s in (3, 5):
                        d_mix(l, s // 4)
                    if s == SUM_AT:
                        pe.wait_ge(sp_ready, l * 4 + (h + 1))
                        c_scores(l, h, "Sx")
                if 9 <= c < 13 and s == 1:
                    pe.wait_ge(cw_exp, l * 4 + (c - 8))
                    c_values(l, c - 9)
                if 12 <= c < 16:
                    tt = c - 12
                    if s == 0:
                        a_logits(l, tt, 0)
                        a_logits(l, tt, 1)
                    if s == 2:
                        a_transpose(l, tt, 0)
                        a_logits(l, tt, 2)
                    if s == 3:
                        a_transpose(l, tt, 1)
                        a_values(l, tt, 0)
                        a_logits(l, tt, 3)
                    if s == 4:
                        a_transpose(l, tt, 2)
                        a_values(l, tt, 1)
                    if s == 5:
                        a_transpose(l, tt, 3)
                        a_values(l, tt, 2)
                    if s == 6:
                        a_values(l, tt, 3)

            def column_sums(l, key, total, count):
                out = wait_empty(pe, l, key)
                pe.wait_ge(sum_ready, count)
                for tt in range(TT):
                    last = pe.matmul(out[:, tt:tt + 1], total[:, tt * P:(tt + 1) * P], ones[:, 0:1], start=True, stop=True)
                last.then_inc(full[now[0].side[key][0]], 1)

            def spread(l, key, diagonal, count):
                out = wait_empty(pe, l, key)
                pe.wait_ge(diag_ready, count)
                pe.matmul(out[:, :], ones, diagonal[:, :], start=True, stop=True).then_inc(full[now[0].side[key][0]], 1)

            def branches(l, c):
                pe.wait_ge(w_split, split_count(l, c, 0))
                if c == 18:
                    pe.wait_ge(o_split, l * 8 + 8)
                for n, g in enumerate(GROUPS[c]):
                    if n == 2:
                        pe.wait_ge(w_split, split_count(l, c, 1))
                    acc_empty(pe, l, g)
                    product(banks[g % 4][:, :], [(weights(c, (2 * n + kk) * P, P),
                                                  (o_hi[:, 2 * n + kk, :], o_lo[:, 2 * n + kk, :]))
                                                 for kk in range(2)], True, True).then_inc(full[g % 4], 1)

            def embedding(l, c):
                pe.wait_ge(w_split, split_count(l, c))
                if c == 44:
                    pe.wait_ge(pt_split, l * 2 + 2)
                for b, g in enumerate(GROUPS[c]):
                    if c == 44 and b == 2:
                        column_sums(l, "ssy", sq[:, KT - 1, :], l * 2 + 2)
                    acc_empty(pe, l, g)
                    product(banks[g % 4][:, :], [(weights(c, kk * S + b * P, P), (pT_hi[:, kk, :], pT_lo[:, kk, :]))
                                                 for kk in range(2)], True, True).then_inc(full[g % 4], 1)
                if c == 44:
                    spread(l, "rsy", diag, l * 2 + 2)

            def normaliser(l):
                column_sums(l, "ssx", U[:, KT - 1, :], l * 2 + 1)
                spread(l, "rsx", diag, l * 2 + 1)

            for b in range(8):
                pe.sem_inc(full[b], 1)
            pe.wait_ge(first_in, 16 * len(first_loads))
            pe.matmul(banks[0][0:16, :], rel[:, :], onehot[:, 0:512], start=True, stop=True)
            pe.matmul(banks[1][0:16, 0:128], rel[:, :], onehot[:, 512:640], start=True, stop=True).then_inc(bias_product, 1)
            pe.wait_ge(setup_dve, SETUP_BIAS)
            pe.wait_ge(const_in, 16 * NCONST)
            normaliser(0)
            with pe.Fori(0, DEPTH) as l:
                for c, (kind, i) in enumerate(CH):
                    if kind == "branch":
                        branches(l, c)
                    elif kind == "ple":
                        embedding(l, c)
                    else:
                        for s in range(8):
                            part(l, c, s)
                            side(l, c, s)
                normaliser(l + 1)
            second_products(pe, product, weights, act, part, column_sums, spread)

        @block.scalar
        def _(act):
            for k in range(0, KT, 4):
                act.dma_start(xT[:, k:k + 4, :], a["xT"][:, k:k + 4, :]).then_inc(x_in[k // 4], 16)
            for k in range(KT):
                act.wait_ge(x_in[k // 4], 16)
                act.activation(U[:, k, :], xT[:, k, :], ACT.Square).then_inc(sq_ready, 1)

            def round_weights(l, c):
                slot = c % 2
                act.wait_ge(w_landed[slot], (l * (now[0].n // 2) + ((now[0].c0 + c) // 2 + 1)) * 16)
                start = now[0].groups[c][0]
                between = now[0].groups[c - 1] if c else now[0].before_first if type(l) is int and l == 0 else now[0].groups[-1]
                before = start - len(between) - 1
                act.wait_ge(full[before % 4], acc_count(l, before, 1))
                n = columns(now[0].chunks[c])
                for cols in (slice(0, n // 2), slice(n // 2, n)):
                    act.activation(w_hi[:, slot, cols], w_raw[:, slot, cols], ACT.Copy).then_inc(w_rounded, 1)

            def round_ahead(l, c):
                if c < NCH:
                    round_weights(l, c)
                else:
                    round_weights(l + 1, c - NCH)

            def evacuate(l, g, dst, scale=1.0):
                src = acc_full(act, l, g)
                act.activation(dst, src[:, :], ACT.Copy, scale=scale).then_inc(emptied[g % 4], 1)

            def move_side(l, key, dst, src, func=ACT.Copy, scale=1.0):
                wait_full(act, l, key)
                act.activation(dst, src, func, scale=scale).then_inc(emptied[now[0].side[key][0]], 1)

            def square_root(l, n, t):
                act.wait_ge(var_ready, l * 3 + n)
                act.activation(t, t, ACT.Sqrt).then_inc(rstd_ready, 1)

            def round_tile(l, k, first, src):
                act.activation(h_hi[:, k, :], src, ACT.Copy).then_inc(h_rounded, 1)

            def a_exp(l, tt, h):
                wait_emptied(act, l, ("L", tt, h))
                n = (tt + 1) * P
                act.activation(probs[:, h % 2, 0:n], probs[:, h % 2, 0:n], ACT.Exp, scale=-1.0,
                               bias=small[:, 24 + h:25 + h], accum_out=small[:, 28 + h:29 + h]).then_inc(pexp, 1)

            def a_move(l, tt, h):
                move_side(l, ("T", tt, h), probT[:, h % 2, 0:(tt + 1) * P], banks[6][:, 0:(tt + 1) * P])

            def index_relu(l, tt):
                for h in range(4):
                    if tt < 3:
                        act.wait_ge(relu_used, l * 12 + (4 * (2 - tt) + h + 1))
                    n = (tt + 1) * P
                    move_side(l, ("idx", tt, h), relu[:, h, 0:n], banks[4 + h][:, 0:n], ACT.Relu)

            def c_exp(l, h):
                act.wait_ge(cw_ready, l * 4 + (h + 1))
                act.activation(wt[:, :], wt[:, :], ACT.Exp).then_inc(cw_exp, 1)

            def c_out(l, c):
                if 9 <= c < 13:
                    h = c - 9
                    rows = slice(64 * (h % 2), 64 * (h % 2) + 64)
                    move_side(l, ("CO", h), U[rows, 4 + h // 2, :], banks[7][rows, :])

            def gate_tanh(l, c, b):
                g = GROUPS[c][b]
                src = acc_full(act, l, g)
                if c > 12:
                    act.wait_ge(o_f32, l * 8 + 2 * (c - 12))
                act.activation(cvt[:, b, :], src[:, :], ACT.Tanh, scale=0.5).then_inc(th_ready, 1)

            def round_branch(l, c):
                n = int(CH[c][1][1])
                for b in range(2):
                    act.wait_ge(o_f32, l * 8 + (2 * (c - 12) + b + 1))
                    act.activation(o_hi[:, 2 * n + b, :], U[:, 2 * n + b, :], ACT.Copy).then_inc(o_rounded, 1)

            def open_layer(l):
                for k in range(KT):
                    act.wait_ge(h_ready, l * 16 + (k + 1))
                    round_tile(l, k, 0, U[:, k, :])

            square_root(0, 1, small[:, 44:48])
            round_weights(0, 0)
            round_weights(0, 1)
            open_layer(0)
            act.wait_ge(setup_dve, SETUP_ANGLES)
            for i, t in enumerate((sin64, cos64, sin32, cos32)):
                act.activation(t[:, :], ang[:, i, :], ACT.Sin).then_inc(setup_act, 1)
            act.wait_ge(bias_stored, 16)
            with act.Fori(0, DEPTH) as l:
                for c in range(16):
                    name = CH[c][1]
                    g0, g1 = GROUPS[c]
                    if 9 <= c < 13:
                        c_exp(l, c - 9)
                    if 8 <= c < 12:
                        h = c - 8
                        for bank in range(3):
                            src = wait_full(act, l, ("Z", h, bank))
                            n = (512, 384, 384)[bank]
                            o = WOFF[bank]
                            act.activation(az[:, o:o + n], src[:, 0:n], ACT.Abs).then_inc(act_step, 1)
                        act.wait_ge(act_step, l * 16 + (4 * h + 3))
                        act.activation(az[:, :], az[:, :], ACT.Exp, scale=-1.0).then_inc(act_step, 1)
                        act.wait_ge(act_step, l * 16 + (4 * h + 4))
                        act.activation(az[:, :], az[:, :], ACT.Ln, bias=1.0).then_inc(z_ln, 1)
                    if 12 <= c:
                        tt = c - 12
                        a_exp(l, tt, 0)
                        a_exp(l, tt, 1)
                        a_move(l, tt, 0)
                        a_exp(l, tt, 2)
                        a_move(l, tt, 1)
                    if c == 10:
                        square_root(l, 2, small[:, 16:20])
                    c_out(l, c)
                    dst = {"aq": raw[:, 0:2, :], "ak": raw[:, 2:4, :], "idx": raw[:, 4:6, :], "cq": cq, "ck": ck,
                           "du": U[:, 6:8, :], "bc": U[:, 2:4, :]}.get(name)
                    if name in TOKEN_MAJOR:
                        t = {"av": av, "cv": cv, "dv": dvt}[name]
                        for b in range(2):
                            evacuate(l, GROUPS[c][b], t[:, 2 * b:2 * b + 2, :].rearrange("p t n -> p (t n)"))
                    elif dst is not None:
                        for b in range(2):
                            if c == 4:
                                index_relu(l, 3 - b)
                            evacuate(l, GROUPS[c][b], dst[:, b, :], scale=0.125 if name in ("aq", "cq") else 1.0)
                    elif c >= 12:
                        a_exp(l, tt, 3)
                        a_move(l, tt, 2)
                        if c > 12:
                            gate_tanh(l, c, 0)
                        a_move(l, tt, 3)
                        move_side(l, ("AO", tt), U[:, 0:2, tt * P:(tt + 1) * P],
                                  banks[7][:, 0:2 * P].rearrange("p (i t) -> p i t", i=2))
                        if c == 12:
                            for g in GROUPS[11]:
                                acc_emptied(act, l, g)
                            gate_tanh(l, c, 0)
                        gate_tanh(l, c, 1)
                    if name == "idx":
                        move_side(l, "iw", diag[0:4, :], banks[6][0:4, :], scale=(4 * 32) ** -0.5)
                    if c == 3:
                        move_side(l, "iwT", small[:, 0:16], banks[7][:, 0:16])
                    if c == 4:
                        index_relu(l, 1)
                    round_weights(l, c + 2)
                    if c >= 13:
                        round_branch(l, c - 1)
                round_branch(l, 15)
                for d in range(KT):
                    c = 16 + 3 * d
                    for n in range(4):
                        g = GROUPS[c + n // 2][n % 2]
                        src = acc_full(act, l, g)
                        if n == 0 and d > 0:
                            act.wait_ge(merged, l * 8 + d)
                        act.activation(th[:, n, :], src[:, :], ACT.Tanh, scale=0.5,
                                       bias=pcur[:, BM + 8 * n + d:BM + 8 * n + d + 1]).then_inc(emptied[g % 4], 1)
                        if n % 2:
                            round_weights(l, c + n // 2 + 2)
                    if d == 2:
                        act.wait_ge(p_in, l * 16 + 16)
                        for i in range(2):
                            act.activation(pT_hi[:, i, :], ptok[:, i, :], ACT.Copy).then_inc(pt_rounded, 1)
                    if d < 7:
                        round_weights(l, c + 4)
                for k in range(KT):
                    act.wait_ge(merged, l * 8 + (k + 1))
                    round_tile(l, k, 8, U[:, k, :])
                round_weights(l, 41)
                for c in range(40, 44):
                    for b, g in enumerate(GROUPS[c]):
                        e = 2 * (c - 40) + b
                        src = acc_full(act, l, g)
                        act.activation(U[:, e, :], src[:, :], ACT.Copy).then_inc(emptied[g % 4], 1)
                    round_weights(l, c + 2)
                square_root(l, 3, small[:, 44:48])
                for k in range(KT):
                    evacuate(l, GROUPS[44 + k // 4][k % 4], embedded[:, k, :])
                    if k == 3:
                        round_weights(l, 46)
                    if k >= 4:
                        act.wait_ge(h_ready, l * 16 + (8 + k - 3))
                        round_tile(l, k - 4, 16, xT[:, k - 4, :])
                for k in range(4, KT):
                    act.wait_ge(h_ready, l * 16 + (8 + k + 1))
                    round_tile(l, k, 16, xT[:, k, :])
                round_weights(l, 47)
                for e in range(4):
                    for b, g in enumerate(GROUPS[46 + e]):
                        src = acc_full(act, l, g)
                        if e > 0:
                            act.wait_ge(x_ready, l * 8 + (8 + 2 * (e - 1) + b + 1))
                        act.activation(th[:, b, :], src[:, :], ACT.Tanh, scale=0.5).then_inc(emptied[g % 4], 1)
                    round_ahead(l, 48 + e)
                square_root(l + 1, 1, small[:, 44:48])
                open_layer(l + 1)
            second_scalar(act, round_weights)

        @block.vector
        def _(dve):
            setup = [0]

            def sstep(ins):
                setup[0] += 1
                ins.then_inc(setup_dve, 1)
                dve.wait_ge(setup_dve, setup[0])

            def add_square(link, k, src, total):
                link(dve.tensor_tensor(total[:, k, :], src[:, k, :], src[:, k, :], ALU.mult))
                if k > 0:
                    ins = dve.tensor_tensor(total[:, k, :], total[:, k - 1, :], total[:, k, :], ALU.add)
                    if k < KT - 1:
                        link(ins)
                    else:
                        ins.then_inc(sum_ready, 1)

            def rstd_of(l, key, spread_key, scale, columns, diagonal, n):
                src = wait_full(dve, l, key)
                b = now[0].side[key][0]
                dve.tensor_scalar(columns, src[:, 0:TT], scale, EPS, ALU.mult, ALU.add).then_inc(emptied[b], 1)
                wait_emptied(dve, l, key)
                dve.reciprocal(columns, columns).then_inc(var_ready, 1)
                dve.wait_ge(rstd_ready, l * 3 + n)
                dve.tensor_tensor(diagonal[:, :].rearrange("p (t n) -> p t n", t=TT), ident.unsqueeze(1).broadcast_to((P, TT, P)),
                                  columns.unsqueeze(2).broadcast_to((P, TT, P)), ALU.mult).then_inc(diag_ready, 1)
                return wait_full(dve, l, spread_key)

            def normalise(l):
                rstd = rstd_of(l, "ssx", "rsx", 1.0 / D, small[:, 44:48], diag, 1)
                for k in range(KT):
                    n = l * NPAR + (G_PRE + k)
                    gain = pall[:, n:n + 1] if type(n) is int else pall[:, ds(n, 1)]
                    dve.scalar_tensor_tensor(U[:, k, :], xT[:, k, :], gain, rstd[:, :], ALU.mult, ALU.mult).then_inc(h_ready, 1)
                dve.wait_ge(h_ready, l * 16 + 8)
                dve.sem_inc(emptied[5], 1)

            for b in range(8):
                dve.sem_inc(emptied[b], 1)
            for k in range(1, KT):
                dve.wait_ge(sq_ready, k + 1)
                ins = dve.tensor_tensor(U[:, k, :], U[:, k - 1, :], U[:, k, :], ALU.add)
                if k < KT - 1:
                    sstep(ins)
                else:
                    ins.then_inc(sum_ready, 1)
            dve.wait_ge(first_in, 16 * len(first_loads))
            dve.wait_ge(bias_product, 1)
            sstep(dve.tensor_tensor(biasv[:, 0:512], banks[0][0:16, :], lnmult[:, 0:512], ALU.add))
            sstep(dve.tensor_tensor(biasv[:, 512:640], banks[1][0:16, 0:128], lnmult[:, 512:640], ALU.add))
            for half in range(2):
                dve.wait_ge(x_in[half], 16)
            for k in range(KT):
                dve.sem_inc(x_ready, 1)
            dve.wait_ge(const_in, 16 * NCONST)
            normalise(0)
            pos = ang[:, 3, :]
            sstep(dve.tensor_copy(pos, posb[:, :]))
            ROUND = 1.5 * 2 ** 23
            for i in range(2):
                r, q = ang[:, 2 * i, :], turns[:, :]
                sstep(dve.tensor_scalar(r, pos, freq[:, i:i + 1], None, ALU.mult))
                sstep(dve.tensor_scalar(q, r, 0.15915494309189535, ROUND, ALU.mult, ALU.add))
                sstep(dve.tensor_scalar(q, q, ROUND, None, ALU.subtract))
                sstep(dve.scalar_tensor_tensor(r, q, -6.28125, r, ALU.mult, ALU.add))
                sstep(dve.scalar_tensor_tensor(r, q, -0.0019353071795864769, r, ALU.mult, ALU.add))
                sstep(dve.tensor_scalar(r, r, 3.1415925, -3.1415925, ALU.min, ALU.max))
            for i in range(2):
                r, c = ang[:, 2 * i, :], ang[:, 2 * i + 1, :]
                sstep(dve.scalar_tensor_tensor(c, r, -1.0, r, ALU.mult, ALU.max))
                sstep(dve.tensor_scalar(c, c, -1.0, 1.5707963267948966, ALU.mult, ALU.add))
            assert setup[0] == SETUP_ANGLES, setup
            sstep(dve.tensor_scalar(par2[:, GATE_B:144], par2[:, GATE_B:144], 0.5, None, ALU.mult))

            steps = [0]

            def link(ins):
                steps[0] += 1
                ins.then_inc(dve_step, 1)
                dve.wait_ge(dve_step, steps[0])

            def rope(l, key, n, dst, src, cos, sin):
                rot = wait_full(dve, l, key)
                dve.tensor_tensor(rt[:, 0, :], src, cos[:, :], ALU.mult).then_inc(rope_cos, 1)
                dve.tensor_tensor(rt[:, 1, :], rot[:, :], sin[:, :], ALU.mult).then_inc(emptied[now[0].side[key][0]], 1)
                dve.wait_ge(rope_cos, l * 6 + (n + 1))
                wait_emptied(dve, l, key)
                dve.tensor_tensor(dst, rt[:, 0, :], rt[:, 1, :], ALU.add).then_inc(rot_ready, 1)
                dve.wait_ge(rot_ready, l * 6 + (n + 1))

            def index_scores(l, tt):
                n = (tt + 1) * P
                kp = keep[:, KOFF[tt]:KOFF[tt] + n]
                for h in range(4):
                    i = 4 * (3 - tt) + h
                    wait_emptied(dve, l, ("idx", tt, h))
                    w = small[:, 4 * tt + h:4 * tt + h + 1]
                    if h == 0:
                        dve.tensor_scalar(kp, relu[:, h, 0:n], w, None, ALU.mult).then_inc(relu_used, 1)
                    else:
                        dve.scalar_tensor_tensor(kp, relu[:, h, 0:n], w, kp, ALU.mult, ALU.add).then_inc(relu_used, 1)
                    dve.wait_ge(relu_used, l * 12 + (i + 1))
                link(dve.tensor_tensor(kp[:, n - P:n], kp[:, n - P:n], tri_neg, ALU.add))

            def top_keys(tt, rounds=range(P // 8)):
                n = (tt + 1) * P
                kp = keep[:, KOFF[tt]:KOFF[tt] + n]
                top8 = small[:, 36:44]
                for r in rounds:
                    link(dve.max(top8, kp))
                    link(dve.match_replace(kp, top8, kp, MARK))
                if rounds[-1] == P // 8 - 1:
                    link(dve.tensor_scalar(kp, kp, -3.1e38, NEG, ALU.is_gt, ALU.mult))

            def layer_norm(l):
                for g in GROUPS[7]:
                    acc_emptied(dve, l, g)
                for tt in range(TT):
                    link(dve.bn_stats(stats[:, tt, 0:6], dvt[:, tt, :]))
                    link(dve.bn_aggr(stats[:, tt, 6:8], stats[:, tt, 0:6]))
                link(dve.tensor_scalar(small[:, 16:20], stats[:, :, 7], EPS, None, ALU.add))
                dve.reciprocal(small[:, 16:20], small[:, 16:20]).then_inc(var_ready, 1)

            def layer_norm_apply(l):
                dve.wait_ge(rstd_ready, l * 3 + 2)
                for tt in range(TT):
                    v = dvt[:, tt, :]
                    link(dve.tensor_scalar(v, v, stats[:, tt, 6:7], small[:, 16 + tt:17 + tt], ALU.subtract, ALU.mult))
                    link(dve.tensor_tensor(v, v, lngb[:, ds(l, 1), 0, :].rearrange("p o n -> p (o n)"), ALU.mult))
                    ins = dve.tensor_tensor(v, v, lngb[:, ds(l, 1), 1, :].rearrange("p o n -> p (o n)"), ALU.add)
                    if tt < 3:
                        link(ins)
                    else:
                        ins.then_inc(vn_ready, 1)

            def d_weights(l):
                dve.wait_ge(ws_in, l * 16 + 16)
                dve.tensor_tensor(ws[:, :, :], ws[:, :, :], trilT.unsqueeze(1).broadcast_to((P, 4, P)),
                                  ALU.mult).then_inc(ws_ready, 1)

            def d_output(l):
                for g in GROUPS[8]:
                    acc_emptied(dve, l, g)
                for i in range(2):
                    src = wait_full(dve, l, ("dmix", i))
                    bias = bsp[:, ds(l, 1), i, :].broadcast_to((P, TT, P))
                    dve.tensor_tensor(rt[:, i, :].rearrange("p (t c) -> p t c", t=TT),
                                      src[:, :].rearrange("p (t c) -> p t c", t=TT), bias, ALU.add).then_inc(emptied[7], 1)
                    wait_emptied(dve, l, ("dmix", i))
                    link(dve.tensor_tensor(U[:, 6 + i, :], rt[:, i, :], U[:, 6 + i, :], ALU.mult))

            def z_pieces(js):
                return [(WOFF[j], WOFF[j] - WOFF[js[0]], S - j * P) for j in js]

            def c_softplus(l, h):
                dve.wait_ge(z_ln, l * 4 + (h + 1))
                for bank in range(3):
                    n = (512, 384, 384)[bank]
                    o = WOFF[bank]
                    dve.scalar_tensor_tensor(sp[:, o:o + n], banks[4 + bank][:, 0:n], 0.0, az[:, o:o + n],
                                             ALU.max, ALU.add).then_inc(emptied[4 + bank], 1)
                for bank in range(3):
                    wait_emptied(dve, l, ("Z", h, bank))
                for j in range(TT):
                    ins = dve.tensor_tensor(sp[:, WOFF[j]:WOFF[j] + P], sp[:, WOFF[j]:WOFF[j] + P], trisT, ALU.mult)
                    if j == 3:
                        ins.then_inc(sp_ready, 1)

            def c_weights(l, h):
                for bank in range(3):
                    src = wait_full(dve, l, ("Sx", h, bank))
                    n = (512, 384, 384)[bank]
                    o = WOFF[bank]
                    dve.tensor_scalar(wt[:, o:o + n], src[:, 0:n], 0.0, None, ALU.min).then_inc(emptied[4 + bank], 1)
                for bank in range(3):
                    wait_emptied(dve, l, ("Sx", h, bank))
                for j in range(TT):
                    ins = dve.tensor_tensor(wt[:, WOFF[j]:WOFF[j] + P], wt[:, WOFF[j]:WOFF[j] + P], trisT_add, ALU.add)
                    if j == 3:
                        ins.then_inc(cw_ready, 1)

            def b_gate_x(l):
                for g in GROUPS[9]:
                    acc_emptied(dve, l, g)
                for b, g in enumerate(GROUPS[10]):
                    src = acc_full(dve, l, g)
                    dve.tensor_tensor(U[:, 2 + b, :], U[:, 2 + b, :], src[:, :], ALU.mult).then_inc(emptied[g % 4], 1)
                    acc_emptied(dve, l, g)

            def b_conv(l):
                for b in range(2):
                    y, o = U[:, 2 + b, :], cvt[:, b, :]
                    w = [pcur[:, CW + 2 * k + b:CW + 2 * k + b + 1] for k in range(3)]
                    link(dve.tensor_scalar(o, y, w[2], pcur[:, CB + b:CB + b + 1], ALU.mult, ALU.add))
                    link(dve.scalar_tensor_tensor(o[:, 1:S], y[:, 0:S - 1], w[1], o[:, 1:S], ALU.mult, ALU.add))
                    link(dve.scalar_tensor_tensor(o[:, 2:S], y[:, 0:S - 2], w[0], o[:, 2:S], ALU.mult, ALU.add))

            def b_gate_b(l):
                for b, g in enumerate(GROUPS[11]):
                    src = acc_full(dve, l, g)
                    dve.tensor_tensor(U[:, 2 + b, :], cvt[:, b, :], src[:, :], ALU.mult).then_inc(emptied[g % 4], 1)
                    acc_emptied(dve, l, g)

            def a_max(l, tt, h):
                src = wait_full(dve, l, ("L", tt, h))
                n = (tt + 1) * P
                if h >= 2:
                    wait_full(dve, l, ("T", tt, h - 2))
                elif tt > 0:
                    wait_full(dve, l, ("T", tt - 1, h + 2))
                link(dve.memset(small[:, 24 + h:25 + h], 0.0))
                mask = keep[:, KOFF[tt]:KOFF[tt] + n] if tt else tri_add
                dve.tensor_tensor_reduce(probs[:, h % 2, 0:n], src[:, 0:n], mask, -1.0, 3.0e38, ALU.add, ALU.min,
                                         small[:, 24 + h:25 + h]).then_inc(emptied[4 + h % 2], 1)

            def a_norm(l, tt, h):
                n = (tt + 1) * P
                dve.wait_ge(pexp, l * 16 + (4 * tt + h + 1))
                link(dve.reciprocal(small[:, 32 + h:33 + h], small[:, 28 + h:29 + h]))
                dve.tensor_scalar(probs[:, h % 2, 0:n], probs[:, h % 2, 0:n], small[:, 32 + h:33 + h], None,
                                  ALU.mult).then_inc(pn_ready, 1)

            def gate(l, c, b):
                n, g = int(CH[c][1][1]), GROUPS[c][b]
                dve.wait_ge(th_ready, l * 8 + (2 * (c - 12) + b + 1))
                dve.scalar_tensor_tensor(cvt[:, b, :], cvt[:, b, :], 1.0, banks[g % 4][:, :], ALU.add, ALU.mult)\
                   .then_inc(emptied[g % 4], 1)
                acc_emptied(dve, l, g)
                o = U[:, 2 * n + b, :]
                dve.scalar_tensor_tensor(o, o, 0.5, cvt[:, b, :], ALU.mult, ALU.mult).then_inc(o_f32, 1)

            with dve.Fori(0, DEPTH) as l:
                steps[0] = 0
                dve.sem_clear(dve_step)
                dve.wait_ge(x_ready, l * 8 + 8)
                link(dve.tensor_copy(pcur[:, :], pall[:, ds(l * NPAR, NPAR)]))
                link(dve.tensor_scalar(pcur[:, G_POST:CW], pcur[:, G_POST:CW], 0.5, None, ALU.mult))
                dve.wait_ge(setup_act, 4)
                for i in range(2):
                    rope(l, f"rotq{i}", i, aq[:, i, :], raw[:, i, :], cos64, sin64)
                for i in range(2):
                    rope(l, f"rotk{i}", 2 + i, ak[:, i, :], raw[:, 2 + i, :], cos64, sin64)
                for i in range(2):
                    rope(l, f"roti{i}", 4 + i, iqk[:, i, :], raw[:, 4 + i, :], cos32, sin32)
                wait_emptied(dve, l, "iwT")
                for tt in (3, 2, 1):
                    index_scores(l, tt)
                top_keys(3)
                top_keys(2, range(0, 5))
                c_softplus(l, 0)
                top_keys(2, range(5, 7))
                c_weights(l, 0)
                layer_norm(l)
                top_keys(1, range(0, 3))
                c_softplus(l, 1)
                top_keys(2, range(7, 9))
                c_weights(l, 1)
                d_weights(l)
                top_keys(1, range(3, 8))
                c_softplus(l, 2)
                layer_norm_apply(l)
                c_weights(l, 2)
                top_keys(1, range(8, 13))
                b_gate_x(l)
                c_softplus(l, 3)
                d_output(l)
                b_conv(l)
                c_weights(l, 3)
                top_keys(1, range(13, 16))
                for c in range(12, 16):
                    tt = c - 12
                    a_max(l, tt, 0)
                    a_max(l, tt, 1)
                    a_norm(l, tt, 0)
                    a_max(l, tt, 2)
                    a_norm(l, tt, 1)
                    a_max(l, tt, 3)
                    a_norm(l, tt, 2)
                    if c == 12:
                        a_norm(l, tt, 3)
                        b_gate_b(l)
                        gate(l, c, 0)
                        top_keys(2, range(9, 12))
                    elif c == 13:
                        a_norm(l, tt, 3)
                        top_keys(2, range(12, 16))
                        gate(l, c, 0)
                    elif c == 15:
                        a_norm(l, tt, 3)
                        wait_emptied(dve, l, ("AO", tt))
                        gate(l, c, 0)
                    elif c == 14:
                        gate(l, c, 0)
                        a_norm(l, tt, 3)
                    else:
                        gate(l, c, 0)
                        a_norm(l, tt, 3)
                    gate(l, c, 1)
                for d in range(KT):
                    c = 16 + 3 * d
                    if d == 3:
                        for i in range(2):
                            dve.wait_ge(pt_rounded, l * 2 + (i + 1))
                            dve.tensor_tensor(pT_lo[:, i, :], ptok[:, i, :], pT_hi[:, i, :], ALU.subtract).then_inc(pt_split, 1)
                    for n, g in enumerate(GROUPS[c + 2]):
                        acc_emptied(dve, l, GROUPS[c + n // 2][n % 2])
                        src = acc_full(dve, l, g)
                        dst = U[:, d, :] if n == 0 else mtmp[:, 0, :]
                        dve.scalar_tensor_tensor(dst, th[:, n, :], 1.0, src[:, :], ALU.add, ALU.mult)\
                           .then_inc(emptied[g % 4], 1)
                        acc_emptied(dve, l, g)
                        if n > 0:
                            ins = dve.tensor_tensor(U[:, d, :], U[:, d, :], mtmp[:, 0, :], ALU.add)
                            if n < 3:
                                link(ins)
                            else:
                                ins.then_inc(merged, 1)
                for e in range(KT):
                    acc_emptied(dve, l, GROUPS[40 + e // 2][e % 2])
                    add_square(link, e, U, sq)
                rstd = rstd_of(l, "ssy", "rsy", 0.25 / D, small[:, 44:48], diag, 3)
                for k in range(KT):
                    link(dve.scalar_tensor_tensor(U[:, k, :], U[:, k, :], pcur[:, G_POST + k:G_POST + k + 1],
                                                  rstd[:, :], ALU.mult, ALU.mult))
                    dve.tensor_tensor(xT[:, k, :], xT[:, k, :], U[:, k, :], ALU.add).then_inc(h_ready, 1)
                dve.sem_inc(emptied[7], 1)
                for e in range(4):
                    for b in range(2):
                        k = 2 * e + b
                        if e == 0 and b == 0:
                            for g in GROUPS[45]:
                                acc_emptied(dve, l, g)
                        acc_emptied(dve, l, GROUPS[46 + e][b])
                        link(dve.scalar_tensor_tensor(U[:, k, :], th[:, b, :], 1.0, embedded[:, k, :], ALU.add, ALU.mult))
                        dve.wait_ge(h_split, l * 24 + 24)
                        dve.scalar_tensor_tensor(xT[:, k, :], U[:, k, :], 0.5, xT[:, k, :], ALU.mult, ALU.add)\
                           .then_inc(x_ready, 1)
                        dve.wait_ge(x_ready, l * 8 + (8 + k + 1))
                        add_square(link, k, xT, U)
                normalise(l + 1)
            second_vector(dve, rstd_of, add_square)

        @block.gpsimd
        def _(pool):
            def split_weights(l, c):
                n = columns(now[0].chunks[c])
                for half, cols in enumerate((slice(0, n // 2), slice(n // 2, n))):
                    pool.wait_ge(w_rounded, halves_count(l, c, half))
                    pool.tensor_tensor(w_lo[:, c % 2, cols], w_raw[:, c % 2, cols], w_hi[:, c % 2, cols],
                                       ALU.subtract).then_inc(w_split, 1)

            def split_tiles(l, first, src):
                for k in range(KT):
                    pool.wait_ge(h_rounded, l * 24 + (first + k + 1))
                    pool.tensor_tensor(h_lo[:, k, :], src[:, k, :], h_hi[:, k, :], ALU.subtract).then_inc(h_split, 1)

            def split_branch(l, c):
                n = int(CH[c][1][1])
                for b in range(2):
                    i = 2 * n + b
                    pool.wait_ge(o_rounded, l * 8 + (2 * (c - 12) + b + 1))
                    pool.tensor_tensor(o_lo[:, i, :], U[:, i, :], o_hi[:, i, :], ALU.subtract).then_inc(o_split, 1)

            pool.sem_inc(w_split, 4)
            pool.wait_ge(setup_dve, SETUP_BIAS)
            pool.dma_start(bias_s, biasv[:, :]).then_inc(bias_stored, 16)
            pool.wait_ge(bias_stored, 16)
            pool.dma_start(skew_s, bias_s.unsqueeze(1).broadcast_to((16, P, 640))).then_inc(skewed, 16)
            split_weights(0, 0)
            split_weights(0, 1)
            with pool.Fori(0, DEPTH) as l:
                split_tiles(l, 0, U)
                for c in range(2, 41):
                    split_weights(l, c)
                    if 15 <= c <= 17:
                        split_branch(l, c - 3)
                    if c == 17:
                        split_branch(l, 15)
                split_tiles(l, 8, U)
                for c in range(41, 47):
                    split_weights(l, c)
                split_tiles(l, 16, xT)
                for c in range(47, NCH):
                    split_weights(l, c)
                split_weights(l + 1, 0)
                split_weights(l + 1, 1)
            second_pool(pool, split_weights)


def program_inputs(x, p, positions, g_pre, w_in, conv_w, conv_b, ln_g, ln_b, w_spatial, b_spatial, b_merge, w_branch,
                   w_out, g_post, w_ple, w_ple_gate, norm_in_g_2, w_in_2, gate_b_2, conv_w_2, conv_b_2, wq_m_2, wk_m_2,
                   wv_m_2, w_if_2, b_if_2, head_norm_g_2, skip_m_2, w_pa_2, w_pb_2, w_out_2, rel_bias_2, norm_out_g_2):
    import numpy as np
    C = WIDTH

    def tiles(w, cols, kt=8):
        return np.ascontiguousarray(w[:, cols].reshape(kt, P, -1).transpose(1, 0, 2)).reshape(P, -1)

    def columns_of(*vectors):
        return np.concatenate([np.asarray(v).reshape(-1, P) for v in vectors]).T

    depth = w_in.shape[0]
    off = {"aq": 0, "ak": C, "av": 2 * C}
    iq = 3 * C
    ik, iw = iq + 128, iq + 160
    off.update({n: iq + 164 + j * C for j, n in enumerate(("bb", "bc", "bx", "cq", "ck", "cv", "du", "dv", "g0", "g1", "g2", "g3"))})
    merge = off["g3"] + C
    D, IN2 = 1024, {"q": 0, "k": 1024, "v": 2048, "z": 3072, "xm": 4096, "zm": 6144, "om": 8192, "ga": 10240, "gm": 11264}

    def block(kind, i, l):
        r = np.arange
        if kind == "proj":
            if i == "idx":
                return tiles(w_in[l], np.concatenate([r(iq, iq + 128)] + [r(ik, ik + 32)] * 4 + [r(iw, iw + 4)]))
            return tiles(w_in[l], r(off[i], off[i] + C))
        if kind == "logits":
            d, half = i
            return tiles(w_in[l], np.concatenate([r(merge + n * D + d * P, merge + n * D + (d + 1) * P) for n in (2 * half, 2 * half + 1)]))
        if kind == "branch":
            return tiles(w_branch[l].reshape(-1, D), r(i * P, (i + 1) * P))
        if kind in ("out", "pgate", "pa", "fo"):
            w = {"out": w_out, "pgate": w_ple_gate, "pa": w_pa_2, "fo": w_out_2}[kind][l]
            return tiles(w, r(i * C, (i + 1) * C))
        if kind == "ple":
            return tiles(w_ple[l], r(i * 512, (i + 1) * 512), 2)
        if kind == "pb":
            h, half = i // 2, i % 2
            return tiles(w_pb_2[0][h * 512:(h + 1) * 512], r(half * 512, (half + 1) * 512), 4)
        return tiles(w_in_2[0], r(IN2[kind] + i * C, IN2[kind] + (i + 1) * C))

    chunks = [(k, i, l) for l in range(depth) for k, i in layer_chunks()]
    rest = attention_chunks() + [("xm", j) for j in range(8)] + [c for h in range(4) for c in head_chunks(h)] + tail_chunks()
    chunks += [(k, i, 0) for k, i in rest]
    stream = np.zeros((len(chunks), P, CHUNK), np.float32)
    for n, (k, i, l) in enumerate(chunks):
        b = block(k, i, l)
        stream[n, :, :b.shape[1]] = b

    def diagonal_blocks(w):
        return w.reshape(16, P, 4).transpose(1, 0, 2)

    t = lambda w: np.ascontiguousarray(w.transpose(0, 2, 1))
    wqkv = np.stack([np.stack([diagonal_blocks(f(w[0])) for w in (wq_m_2, wk_m_2, wv_m_2)], 1) for f in (lambda w: w, t)], 1)
    arrays = {
        "stream": stream,
        "xT": x[0].T.reshape(8, P, -1).transpose(1, 0, 2),
        "pT": p[:, 0].transpose(2, 0, 1).reshape(2, P, depth, -1).transpose(1, 2, 0, 3),
        "positions": positions,
        "par1": np.stack([columns_of(g_pre[l], g_post[l], b_merge[l], conv_w[l], conv_b[l]) for l in range(depth)]
                         + [np.pad(columns_of(norm_in_g_2[0]), ((0, 0), (0, 48)))], 1),
        "ln_gb": np.stack([ln_g, ln_b], 1).reshape(1, -1),
        "b_spatial": b_spatial.reshape(depth, 2, 2, P).transpose(2, 0, 1, 3).reshape(2, -1),
        "wsT": w_spatial.transpose(3, 0, 1, 2),
        "par2": columns_of(norm_in_g_2[0], norm_out_g_2, head_norm_g_2[0], skip_m_2[0], gate_b_2[0], conv_b_2[0], conv_w_2[0]),
        "wqkv": wqkv,
        "w_if": w_if_2[0].reshape(48, P, 8).transpose(1, 0, 2),
        "b_if": b_if_2[0].reshape(8, 1),
        "rel_bias": rel_bias_2,
    }
    arrays.update(host_constants())
    return {k: np.ascontiguousarray(v) for k, v in arrays.items()}


def host_constants():
    import math
    import numpy as np
    dist = 511 - np.arange(640)
    large = 16 + (np.log(np.maximum(dist, 16).astype(np.float32) / np.float32(16)) / np.float32(math.log(2048 / 16))
                  * np.float32(16)).astype(np.int32)
    bucket = np.where(dist < 16, dist, np.minimum(large, 31))
    times = (dist <= 128).astype(int) + (dist % 4 == 0) + (dist % 16 == 0)
    times[dist < 0] = 0
    onehot = ((np.arange(32)[:, None] == bucket[None, :]) & (dist >= 0)).astype(np.float32)
    lnmult = np.where(times > 0, np.log(np.maximum(times, 1).astype(np.float32)), np.float32(-1e30)).astype(np.float32)
    lnmult = np.ascontiguousarray(np.broadcast_to(lnmult, (16, 640)))
    i = np.arange(P)
    part, col = i[:, None], i[None, :]
    rot = []
    for half in (32, 16):
        m = np.zeros((P, P), np.float32)
        for j in range(P):
            if j % (2 * half) < half:
                m[j + half, j] = -1.0
            else:
                m[j - half, j] = 1.0
        rot.append(m)
    f = np.float32
    mats = [np.eye(P, dtype=f), np.ones((P, P), f), (part <= col).astype(f), np.where(part <= col, f(0), f(-1e30)),
            rot[0], rot[1], np.where(col > part, f(-3.0e38), f(0)), np.where(col > part, f(-1e30), f(0)),
            (part < col).astype(f), np.where(part < col, f(0), f(-1e30)),
            -(part >= col).astype(f), -np.ones((P, P), f)]
    consts = np.ascontiguousarray(np.stack(mats, 1).astype(f))
    freq = np.stack([f(10000.0) ** (-(np.arange(0, d, 2, dtype=f) / f(d)))[i % (d // 2)] for d in (64, 32)], 1).astype(f)
    mask4 = (part // 4 == np.arange(32)[None, :]).astype(f)
    return {"consts": consts, "freq": freq, "mask4": mask4, "onehot": onehot, "lnmult": lnmult}


def kernel(**inputs):
    import numpy as np
    import concourse.bacc as bacc
    from concourse import mybir
    from concourse.bass_utils import run_bass_kernel_spmd

    nc = bacc.Bacc("TRN2", target_bir_lowering=False, num_devices=1)
    arrays = {f"in_{k}_dram": v for k, v in program_inputs(**{k: np.asarray(v) for k, v in inputs.items()}).items()}
    a = {n[3:-5]: nc.dram_tensor(n, v.shape, mybir.dt.from_np(v.dtype), kind="ExternalInput").ap() for n, v in arrays.items()}
    kt, tokens = a["xT"].shape[1:]
    a["out"] = nc.dram_tensor("out_0_dram", (P, kt, tokens), mybir.dt.float32, kind="ExternalOutput").ap()
    build_program(nc, a)
    out = run_bass_kernel_spmd(nc, [arrays], core_ids=[0]).results[0]["out_0_dram"]
    return out.transpose(2, 1, 0).reshape(1, tokens, kt * P)
```
